# Optimizing a Trainium2 kernel written in Bass

```python
import math
import jax, jax.numpy as jnp
from jax import lax
import numpy as np

D_MODEL = 1024
BATCH = 1
SEQ = 256
DEPTH = 2

CHUNK = 64
Q_BLOCK = 128
ROPE_THETA = 10000.0
EPS = 1e-6

A_HEADS = 4
A_HEAD_DIM = 64
A_V_DIM = 2 * A_HEAD_DIM
B_HEADS = 8
B_KV_HEADS = 2
B_HEAD_DIM = 64
WINDOW = 128
WINDOW_CHUNKS = WINDOW // CHUNK

A_Q = A_HEADS * 2 * A_HEAD_DIM
A_K = A_HEADS * 2 * A_HEAD_DIM
A_V = A_HEADS * A_V_DIM
B_Q = B_HEADS * B_HEAD_DIM
B_K = B_KV_HEADS * B_HEAD_DIM
B_V = B_KV_HEADS * B_HEAD_DIM
L0_IN = A_Q + A_K + A_V + B_Q + B_K + B_V
L0_OUT = A_V + B_Q
L0_SPLIT = (A_Q, A_Q + A_K, A_Q + A_K + A_V, A_Q + A_K + A_V + B_Q,
            A_Q + A_K + A_V + B_Q + B_K)

C_HEADS = 16
C_Q_RANK = 256
C_KV_RANK = 128
C_NOPE = 64
C_ROPE = 32
C_V = 64
C_QK = C_NOPE + C_ROPE
C_IN = C_Q_RANK + C_KV_RANK + C_ROPE
C_OUT = C_HEADS * C_V

D_FF = 2816
N_EXPERTS = 8
TOP_K = 2
D_FF_EXPERT = 3584

kernel_name = "hybrid_diff_swa_mla_moe_trunk"

def rms_norm(x, g):
    xf = x.astype(jnp.float32)
    y = xf * lax.rsqrt(jnp.mean(xf * xf, axis=-1, keepdims=True) + EPS)
    return (y * g.astype(jnp.float32)).astype(x.dtype)

def rope_tables(seq, dim):
    pos = jnp.arange(seq, dtype=jnp.float32)
    inv = ROPE_THETA ** (-jnp.arange(0, dim, 2, dtype=jnp.float32) / dim)
    ang = pos[:, None] * inv[None, :]
    return jnp.cos(ang), jnp.sin(ang)

def apply_rope(x, cos, sin):
    shape = (1, cos.shape[0]) + (1,) * (x.ndim - 3) + (cos.shape[1],)
    c = cos.reshape(shape).astype(x.dtype)
    s = sin.reshape(shape).astype(x.dtype)
    x1, x2 = jnp.split(x, 2, axis=-1)
    return jnp.concatenate([x1 * c - x2 * s, x2 * c + x1 * s], axis=-1)

def to_blocks(x):
    nb = x.shape[1] // Q_BLOCK
    x = x.reshape((x.shape[0], nb, Q_BLOCK) + x.shape[2:])
    return jnp.moveaxis(x, 1, 0)

def from_blocks(y):
    y = jnp.moveaxis(y, 0, 1)
    return y.reshape((y.shape[0], y.shape[1] * y.shape[2]) + y.shape[3:])

def chunk_causal_mask(block_idx, seq):
    q_chunk = (block_idx * Q_BLOCK + jnp.arange(Q_BLOCK)) // CHUNK
    k_chunk = jnp.arange(seq) // CHUNK
    return k_chunk[None, :] <= q_chunk[:, None]

def masked_softmax(s, mask):
    return jax.nn.softmax(jnp.where(mask, s, -jnp.inf), axis=-1)

def diff_attention(q, k, v, lam):
    scale = A_HEAD_DIM ** -0.5
    seq = k.shape[1]
    nb = seq // Q_BLOCK

    def one_block(args):
        b, qb = args
        s = jnp.einsum('bqhmd,bkhmd->bhmqk', qb, k).astype(jnp.float32) * scale
        p = masked_softmax(s, chunk_causal_mask(b, seq))
        w = p[:, :, 0] - lam * p[:, :, 1]
        return jnp.einsum('bhqk,bkhd->bqhd', w.astype(v.dtype), v)

    return from_blocks(lax.map(one_block, (jnp.arange(nb), to_blocks(q))))

def swa_sink_attention(q, k, v, sinks):
    B, S, _, D = q.shape
    nb = S // Q_BLOCK
    G = B_HEADS // B_KV_HEADS
    scale = B_HEAD_DIM ** -0.5
    qb = q.reshape(B, nb, Q_BLOCK, B_KV_HEADS, G, D)

    def band(t):
        tp = jnp.pad(t, ((0, 0), (Q_BLOCK, 0), (0, 0), (0, 0)))
        tb = tp.reshape(B, nb + 1, Q_BLOCK, B_KV_HEADS, D)
        return jnp.concatenate([tb[:, :-1], tb[:, 1:]], axis=2)

    kb, vb = band(k), band(v)
    q_pos = jnp.arange(S).reshape(nb, Q_BLOCK)
    k_pos = jnp.arange(nb)[:, None] * Q_BLOCK - Q_BLOCK + jnp.arange(2 * Q_BLOCK)[None, :]
    qc = (q_pos // CHUNK)[:, :, None]
    kc = (k_pos // CHUNK)[:, None, :]
    mask = (k_pos >= 0)[:, None, :] & (kc <= qc) & (kc >= qc - WINDOW_CHUNKS)
    s = jnp.einsum('bnqhgd,bnkhd->bnhgqk', qb, kb).astype(jnp.float32) * scale
    s = jnp.where(mask[None, :, None, None], s, -jnp.inf)
    sink = sinks.astype(jnp.float32).reshape(1, 1, B_KV_HEADS, G, 1, 1)
    m = jnp.maximum(jnp.max(s, axis=-1, keepdims=True), sink)
    e = jnp.exp(s - m)
    p = e / (jnp.sum(e, axis=-1, keepdims=True) + jnp.exp(sink - m))
    out = jnp.einsum('bnhgqk,bnkhd->bnqhgd', p.astype(v.dtype), vb)
    return out.reshape(B, S, B_HEADS, D)

def dense_chunk_causal_attention(q, k, v, scale):
    seq = k.shape[1]
    nb = seq // Q_BLOCK

    def one_block(args):
        b, qb = args
        s = jnp.einsum('bqhd,bkhd->bhqk', qb, k).astype(jnp.float32) * scale
        p = masked_softmax(s, chunk_causal_mask(b, seq))
        return jnp.einsum('bhqk,bkhd->bqhd', p.astype(v.dtype), v)

    return from_blocks(lax.map(one_block, (jnp.arange(nb), to_blocks(q))))

def hybrid_a_b_mixer(h, w_in, a_q_norm, a_k_norm, a_lambda, a_subln,
                     b_q_norm, b_k_norm, b_sinks, w_out, cos, sin, layer):
    B, S, _ = h.shape
    z = h @ w_in
    aq, ak, av, bq, bk, bv = jnp.split(z, L0_SPLIT, axis=-1)
    aq = apply_rope(rms_norm(aq.reshape(B, S, A_HEADS, 2, A_HEAD_DIM), a_q_norm), cos, sin)
    ak = apply_rope(rms_norm(ak.reshape(B, S, A_HEADS, 2, A_HEAD_DIM), a_k_norm), cos, sin)
    av = av.reshape(B, S, A_HEADS, A_V_DIM)
    lam_init = 0.8 - 0.6 * math.exp(-0.3 * layer)
    lf = a_lambda.astype(jnp.float32)
    lam = jnp.exp(jnp.sum(lf[0] * lf[1])) - jnp.exp(jnp.sum(lf[2] * lf[3])) + lam_init
    a_out = diff_attention(aq, ak, av, lam)
    a_out = rms_norm(a_out, a_subln) * (1.0 - lam_init)
    bq = apply_rope(rms_norm(bq.reshape(B, S, B_HEADS, B_HEAD_DIM), b_q_norm), cos, sin)
    bk = apply_rope(rms_norm(bk.reshape(B, S, B_KV_HEADS, B_HEAD_DIM), b_k_norm), cos, sin)
    bv = bv.reshape(B, S, B_KV_HEADS, B_HEAD_DIM)
    b_out = swa_sink_attention(bq, bk, bv, b_sinks)
    merged = jnp.concatenate([a_out.reshape(B, S, A_V), b_out.reshape(B, S, B_Q)], axis=-1)
    return merged @ w_out

def mla_mixer(h, w_in, q_lora_norm, kv_lora_norm, w_uq, w_ukv, q_norm, k_norm,
              w_out, cos, sin):
    B, S, _ = h.shape
    z = h @ w_in
    c_q, c_kv, k_rope = jnp.split(z, (C_Q_RANK, C_Q_RANK + C_KV_RANK), axis=-1)
    c_q = rms_norm(c_q, q_lora_norm)
    c_kv = rms_norm(c_kv, kv_lora_norm)
    q = (c_q @ w_uq).reshape(B, S, C_HEADS, C_QK)
    kv = (c_kv @ w_ukv).reshape(B, S, C_HEADS, C_NOPE + C_V)
    k_nope, v = jnp.split(kv, (C_NOPE,), axis=-1)
    k_r = jnp.broadcast_to(k_rope[:, :, None, :], (B, S, C_HEADS, C_ROPE))
    k = jnp.concatenate([k_nope, k_r], axis=-1)
    q = rms_norm(q, q_norm)
    k = rms_norm(k, k_norm)
    q = jnp.concatenate([q[..., :C_NOPE], apply_rope(q[..., C_NOPE:], cos, sin)], axis=-1)
    k = jnp.concatenate([k[..., :C_NOPE], apply_rope(k[..., C_NOPE:], cos, sin)], axis=-1)
    out = dense_chunk_causal_attention(q, k, v, C_QK ** -0.5)
    return out.reshape(B, S, C_OUT) @ w_out

def swiglu(h, w_gu, w_down):
    g, u = jnp.split(h @ w_gu, 2, axis=-1)
    return (jax.nn.silu(g) * u) @ w_down

def moe_swiglu(h, w_router, w_gu, w_down):
    logits = (h @ w_router).astype(jnp.float32)
    vals, idx = lax.top_k(logits, TOP_K)
    gates = jax.nn.softmax(vals, axis=-1)
    combine = jnp.sum(jax.nn.one_hot(idx, N_EXPERTS, dtype=jnp.float32) * gates[..., None], axis=-2)
    y = jnp.zeros_like(h)
    for e in range(N_EXPERTS):
        y = y + combine[..., e:e + 1].astype(h.dtype) * swiglu(h, w_gu[e], w_down[e])
    return y

def setup_inputs(seed: int = 0) -> dict:
    key = jax.random.key(seed)
    ks = jax.random.split(key, 32)

    def w(k, shape, fan_in):
        return jax.random.normal(k, shape, jnp.float32) * fan_in ** -0.5

    def gain(k, n):
        return 1.0 + 0.05 * jax.random.normal(k, (n,), jnp.float32)

    return {
        "x": jax.random.normal(ks[0], (BATCH, SEQ, D_MODEL), jnp.float32),
        "l0_norm_attn": gain(ks[1], D_MODEL),
        "l0_w_in": w(ks[2], (D_MODEL, L0_IN), D_MODEL),
        "l0_a_q_norm": gain(ks[3], A_HEAD_DIM),
        "l0_a_k_norm": gain(ks[4], A_HEAD_DIM),
        "l0_a_lambda": 0.1 * jax.random.normal(ks[5], (4, A_HEAD_DIM), jnp.float32),
        "l0_a_subln": gain(ks[6], A_V_DIM),
        "l0_b_q_norm": gain(ks[7], B_HEAD_DIM),
        "l0_b_k_norm": gain(ks[8], B_HEAD_DIM),
        "l0_b_sinks": 0.5 * jax.random.normal(ks[9], (B_HEADS,), jnp.float32),
        "l0_w_out": w(ks[10], (L0_OUT, D_MODEL), L0_OUT),
        "l0_norm_ffn": gain(ks[11], D_MODEL),
        "l0_ffn_w_gu": w(ks[12], (D_MODEL, 2 * D_FF), D_MODEL),
        "l0_ffn_w_down": w(ks[13], (D_FF, D_MODEL), D_FF),
        "l1_norm_attn": gain(ks[14], D_MODEL),
        "l1_c_w_in": w(ks[15], (D_MODEL, C_IN), D_MODEL),
        "l1_c_q_lora_norm": gain(ks[16], C_Q_RANK),
        "l1_c_kv_lora_norm": gain(ks[17], C_KV_RANK),
        "l1_c_w_uq": w(ks[18], (C_Q_RANK, C_HEADS * C_QK), C_Q_RANK),
        "l1_c_w_ukv": w(ks[19], (C_KV_RANK, C_HEADS * (C_NOPE + C_V)), C_KV_RANK),
        "l1_c_q_norm": gain(ks[20], C_QK),
        "l1_c_k_norm": gain(ks[21], C_QK),
        "l1_c_w_out": w(ks[22], (C_OUT, D_MODEL), C_OUT),
        "l1_norm_ffn": gain(ks[23], D_MODEL),
        "l1_router": w(ks[24], (D_MODEL, N_EXPERTS), D_MODEL),
        "l1_exp_w_gu": w(ks[25], (N_EXPERTS, D_MODEL, 2 * D_FF_EXPERT), D_MODEL),
        "l1_exp_w_down": w(ks[26], (N_EXPERTS, D_FF_EXPERT, D_MODEL), D_FF_EXPERT),
    }

def reference(x, l0_norm_attn, l0_w_in, l0_a_q_norm, l0_a_k_norm, l0_a_lambda, l0_a_subln,
              l0_b_q_norm, l0_b_k_norm, l0_b_sinks, l0_w_out, l0_norm_ffn, l0_ffn_w_gu,
              l0_ffn_w_down, l1_norm_attn, l1_c_w_in, l1_c_q_lora_norm, l1_c_kv_lora_norm,
              l1_c_w_uq, l1_c_w_ukv, l1_c_q_norm, l1_c_k_norm, l1_c_w_out, l1_norm_ffn,
              l1_router, l1_exp_w_gu, l1_exp_w_down):
    seq = x.shape[1]
    cos64, sin64 = rope_tables(seq, A_HEAD_DIM)
    cos32, sin32 = rope_tables(seq, C_ROPE)
    for layer in range(DEPTH):
        if layer % 2 == 0:
            h = rms_norm(x, l0_norm_attn)
            x = x + hybrid_a_b_mixer(h, l0_w_in, l0_a_q_norm, l0_a_k_norm, l0_a_lambda,
                                     l0_a_subln, l0_b_q_norm, l0_b_k_norm, l0_b_sinks,
                                     l0_w_out, cos64, sin64, layer)
            h = rms_norm(x, l0_norm_ffn)
            x = x + swiglu(h, l0_ffn_w_gu, l0_ffn_w_down)
        else:
            h = rms_norm(x, l1_norm_attn)
            x = x + mla_mixer(h, l1_c_w_in, l1_c_q_lora_norm, l1_c_kv_lora_norm, l1_c_w_uq,
                              l1_c_w_ukv, l1_c_q_norm, l1_c_k_norm, l1_c_w_out, cos32, sin32)
            h = rms_norm(x, l1_norm_ffn)
            x = x + moe_swiglu(h, l1_router, l1_exp_w_gu, l1_exp_w_down)
    return x


_drawn_inputs = setup_inputs


def setup_inputs(seed=0):
    import zlib

    import numpy as np

    out = dict(_drawn_inputs(seed))
    spreads = {}
    factors = {'l0_b_q_norm': 4.691,
     'l0_b_k_norm': 4.711,
     'l0_b_sinks': 8.0,
     'l1_c_q_lora_norm': 3.955,
     'l1_c_kv_lora_norm': 3.08,
     'l1_c_q_norm': 8.0,
     'l1_c_k_norm': 4.146}
    for name, (base, spread) in spreads.items():
        noise = np.random.default_rng([zlib.crc32(name.encode()), seed]).standard_normal(out[name].shape)
        drawn = base * np.exp(spread * noise) if base else spread * noise
        out[name] = __import__('jax').numpy.asarray(drawn.astype(out[name].dtype))
    for name, factor in factors.items():
        out[name] = (out[name] * factor).astype(out[name].dtype)
    return out
```

```python
import math
import numpy as np
import concourse.bass as bass
from concourse import mybir
from contextlib import ExitStack

P = 128
D = 1024
SEQ = 256
NT = SEQ // P
KC = D // P
CHUNK = 64
EPS = 1e-6
A_HEADS, A_MAPS, HD, A_VD = 4, 2, 64, 128
B_HEADS, B_KV = 8, 2
ZA_Q, ZA_K, ZA_V = 0, 512, 1024
ZB_Q, ZB_K, ZB_V = 1536, 2048, 2176
L0_IN = 2304
N_QK_A, N_QK_B = 16, 10
C_HEADS, C_NOPE, C_ROPE, C_V = 16, 64, 32, 64
C_QK = C_NOPE + C_ROPE
C_QR, C_KVR = 256, 128
C_IN = C_QR + C_KVR + C_ROPE
FF = 2816
NE, FFE = 8, 3584
LAM_INIT = 0.8 - 0.6 * math.exp(-0.3 * 0)
NEG = -1.0e30
COLS = 512

RING = 6
SLOTS = 3
PIECE = 2048


def dense_pieces(name, rows, cols):
    out = []
    for n in range(0, cols, COLS):
        w = min(COLS, cols - n)
        step = min(rows // P, PIECE // w)
        for c in range(0, rows // P, step):
            out.append((name, n // COLS, c, c + step, w))
    return out


IN0 = dense_pieces("w_in0", D, L0_IN)
OUT0 = dense_pieces("w_out0", D, D)
IN1 = dense_pieces("w_in1", D, C_IN)
UQ = dense_pieces("w_uq", C_QR, C_HEADS * C_QK)
UKV = [("w_ukv", 0, 0, 1, 2048)]
OUT1 = dense_pieces("w_out1", D, D)


def ffn_pieces():
    out, chunks = [], [(k, min(COLS, FF - k * COLS)) for k in range(-(-FF // COLS))]

    def down(k, w):
        return [("ffn_d", k, j, min(j + 2, w // P), w) for j in range(0, w // P, 2)]

    for k, w in chunks:
        step = PIECE // w
        for kind in ("ffn_g", "ffn_u"):
            out += [(kind, k, c, c + step, w) for c in range(0, KC, step)]
        if k:
            out += down(k - 1, COLS)
    return out + down(*chunks[-1])


FFN = ffn_pieces()
FFN_CHUNKS = -(-FF // COLS)
EXP_CHUNKS = FFE // COLS
EXP = []
for _k in range(EXP_CHUNKS):
    EXP += [("g", _k, 0), ("g", _k, 1), ("u", _k, 0), ("u", _k, 1)]
    if _k:
        EXP += [("d", _k - 1, 0), ("d", _k - 1, 1)]
EXP += [("d", EXP_CHUNKS - 1, 0), ("d", EXP_CHUNKS - 1, 1)]
NU = len(EXP)
assert NU % RING == 0 and NU % SLOTS == 0

STREAM = IN0 + OUT0 + FFN + IN1 + UQ + UKV + OUT1
U0 = len(STREAM)


def first(pieces):
    return STREAM.index(pieces[0])


def piece_floats(piece):
    return PIECE if piece[0].startswith("ffn_d") else (piece[3] - piece[2]) * piece[4]


X_NORM0, X_MERGE0, X_NORM1 = 0, 4, 8
X_FFN = 12
X_NORM2 = X_FFN + NT * FFN_CHUNKS
X_LORA = X_NORM2 + 4
X_MERGE1 = X_LORA + 2
X_NORM3 = X_MERGE1 + 4
X_EXP = X_NORM3 + 4
X_PER_PASS = 2 + 8 * 9

R_NORM0, R_QK0, R_SUB, R_NORM1, R_NORM2, R_LORA, R_Q1, R_K1, R_NORM3 = 0, 2, 4, 6, 8, 10, 12, 14, 16
R_COLS = [1, 1, 26, 26, 4, 4, 1, 1, 1, 1, 2, 2, 16, 16, 16, 16, 1, 1]
R_OFF = [sum(R_COLS[:i]) for i in range(len(R_COLS))]


def build(nc, A):
    f32, f32r, i32 = mybir.dt.float32, mybir.dt.float32r, mybir.dt.int32
    ALU, ACT, AX = mybir.AluOpType, mybir.ActivationFunctionType, mybir.AxisListType
    ctx = ExitStack()
    with ctx:
        def sb(name, shape, dt=f32):
            return ctx.enter_context(nc.sbuf_tensor(name, shape, dt))

        def sem(name):
            return ctx.enter_context(nc.semaphore(name))

        ring = sb("ring", [P, RING, PIECE])
        w_hi = sb("w_hi", [P, SLOTS, PIECE], f32r)
        w_lo = sb("w_lo", [P, SLOTS, PIECE], f32r)
        x = sb("x_res", [P, NT, D])
        h = sb("h_tok", [P, NT, D])
        hT_hi = sb("hT_hi", [P, KC, SEQ], f32r)
        hT_lo = sb("hT_lo", [P, KC, SEQ], f32r)
        aT_hi = sb("aT_hi", [P, 4, SEQ], f32r)
        aT_lo = sb("aT_lo", [P, 4, SEQ], f32r)
        ident = sb("ident", [P, P])
        masks = sb("masks", [P, 2, SEQ])
        stat = sb("stat", [P, sum(R_COLS)])
        neg_half = sb("neg_half", [P, 26])
        subln = sb("subln", [P, A_VD])
        sinks = sb("sinks", [P, B_HEADS])
        small = sb("small", [P, 2, 16])
        rinv = sb("rinv", [P, NT, 16])
        lam = sb("lam", [P, 8])
        rw_hi = sb("rw_hi", [P, KC, NE], f32r)
        rw_lo = sb("rw_lo", [P, KC, NE], f32r)
        rw = sb("rw", [P, KC, NE])
        nmax = sb("nmax", [1, 1])
        nmax_i = sb("nmax_i", [1, 1], i32)
        rope = sb("rope", [P, NT, 96])
        tabs = sb("tabs", [P, 1024])
        arena1 = sb("arena1", [P, 5120])
        arena2 = sb("arena2", [P, 8192])
        arena3 = sb("arena3", [P, 2048])

        z = arena1[:, 0:NT * L0_IN].rearrange("p (t n) -> p t n", t=NT)
        qk1 = arena1[:, 0:NT * 1536].rearrange("p (t n) -> p t n", t=NT)
        v1 = arena1[:, 3072:3072 + NT * 1024].rearrange("p (t n) -> p t n", t=NT)
        triu = arena1[:, 0:P]
        iota = arena1[:, P:2 * P]
        ones = arena1[:, 2 * P:3 * P]
        tie = arena1[:, 384:448].rearrange("p (e f) -> p e f", e=NE)
        rt = arena1[:, 512:1024]
        onehot_gated = arena1[:, 1024:3072].rearrange("p (t e s) -> p t e s", t=NT, e=NE)
        qkT0 = arena2[:, 0:13 * SEQ].rearrange("p (s n) -> p s n", s=13)
        qT1 = arena2[:, 0:16 * SEQ].rearrange("p (s n) -> p s n", s=16)
        kT1 = arena2[:, 16 * SEQ:32 * SEQ].rearrange("p (s n) -> p s n", s=16)
        z1 = arena2[:, 16 * SEQ:16 * SEQ + NT * C_IN].rearrange("p (t n) -> p t n", t=NT)
        onehot = arena2[:, 0:2304].rearrange("p (t e s) -> p t e s", t=NT, e=NE + 1)
        scatT_all = arena2[:, 2304:4352].rearrange("p (e n) -> p e n", e=NE)
        scatT = arena2[:, 4352:4608]
        y_exp = arena2[:, 4608:5632]
        gain = arena3[:, 0:D]
        raw_gains = arena3[:, D:D + 4 * HD].rearrange("p (k d) -> p k d", k=4)
        raw_lam = arena3[:, D + 256:D + 512].rearrange("p (k d) -> p k d", k=4)
        raw_gains1 = arena3[:, D + 512:D + 704].rearrange("p (k d) -> p k d", k=2)
        lora_gain = arena3[:, D:D + C_QR + C_KVR]
        sq = arena3[:, 0:26 * HD]
        probs = arena3[:, 0:1024].rearrange("p (b m n) -> p b m n", b=2, m=2)
        probsT = arena3[:, 1024:2048].rearrange("p (b m n) -> p b m n", b=2, m=4)
        sig = arena3[:, 0:1024].rearrange("p (b n) -> p b n", b=2)
        act = arena3[:, 1024:2048].rearrange("p (b n) -> p b n", b=2)
        hflat = h[:, :, :].rearrange("p t n -> p (t n)")
        rope_tmp = hflat[:, 0:26 * HD]
        tab0 = tabs[:, 0:1024].rearrange("p (k t c d) -> p k t c d", k=4, t=NT, c=2)
        tab1 = tabs[:, 0:512].rearrange("p (k t c) -> p k t c", k=2, t=NT)

        PS = ctx.enter_context(nc.psum_tensor("PS", [P, 8, COLS], f32))

        def bank(b):
            return PS[:, b, :]

        x_loaded = sem("x_loaded")
        gain0_loaded = sem("gain0_loaded")
        gain_loaded = sem("gain_loaded")
        early_loaded = sem("early_loaded")
        tab_in = sem("tab_in")
        lora_loaded = sem("lora_loaded")
        moe_loaded = sem("moe_loaded")
        ring_loaded = [sem(f"ring_loaded{i}") for i in range(RING)]
        hi_ready = sem("hi_ready")
        lo_ready = sem("lo_ready")
        used = sem("pieces_used")
        neg_half_set = sem("neg_half_set")
        tabs_built = sem("tabs_built")
        pool_step = sem("pool_step")
        dve_step = sem("dve_step")
        act_step = sem("act_step")
        squared = sem("squared")
        ms_ready = sem("ms_ready")
        rstd_ready = sem("rstd_ready")
        normed = sem("normed")
        x_updated = sem("x_updated")
        transposed = sem("transposed")
        hi_split = sem("hi_split")
        lo_split = sem("lo_split")
        evacuated = sem("evacuated")
        qk_normed = sem("qk_normed")
        qk_transposed = sem("qk_transposed")
        qkT_ready = sem("qkT_ready")
        scored = sem("scored")
        masked = sem("masked")
        bias_ready = sem("bias_ready")
        exp_done = sem("exp_done")
        probs_ready = sem("probs_ready")
        probs_transposed = sem("probs_transposed")
        probsT_ready = sem("probsT_ready")
        pv_done = sem("pv_done")
        merged = sem("merged")
        lam_exp = sem("lam_exp")
        sig_ready = sem("sig_ready")
        act_ready = sem("act_ready")
        silu_step = sem("silu_step")
        routed = sem("routed")
        router_step = sem("router_step")
        logit_exp = sem("logit_exp")
        ranks_ready = sem("ranks_ready")
        counted = sem("counted")
        onehot_ready = sem("onehot_ready")
        scat_transposed = sem("scat_transposed")
        scat_ready = sem("scat_ready")
        y_evac = sem("y_evac")
        scattered = sem("scattered")
        scat_added = sem("scat_added")
        flag_ready = sem("flag_ready")
        stored = sem("stored")

        block = ctx.enter_context(nc.Block())

        def rows(name, c0, c1, n0, w):
            return A[name][c0 * P:c1 * P, n0:n0 + w].rearrange("(c p) n -> p c n", p=P)

        def piece_source(piece):
            name, n, c0, c1, w = piece
            if name == "ffn_g":
                return rows("l0_ffn_w_gu", c0, c1, n * COLS, w)
            if name == "ffn_u":
                return rows("l0_ffn_w_gu", c0, c1, FF + n * COLS, w)
            if name == "ffn_d":
                return rows("l0_ffn_w_down", n * 4 + c0, n * 4 + c1, 0, D)
            src = {"w_in0": "l0_w_in", "w_out0": "l0_w_out", "w_in1": "l1_c_w_in", "w_uq": "l1_c_w_uq",
                   "w_ukv": "l1_c_w_ukv", "w_out1": "l1_c_w_out"}[name]
            return rows(src, c0, c1, n * COLS, w)

        def expert_source(e, piece):
            kind, k, half = piece
            if kind == "d":
                r = k * COLS + half * 2 * P
                return A["l1_exp_w_down"][e, r:r + 2 * P, :].rearrange("(c p) n -> p c n", p=P)
            n0 = k * COLS + (FFE if kind == "u" else 0)
            return A["l1_exp_w_gu"][e, half * 4 * P:(half + 1) * 4 * P, n0:n0 + COLS]\
                .rearrange("(c p) n -> p c n", p=P)

        def per(value, e, step):
            return value if e is None else e * step + value

        def bc(ap, axis, n):
            shape = list(ap.shape)
            return ap.unsqueeze(axis).broadcast_to(shape[:axis] + [n] + shape[axis:])

        @block.sync
        def _(sp):
            def load(u, src, n, e=None):
                if u >= RING:
                    sp.wait_ge(lo_ready, per(u - RING + 1, e, NU))
                c = src.shape[1]
                dst = ring[:, u % RING, 0:n].rearrange("p (c n) -> p c n", c=c)
                sp.dma_start(dst, src).then_inc(ring_loaded[u % RING], 16)

            for u, piece in enumerate(STREAM):
                load(u, piece_source(piece), piece_floats(piece))
            for k in range(3):
                load(U0 + k, expert_source(0, EXP[k]), PIECE)

            def expert_pass(base):
                with sp.Fori(0, NE - 1) as e:
                    for k in range(3, NU):
                        load(base + k, expert_source(e, EXP[k]), PIECE, e)
                    for k in range(3):
                        load(base + NU + k, expert_source(e + 1, EXP[k]), PIECE, e)
                last = base + (NE - 1) * NU
                for k in range(3, NU):
                    load(last + k, expert_source(NE - 1, EXP[k]), PIECE)
                for k in range(3):
                    load(last + NU + k, expert_source(0, EXP[k]), PIECE)

            expert_pass(U0)
            sp.wait_ge(flag_ready, 1)
            most = sp.value_load(nmax_i[0:1, 0:1], min_val=0, max_val=SEQ)
            with sp.If(most > P):
                expert_pass(U0 + NE * NU)

        @block.gpsimd
        def _(pool):
            steps = [0]

            def link(ins):
                steps[0] += 1
                ins.then_inc(pool_step, 1)
                pool.wait_ge(pool_step, steps[0])

            pool.memset(neg_half[:, :], -0.5).then_inc(neg_half_set, 1)
            pool.wait_ge(neg_half_set, 1)

            def rsqrt(r):
                pool.wait_ge(ms_ready, r + 1)
                s = stat[:, R_OFF[r]:R_OFF[r] + R_COLS[r]]
                pool.tensor_tensor(s, s, neg_half[:, 0:R_COLS[r]], ALU.pow).then_inc(rstd_ready, 1)

            def build_tables(tab, g, half, lead, cos0, sin0):
                for k in range(g.shape[1]):
                    for t in range(NT):
                        cos, sin = rope[:, t, cos0:cos0 + half], rope[:, t, sin0:sin0 + half]
                        c, s = tab(k, t)
                        if lead:
                            link(pool.tensor_copy(c[:, 0:lead], g[:, k, 0:lead]))
                        link(pool.tensor_tensor(c[:, lead:lead + half], g[:, k, lead:lead + half], cos, ALU.mult))
                        link(pool.tensor_tensor(c[:, lead + half:lead + 2 * half],
                                                g[:, k, lead + half:lead + 2 * half], cos, ALU.mult))
                        link(pool.tensor_tensor(s[:, half:2 * half], g[:, k, lead:lead + half], sin, ALU.mult))
                        link(pool.tensor_tensor(s[:, 0:half], g[:, k, lead + half:lead + 2 * half], sin, ALU.mult))
                        link(pool.tensor_scalar(s[:, 0:half], s[:, 0:half], -1.0, None, ALU.mult))

            rsqrt(R_NORM0)
            rsqrt(R_NORM0 + 1)
            pool.wait_ge(tab_in, 16 * 7)
            build_tables(lambda k, t: (tab0[:, k, t, 0, :], tab0[:, k, t, 1, :]), raw_gains, 32, 0, 0, 32)
            pool.engine_nop().then_inc(tabs_built, 1)
            for r in range(R_QK0, R_NORM1):
                rsqrt(r)
            pool.wait_ge(merged, 2)
            pool.dma_start(gain, A["l0_norm_ffn"].partition_broadcast(P)).then_inc(gain_loaded, 16)
            rsqrt(R_NORM1)
            rsqrt(R_NORM1 + 1)
            pool.wait_ge(transposed, X_NORM2)
            pool.dma_start(gain, A["l1_norm_attn"].partition_broadcast(P)).then_inc(gain_loaded, 16)
            pool.dma_start(lora_gain[:, 0:C_QR], A["l1_c_q_lora_norm"].partition_broadcast(P))\
                .then_inc(lora_loaded, 16)
            pool.dma_start(lora_gain[:, C_QR:C_QR + C_KVR], A["l1_c_kv_lora_norm"].partition_broadcast(P))\
                .then_inc(lora_loaded, 16)
            pool.dma_start(raw_gains1[:, 0, :], A["l1_c_q_norm"].partition_broadcast(P)).then_inc(lora_loaded, 16)
            pool.dma_start(raw_gains1[:, 1, :], A["l1_c_k_norm"].partition_broadcast(P)).then_inc(lora_loaded, 16)
            pool.wait_ge(lora_loaded, 64)
            build_tables(lambda k, t: (tab1[:, k, t, 0:96], tab1[:, k, t, 96:128]), raw_gains1, 16, 64, 64, 80)
            pool.engine_nop().then_inc(tabs_built, 1)
            for r in range(R_NORM2, R_NORM3):
                rsqrt(r)
            pool.wait_ge(merged, 4)
            pool.dma_start(gain, A["l1_norm_ffn"].partition_broadcast(P)).then_inc(gain_loaded, 16)
            pool.dma_start(triu, A["triu"]).then_inc(moe_loaded, 16)
            pool.dma_start(iota, A["iota"]).then_inc(moe_loaded, 16)
            pool.dma_start(arena1[:, 384:448], A["tie"]).then_inc(moe_loaded, 16)
            pool.memset(ones, 1.0).then_inc(pool_step, 1)
            steps[0] += 1
            pool.wait_ge(pool_step, steps[0])
            pool.memset(y_exp, 0.0).then_inc(y_evac, 1)
            pool.memset(scatT, 0.0).then_inc(y_evac, 1)
            pool.memset(onehot[:, :, NE, :], 0.0).then_inc(pool_step, 1)
            steps[0] += 1
            pool.wait_ge(pool_step, steps[0])
            pool.engine_nop().then_inc(tabs_built, 1)
            rsqrt(R_NORM3)
            rsqrt(R_NORM3 + 1)

        @block.scalar
        def _(a):
            steps = [0]

            def link(ins):
                steps[0] += 1
                ins.then_inc(act_step, 1)
                a.wait_ge(act_step, steps[0])

            for t in range(NT):
                a.dma_start(x[:, t, :], A["x"][0, t * P:(t + 1) * P, :]).then_inc(x_loaded, 16)
            a.dma_start(gain, A["l0_norm_attn"].partition_broadcast(P)).then_inc(gain0_loaded, 16)
            a.dma_start(ident[:, :], A["ident"]).then_inc(early_loaded, 16)
            for k, name in enumerate(("l0_a_q_norm", "l0_a_k_norm", "l0_b_q_norm", "l0_b_k_norm")):
                a.dma_start(raw_gains[:, k, :], A[name].partition_broadcast(P)).then_inc(tab_in, 16)
            for t in range(NT):
                a.dma_start(rope[:, t, :], A["rope"][t * P:(t + 1) * P, :]).then_inc(tab_in, 16)
            a.dma_start(arena3[:, D + 256:D + 512],
                        A["l0_a_lambda"].rearrange("k d -> (k d)").partition_broadcast(P)).then_inc(tab_in, 16)
            a.dma_start(masks[:, :, :], A["masks"]).then_inc(early_loaded, 16)
            a.dma_start(subln[:, :], A["l0_a_subln"].partition_broadcast(P)).then_inc(early_loaded, 16)
            a.dma_start(sinks[:, :], A["l0_b_sinks"].partition_broadcast(P)).then_inc(early_loaded, 16)
            a.dma_start(rw[:, :, :], A["l1_router"].rearrange("(c p) e -> p c e", p=P)).then_inc(early_loaded, 16)

            def split_piece(u, n, e=None):
                a.wait_ge(ring_loaded[u % RING], per(16 * (u // RING + 1), e, 16 * NU // RING))
                if u >= SLOTS:
                    a.wait_ge(used, per(u - SLOTS + 1, e, NU))
                a.activation(w_hi[:, u % SLOTS, 0:n], ring[:, u % RING, 0:n], ACT.Copy).then_inc(hi_ready, 1)

            def after(u, task=None):
                if task is not None:
                    a.wait_ge(used, u + 1)
                    task()
                v = u + SLOTS
                split_piece(v, piece_floats(STREAM[v]) if v < U0 else PIECE)

            def split_bank(i, dst, src, e=None, step=0):
                a.wait_ge(transposed, per(i + 1, e, step))
                a.activation(dst, src, ACT.Copy).then_inc(hi_split, 1)

            def split_h(i):
                for t in range(NT):
                    for g in range(2):
                        split_bank(i + 2 * t + g, hT_hi[:, 4 * g:4 * g + 4, t * P:(t + 1) * P],
                                   bank(2 * t + g).rearrange("p (c n) -> p c n", c=4))

            def norm_squares(r, i):
                for t in range(NT):
                    if i < 0:
                        a.wait_ge(x_loaded, 32)
                    else:
                        a.wait_ge(x_updated, 4 * i + 4)
                    a.activation(h[:, t, :], x[:, t, :], ACT.Square,
                                 accum_out=stat[:, R_OFF[r + t]:R_OFF[r + t] + 1]).then_inc(squared, 1)

            def attention(s0, kind, heads_exp):
                for i in range(17):
                    if i < 16:
                        t, p = i // 8, i % 8
                        nk = P * (t + 1)
                        a.wait_ge(bias_ready, s0 + i + 1)
                        sm = small[:, i % 2, :]
                        scale = heads_exp
                        with_sink = kind == "AB" and p >= 4
                        for m in range(2):
                            ins = a.activation(probs[:, i % 2, m, 0:nk], probs[:, i % 2, m, 0:nk], ACT.Exp,
                                               bias=sm[:, 2 + m:3 + m], scale=scale,
                                               accum_out=sm[:, 4 + m:5 + m])
                        if with_sink:
                            ins = a.activation(sm[:, 8:10], sm[:, 6:8], ACT.Exp)
                        ins.then_inc(exp_done, 1)
                    if i >= 1:
                        j = i - 1
                        t, p = j // 8, j % 8
                        nb = (t + 1) * (1 if kind == "AB" and p < 4 else 2)
                        a.wait_ge(probs_transposed, s0 + j + 1)
                        if j >= 2:
                            a.wait_ge(pv_done, s0 + j - 1)
                        a.activation(probsT[:, j % 2, 0:nb, :],
                                     bank(2 + j % 2)[:, 0:nb * P].rearrange("p (b n) -> p b n", b=nb),
                                     ACT.Copy).then_inc(probsT_ready, 1)
                    if kind == "AB" and i >= 1 and (i - 1) % 8 == 7:
                        t = (i - 1) // 8
                        a.wait_ge(pv_done, s0 + 8 * t + 4)
                        for hd in range(A_HEADS):
                            c = R_OFF[R_SUB + t] + hd
                            ins = a.activation(h[:, t, hd * P:(hd + 1) * P], bank(4)[:, hd * P:(hd + 1) * P],
                                               ACT.Square, accum_out=stat[:, c:c + 1])
                        ins.then_inc(squared, 1)

            for u in range(SLOTS):
                split_piece(u, piece_floats(STREAM[u]))
            norm_squares(R_NORM0, -1)
            split_h(X_NORM0)

            def evacuate(dst, b):
                a.activation(dst, b, ACT.Copy).then_inc(evacuated, 1)

            k = 0
            for i, (_, n, c0, c1, w) in enumerate(IN0):
                def task():
                    for t in range(NT):
                        dst, src = z[:, t, n * COLS:n * COLS + w], bank((4 + 2 * n + t) % 8)[:, 0:w]
                        if n * COLS == ZB_Q:
                            dst = dst.rearrange("p (s m d) -> p m s d", s=4, m=2)
                            src = src.rearrange("p (m s d) -> p m s d", s=4, m=2)
                        evacuate(dst, src)
                after(i, task if c1 == KC else None)
            for t in range(NT):
                if t == 0:
                    a.wait_ge(normed, 2)
                    a.wait_ge(tabs_built, 1)
                    a.wait_ge(lam_exp, 1)
                    a.activation(lam[:, 2:4], lam[:, 0:2], ACT.Exp).then_inc(lam_exp, 1)
                    a.wait_ge(evacuated, 10)
                else:
                    a.wait_ge(ms_ready, R_QK0 + 1)
                a.activation(sq[:, 0:N_QK_A * HD], z[:, t, 0:N_QK_A * HD], ACT.Square)
                a.activation(sq[:, N_QK_A * HD:26 * HD], z[:, t, ZB_Q:ZB_Q + N_QK_B * HD], ACT.Square)\
                    .then_inc(squared, 1)

            def copy_heads(i, dst, b):
                a.wait_ge(qk_transposed, i + 1)
                a.activation(dst, b, ACT.Copy).then_inc(qkT_ready, 1)

            for t in range(NT):
                for g in range(4):
                    m = min(4, 13 - 4 * g)
                    copy_heads(4 * t + g, qkT0[:, 4 * g:4 * g + m, t * P:(t + 1) * P],
                               bank(4 * t + g)[:, 0:m * P].rearrange("p (s n) -> p s n", s=m))
            attention(0, "AB", HD ** -0.5)
            split_h(X_MERGE0)
            for i in range(len(OUT0)):
                after(first(OUT0) + i)
            norm_squares(R_NORM1, 0)
            split_h(X_NORM1)
            f0 = first(FFN)
            for i, (name, k, c0, c1, w) in enumerate(FFN):
                def exps():
                    for t in range(NT):
                        if k >= 1:
                            a.wait_ge(act_ready, 2 * k)
                        a.activation(sig[:, t, 0:w], bank(t)[:, 0:w], ACT.Tanh, scale=0.5).then_inc(sig_ready, 1)

                def split_act(kk, ww):
                    for t in range(NT):
                        nj = ww // P
                        split_bank(X_FFN + 2 * kk + t, aT_hi[:, 0:nj, t * P:(t + 1) * P],
                                   bank(t)[:, 0:ww].rearrange("p (j n) -> p j n", j=nj))
                after(f0 + i, exps if name == "ffn_g" and c1 == KC else None)
                if name == "ffn_u" and c1 == KC and k == 0:
                    split_act(0, w)
                if name == "ffn_d" and c1 * P == w and k + 1 < FFN_CHUNKS:
                    split_act(k + 1, min(COLS, FF - (k + 1) * COLS))
            norm_squares(R_NORM2, 1)
            split_h(X_NORM2)
            for i, (_, n, c0, c1, w) in enumerate(IN1):
                def task():
                    for t in range(NT):
                        evacuate(z1[:, t, :], bank(4 + t)[:, 0:w])
                after(first(IN1) + i, task if c1 == KC else None)
            a.wait_ge(evacuated, 12)
            for t in range(NT):
                o = R_OFF[R_LORA + t]
                a.activation(hflat[:, 0:C_QR], z1[:, t, 0:C_QR], ACT.Square, accum_out=stat[:, o:o + 1])\
                    .then_inc(act_step, 1)
                a.activation(hflat[:, C_QR:C_QR + C_KVR], z1[:, t, C_QR:C_QR + C_KVR], ACT.Square,
                             accum_out=stat[:, o + 1:o + 2]).then_inc(squared, 1)
                steps[0] += 1
                if t == 0:
                    a.wait_ge(squared, 11)
            for t in range(NT):
                split_bank(X_LORA + t, hT_hi[:, 0:3, t * P:(t + 1) * P],
                           bank(t)[:, 0:3 * P].rearrange("p (c n) -> p c n", c=3))
            for i, (_, n, c0, c1, w) in enumerate(UQ):
                def task():
                    for t in range(NT):
                        evacuate(qk1[:, t, n * COLS:n * COLS + w], bank(2 + 2 * n + t))
                after(first(UQ) + i, task)

            def squares1(q):
                for t in range(NT):
                    if t:
                        a.wait_ge(ms_ready, (R_Q1, R_K1)[q] + 1)
                    elif q == 0:
                        a.wait_ge(normed, 8)
                        a.wait_ge(tabs_built, 2)
                        a.wait_ge(evacuated, 18)
                    else:
                        a.wait_ge(evacuated, 34)
                    a.activation(sq[:, 0:1536], qk1[:, t, :], ACT.Square).then_inc(squared, 1)

            def heads1(q):
                dst = (qT1, kT1)[q]
                for t in range(NT):
                    for g in range(4):
                        copy_heads(8 + 8 * q + 4 * t + g, dst[0:C_QK, 4 * g:4 * g + 4, t * P:(t + 1) * P],
                                   bank(4 * t + g)[0:C_QK, :].rearrange("p (s n) -> p s n", s=4))

            squares1(0)
            heads1(0)

            def kv_out():
                for t in range(NT):
                    kb = qk1[:, t, :].rearrange("p (s n) -> p s n", n=C_QK)
                    vb = v1[:, t, :].rearrange("p (s n) -> p s n", n=C_V)
                    for n in range(4):
                        src = bank(4 * t + n).rearrange("p (s n) -> p s n", n=C_NOPE + C_V)
                        evacuate(kb[:, 4 * n:4 * n + 4, 0:C_NOPE], src[:, :, 0:C_NOPE])
                        evacuate(vb[:, 4 * n:4 * n + 4, :], src[:, :, C_NOPE:])
                    if t == 0:
                        pass
                for t in range(NT):
                    kb = qk1[:, t, :].rearrange("p (s n) -> p s n", n=C_QK)
                    ins = a.activation(kb[:, :, C_NOPE:], bc(z1[:, t, C_QR + C_KVR:C_IN], 1, C_HEADS), ACT.Copy)
                    link(ins)

            after(first(UKV), kv_out)
            squares1(1)
            heads1(1)
            attention(16, "C", C_QK ** -0.5)
            split_h(X_MERGE1)
            for i in range(len(OUT1)):
                after(first(OUT1) + i)
            norm_squares(R_NORM3, 2)
            split_h(X_NORM3)
            a.wait_ge(router_step, 1)
            for t in range(NT):
                a.activation(rt[:, 16 * t:16 * t + 8], rt[:, 32 + 8 * t:40 + 8 * t], ACT.Exp,
                             bias=rt[:, 48 + t:49 + t]).then_inc(logit_exp, 1)

            def expert_pass(p):
                ub = U0 + p * NE * NU
                xb = X_EXP + p * X_PER_PASS
                cb = NT * FFN_CHUNKS + p * NE * EXP_CHUNKS
                gb = NT * FFN_CHUNKS + p * NE * EXP_CHUNKS

                def gather_split(i, e=None):
                    for g in range(2):
                        split_bank(i + g, hT_hi[:, 4 * g:4 * g + 4, 0:P],
                                   bank(6 + g).rearrange("p (c n) -> p c n", c=4), e, 9)

                for b in range(4):
                    a.wait_ge(scat_transposed, 4 * p + b + 1)
                    a.activation(scatT_all[:, 2 * b:2 * b + 2, :],
                                 bank(b).rearrange("p (e n) -> p e n", e=2), ACT.Copy).then_inc(scat_ready, 1)
                gather_split(xb)
                with a.Fori(0, NE) as e:
                    for i, (kind, k, half) in enumerate(EXP):
                        a.wait_ge(used, per(ub + i + 1, e, NU))
                        if kind == "g" and half:
                            a.wait_ge(act_ready, per(cb + k - 1, e, EXP_CHUNKS))
                            a.activation(sig[:, k % 2, :], bank(k % 2), ACT.Tanh, scale=0.5).then_inc(sig_ready, 1)
                        if kind == "u" and half == 0 and k >= 1:
                            split_bank(xb + 2 + k - 1, aT_hi[:, :, 0:P],
                                       bank(6).rearrange("p (j n) -> p j n", j=4), e, 9)
                        if kind == "u" and half and k == 0:
                            a.wait_ge(scattered, per(4 + p * 4 * (NE + 1), e, 4))
                            if p == 0:
                                a.wait_ge(scat_ready, 4)
                            a.activation(scatT, scatT_all[:, bass.ds(e, 1), :].rearrange("p e n -> p (e n)"),
                                         ACT.Copy)
                        if kind == "u" and half and k == EXP_CHUNKS - 1:
                            gather_split(xb + 2 + 6, e)
                        if kind == "d" and half and k == EXP_CHUNKS - 2:
                            split_bank(xb + 2 + 8, aT_hi[:, :, 0:P],
                                       bank(6).rearrange("p (j n) -> p j n", j=4), e, 9)
                        if kind == "d" and half and k == EXP_CHUNKS - 1:
                            for n in range(2):
                                a.activation(y_exp[:, n * COLS:(n + 1) * COLS], bank(4 + n), ACT.Copy)\
                                    .then_inc(y_evac, 1)
                        split_piece(ub + i + SLOTS, PIECE, e)

            expert_pass(0)
            a.wait_ge(flag_ready, 1)
            most = a.value_load(nmax_i[0:1, 0:1], min_val=0, max_val=SEQ)
            with a.If(most > P):
                expert_pass(1)
            a.wait_ge(stored, 1)
            for t in range(NT):
                a.dma_start(A["out"][0, t * P:(t + 1) * P, :], x[:, t, :]).then_inc(stored, 16)
            a.wait_ge(stored, 33)

        @block.vector
        def _(v):
            steps = [0]

            def link(ins):
                steps[0] += 1
                ins.then_inc(dve_step, 1)
                v.wait_ge(dve_step, steps[0])

            def split_piece(u, n, e=None):
                v.wait_ge(hi_ready, per(u + 1, e, NU))
                v.tensor_tensor(w_lo[:, u % SLOTS, 0:n], ring[:, u % RING, 0:n],
                                w_hi[:, u % SLOTS, 0:n].bitcast(f32), ALU.subtract).then_inc(lo_ready, 1)

            def after(u, task=None):
                if task is not None:
                    v.wait_ge(used, u + 1)
                    task()
                w = u + SLOTS
                split_piece(w, piece_floats(STREAM[w]) if w < U0 else PIECE)

            def split_bank(i, dst, hi, src, e=None, step=0):
                v.wait_ge(hi_split, per(i + 1, e, step))
                v.tensor_tensor(dst, src, hi.bitcast(f32), ALU.subtract).then_inc(lo_split, 1)

            def split_h(i):
                for t in range(NT):
                    for g in range(2):
                        s = (slice(None), slice(4 * g, 4 * g + 4), slice(t * P, (t + 1) * P))
                        split_bank(i + 2 * t + g, hT_lo[s], hT_hi[s],
                                   bank(2 * t + g).rearrange("p (c n) -> p c n", c=4))

            def mean_square(r, inv, cols=None):
                s = stat[:, R_OFF[r]:R_OFF[r] + R_COLS[r]]
                v.tensor_scalar(s, s, inv, EPS, ALU.mult, ALU.add).then_inc(ms_ready, 1)

            def norm(i, r, nsq):
                for t in range(NT):
                    v.wait_ge(squared, nsq + t + 1)
                    mean_square(r + t, 1.0 / D)
                for t in range(NT):
                    v.wait_ge(rstd_ready, r + t + 1)
                    if t == 0 and i == 0:
                        v.wait_ge(gain0_loaded, 16)
                    elif t == 0:
                        v.wait_ge(gain_loaded, 16 * i)
                    v.scalar_tensor_tensor(out=h[:, t, :], in0=x[:, t, :], scalar=stat[:, R_OFF[r + t]:R_OFF[r + t] + 1],
                                           in1=gain, op0=ALU.mult, op1=ALU.mult).then_inc(normed, 1)

            def rotate(zt, gr, nh, width, lead, half, cos, sin, tmp):
                s = zt.rearrange("p (s n) -> p s n", n=width)
                link(v.tensor_tensor(tmp[:, :, 0:half], s[:, :, lead + half:lead + 2 * half],
                                     bc(sin[:, 0:half], 1, nh), ALU.mult))
                link(v.tensor_tensor(tmp[:, :, half:2 * half], s[:, :, lead:lead + half],
                                     bc(sin[:, half:2 * half], 1, nh), ALU.mult))
                link(v.tensor_tensor(s, s, bc(cos, 1, nh), ALU.mult))
                link(v.tensor_tensor(s[:, :, lead:], s[:, :, lead:], tmp, ALU.add))

            def attention(s0, kind, scale):
                def front(i):
                    t, p = i // 8, i % 8
                    nk = P * (t + 1)
                    with_sink = kind == "AB" and p >= 4
                    sm = small[:, i % 2, :]
                    pr = probs[:, i % 2, :, 0:nk]
                    mask = masks[:, 0, P:SEQ] if t == 0 else masks[:, 1 if with_sink else 0, :]
                    v.wait_ge(scored, s0 + i + 1)
                    if i >= 2:
                        v.wait_ge(probs_transposed, s0 + i - 1)
                    v.tensor_tensor(pr, PS[:, 6 * (i % 2):6 * (i % 2) + 2, 0:nk],
                                    bc(mask, 1, 2), ALU.add).then_inc(masked, 1)
                    v.wait_ge(masked, s0 + i + 1)
                    link(v.tensor_reduce(sm[:, 0:2], pr, AX.X, ALU.max))
                    if with_sink:
                        snk = sinks[:, p - 4:p - 4 + 5:4]
                        link(v.scalar_tensor_tensor(out=sm[:, 10:12], in0=sm[:, 0:2], scalar=scale, in1=snk,
                                                    op0=ALU.mult, op1=ALU.max))
                        link(v.tensor_scalar(sm[:, 2:4], sm[:, 10:12], -1.0, None, ALU.mult))
                        v.tensor_tensor(sm[:, 6:8], sm[:, 2:4], snk, ALU.add).then_inc(bias_ready, 1)
                    else:
                        v.tensor_scalar(sm[:, 2:4], sm[:, 0:2], -scale, None, ALU.mult).then_inc(bias_ready, 1)

                def back(i):
                    t, p = i // 8, i % 8
                    nk = P * (t + 1)
                    sm = small[:, i % 2, :]
                    v.wait_ge(exp_done, s0 + i + 1)
                    if kind == "C":
                        v.reciprocal(rinv[:, t, 2 * p:2 * p + 2], sm[:, 4:6]).then_inc(probs_ready, 1)
                    elif p >= 4:
                        link(v.tensor_tensor(sm[:, 4:6], sm[:, 4:6], sm[:, 8:10], ALU.add))
                        v.reciprocal(rinv[:, t, p - 4:p - 4 + 5:4], sm[:, 4:6]).then_inc(probs_ready, 1)
                    else:
                        link(v.reciprocal(sm[:, 12:14], sm[:, 4:6]))
                        link(v.tensor_scalar(sm[:, 14:15], sm[:, 13:14], lam[:, 4:5], None, ALU.mult))
                        p0, p1 = probs[:, i % 2, 0, 0:nk], probs[:, i % 2, 1, 0:nk]
                        link(v.tensor_scalar(p0, p0, sm[:, 12:13], None, ALU.mult))
                        v.scalar_tensor_tensor(out=p0, in0=p1, scalar=sm[:, 14:15], in1=p0,
                                               op0=ALU.mult, op1=ALU.add).then_inc(probs_ready, 1)

                def final(t):
                    v.wait_ge(pv_done, s0 + 8 * t + 8)
                    if kind == "AB":
                        o = R_OFF[R_SUB + t]
                        v.wait_ge(squared, 5 + t)
                        mean_square(R_SUB + t, 1.0 / A_VD)
                        link(v.tensor_tensor(h[:, t, 512:1024].rearrange("p (s n) -> p s n", n=HD),
                                             bank(5).rearrange("p (s n) -> p s n", n=HD),
                                             bc(rinv[:, t, 0:8], 2, HD), ALU.mult))
                        v.wait_ge(rstd_ready, R_SUB + t + 1)
                        ha = h[:, t, 0:512].rearrange("p (s n) -> p s n", n=A_VD)
                        link(v.tensor_tensor(ha, bank(4).rearrange("p (s n) -> p s n", n=A_VD),
                                             bc(stat[:, o:o + 4], 2, A_VD), ALU.mult))
                        v.tensor_tensor(ha, ha, bc(subln[:, :], 1, A_HEADS), ALU.mult).then_inc(merged, 1)
                    else:
                        for n in range(2):
                            ins = v.tensor_tensor(h[:, t, n * 512:(n + 1) * 512].rearrange("p (s n) -> p s n", n=C_V),
                                                  bank(4 + n).rearrange("p (s n) -> p s n", n=C_V),
                                                  bc(rinv[:, t, 8 * n:8 * n + 8], 2, C_V), ALU.mult)
                        ins.then_inc(merged, 1)

                for i in range(19):
                    if i < 16:
                        front(i)
                    if 1 <= i <= 16:
                        back(i - 1)
                    if i == 9:
                        final(0)
                    if i == 18:
                        final(1)

            def residual(u0, pieces, xu):
                for i, (_, n, c0, c1, w) in enumerate(pieces):
                    def task():
                        for t in range(NT):
                            xs = x[:, t, n * COLS:(n + 1) * COLS]
                            v.tensor_tensor(xs, xs, bank(4 + 2 * n + t), ALU.add).then_inc(x_updated, 1)
                    after(u0 + i, task if c1 == KC else None)

            for u in range(SLOTS):
                split_piece(u, piece_floats(STREAM[u]))
            v.wait_ge(early_loaded, 80)
            link(v.tensor_copy(rw_hi[:, :, :], rw[:, :, :]))
            link(v.tensor_tensor(rw_lo[:, :, :], rw[:, :, :], rw_hi[:, :, :].bitcast(f32), ALU.subtract))
            link(v.tensor_scalar(subln[:, :], subln[:, :], 1.0 - LAM_INIT, None, ALU.mult))
            norm(0, R_NORM0, 0)
            split_h(X_NORM0)
            for i in range(len(IN0)):
                after(i)
            v.wait_ge(tab_in, 16 * 7)
            link(v.tensor_tensor(rope_tmp[:, 0:HD], raw_lam[:, 0, :], raw_lam[:, 1, :], ALU.mult))
            link(v.tensor_tensor(rope_tmp[:, HD:2 * HD], raw_lam[:, 2, :], raw_lam[:, 3, :], ALU.mult))
            v.tensor_reduce(lam[:, 0:2], rope_tmp[:, 0:2 * HD].rearrange("p (k n) -> p k n", k=2), AX.X, ALU.add)\
                .then_inc(lam_exp, 1)
            v.wait_ge(lam_exp, 2)
            link(v.tensor_tensor(lam[:, 4:5], lam[:, 3:4], lam[:, 2:3], ALU.subtract))
            link(v.tensor_scalar(lam[:, 4:5], lam[:, 4:5], -LAM_INIT, None, ALU.add))
            for t in range(NT):
                o = R_OFF[R_QK0 + t]
                v.wait_ge(squared, 3 + t)
                link(v.tensor_reduce(stat[:, o:o + 26], sq.rearrange("p (s n) -> p s n", n=HD), AX.X, ALU.add))
                mean_square(R_QK0 + t, 1.0 / HD)
                v.wait_ge(rstd_ready, R_QK0 + t + 1)
                for c0, nh, so in ((0, N_QK_A, 0), (ZB_Q, N_QK_B, N_QK_A)):
                    s = z[:, t, c0:c0 + nh * HD].rearrange("p (s n) -> p s n", n=HD)
                    link(v.tensor_tensor(s, s, bc(stat[:, o + so:o + so + nh], 2, HD), ALU.mult))
                for kk, (c0, nh) in enumerate(((ZA_Q, 8), (ZA_K, 8), (ZB_Q, 8), (ZB_K, 2))):
                    rotate(z[:, t, c0:c0 + nh * HD], None, nh, HD, 0, HD // 2, tab0[:, kk, t, 0, :],
                           tab0[:, kk, t, 1, :], rope_tmp[:, 0:nh * HD].rearrange("p (s n) -> p s n", n=HD))
                v.engine_nop().then_inc(qk_normed, 1)
            attention(0, "AB", HD ** -0.5)
            split_h(X_MERGE0)
            residual(first(OUT0), OUT0, 0)
            norm(1, R_NORM1, 6)
            split_h(X_NORM1)
            f0 = first(FFN)

            def silu(src_g, src_u, sg, ac, base):
                v.scalar_tensor_tensor(out=ac, in0=sg, scalar=1.0, in1=src_g, op0=ALU.add, op1=ALU.mult)\
                    .then_inc(silu_step, 1)
                v.wait_ge(silu_step, base + 1)
                v.scalar_tensor_tensor(out=ac, in0=ac, scalar=0.5, in1=src_u, op0=ALU.mult, op1=ALU.mult)\
                    .then_inc(act_ready, 1)

            for i, (name, k, c0, c1, w) in enumerate(FFN):
                def silus():
                    for t in range(NT):
                        v.wait_ge(sig_ready, 2 * k + t + 1)
                        silu(bank(t)[:, 0:w], bank(2 + t)[:, 0:w], sig[:, t, 0:w], act[:, t, 0:w],
                             2 * k + t)

                def split_act(kk, ww):
                    nj = ww // P
                    for t in range(NT):
                        s = (slice(None), slice(0, nj), slice(t * P, (t + 1) * P))
                        split_bank(X_FFN + 2 * kk + t, aT_lo[s], aT_hi[s],
                                   bank(t)[:, 0:ww].rearrange("p (j n) -> p j n", j=nj))
                after(f0 + i, silus if name == "ffn_u" and c1 == KC else None)
                if name == "ffn_u" and c1 == KC and k == 0:
                    split_act(0, w)
                if name == "ffn_d" and c1 * P == w and k + 1 < FFN_CHUNKS:
                    split_act(k + 1, min(COLS, FF - (k + 1) * COLS))
            v.wait_ge(used, f0 + len(FFN))
            for t in range(NT):
                for n in range(2):
                    xs = x[:, t, n * COLS:(n + 1) * COLS]
                    v.tensor_tensor(xs, xs, bank(4 + 2 * t + n), ALU.add).then_inc(x_updated, 1)
            norm(2, R_NORM2, 8)
            split_h(X_NORM2)
            for i in range(len(IN1)):
                after(first(IN1) + i)
            for t in range(NT):
                o = R_OFF[R_LORA + t]
                v.wait_ge(squared, 11 + t)
                link(v.tensor_scalar(stat[:, o:o + 1], stat[:, o:o + 1], 1.0 / C_QR, EPS, ALU.mult, ALU.add))
                v.tensor_scalar(stat[:, o + 1:o + 2], stat[:, o + 1:o + 2], 1.0 / C_KVR, EPS, ALU.mult, ALU.add)\
                    .then_inc(ms_ready, 1)
            v.wait_ge(lora_loaded, 64)
            for t in range(NT):
                o = R_OFF[R_LORA + t]
                v.wait_ge(rstd_ready, R_LORA + t + 1)
                for j, (c0, c1) in enumerate(((0, C_QR), (C_QR, C_QR + C_KVR))):
                    zz = z1[:, t, c0:c1]
                    ins = v.scalar_tensor_tensor(out=zz, in0=zz, scalar=stat[:, o + j:o + j + 1],
                                                 in1=lora_gain[:, c0:c1], op0=ALU.mult, op1=ALU.mult)
                ins.then_inc(normed, 1)
            for t in range(NT):
                s = (slice(None), slice(0, 3), slice(t * P, (t + 1) * P))
                split_bank(X_LORA + t, hT_lo[s], hT_hi[s], bank(t)[:, 0:3 * P].rearrange("p (c n) -> p c n", c=3))
            for i in range(len(UQ)):
                after(first(UQ) + i)

            def norm_heads1(q, r, nsq):
                for t in range(NT):
                    o = R_OFF[r + t]
                    v.wait_ge(squared, nsq + t)
                    s = qk1[:, t, :].rearrange("p (s n) -> p s n", n=C_QK)
                    link(v.tensor_reduce(stat[:, o:o + 16], sq[:, 0:1536].rearrange("p (s n) -> p s n", n=C_QK),
                                         AX.X, ALU.add))
                    mean_square(r + t, 1.0 / C_QK)
                    v.wait_ge(rstd_ready, r + t + 1)
                    link(v.tensor_tensor(s, s, bc(stat[:, o:o + 16], 2, C_QK), ALU.mult))
                    rotate(qk1[:, t, :], None, C_HEADS, C_QK, C_NOPE, C_ROPE // 2, tab1[:, q, t, 0:96],
                           tab1[:, q, t, 96:128], rope_tmp[:, 0:512].rearrange("p (s n) -> p s n", n=C_ROPE))
                    v.engine_nop().then_inc(qk_normed, 1)

            v.wait_ge(tabs_built, 2)
            norm_heads1(0, R_Q1, 13)
            after(first(UKV))
            norm_heads1(1, R_K1, 15)
            attention(16, "C", C_QK ** -0.5)
            split_h(X_MERGE1)
            residual(first(OUT1), OUT1, 2)
            norm(3, R_NORM3, 16)
            split_h(X_NORM3)
            L = rt[:, 32:48]
            v.wait_ge(routed, 2)
            v.wait_ge(moe_loaded, 48)
            v.wait_ge(tabs_built, 3)
            for t in range(NT):
                link(v.tensor_copy(L[:, 8 * t:8 * t + 8], bank(4 + t)[:, 0:NE]))
                link(v.tensor_reduce(rt[:, 50 + t:51 + t], L[:, 8 * t:8 * t + 8], AX.X, ALU.max))
            v.tensor_scalar(rt[:, 48:50], rt[:, 50:52], -1.0, None, ALU.mult).then_inc(router_step, 1)
            gt = rt[:, 64:128].rearrange("p (e f) -> p e f", e=NE)
            eq = rt[:, 128:192].rearrange("p (e f) -> p e f", e=NE)
            sel = rt[:, 192:208]
            gates = rt[:, 208:224]
            for t in range(NT):
                Lt = L[:, 8 * t:8 * t + 8]
                link(v.tensor_tensor(gt, bc(Lt, 1, NE), bc(Lt, 2, NE), ALU.is_gt))
                link(v.tensor_tensor(eq, bc(Lt, 1, NE), bc(Lt, 2, NE), ALU.is_equal))
                link(v.tensor_tensor(eq, eq, tie, ALU.mult))
                link(v.tensor_tensor(gt, gt, eq, ALU.add))
                link(v.tensor_reduce(sel[:, 8 * t:8 * t + 8], gt, AX.X, ALU.add))
                link(v.tensor_scalar(sel[:, 8 * t:8 * t + 8], sel[:, 8 * t:8 * t + 8], 1.5, None, ALU.is_lt))
            v.engine_nop().then_inc(ranks_ready, 1)
            v.wait_ge(logit_exp, 2)
            for t in range(NT):
                g = gates[:, 8 * t:8 * t + 8]
                link(v.tensor_tensor(g, rt[:, 16 * t:16 * t + 8], sel[:, 8 * t:8 * t + 8], ALU.mult))
                link(v.tensor_reduce(rt[:, 52 + t:53 + t], g, AX.X, ALU.add))
                link(v.reciprocal(rt[:, 54 + t:55 + t], rt[:, 52 + t:53 + t]))
                link(v.tensor_scalar(g, g, rt[:, 54 + t:55 + t], None, ALU.mult))
            slot = rt[:, 224:240]
            v.wait_ge(counted, 1)
            for t in range(NT):
                st = slot[:, 8 * t:8 * t + 8]
                link(v.scalar_tensor_tensor(out=st, in0=bank(6)[:, 8 * t:8 * t + 8], scalar=1.0,
                                            in1=sel[:, 8 * t:8 * t + 8], op0=ALU.add, op1=ALU.mult))
                link(v.tensor_scalar(st, st, -1.0, None, ALU.add))
            link(v.tensor_reduce(nmax[0:1, :], bank(6)[0:1, 16:24], AX.X, ALU.max))
            v.tensor_copy(nmax_i[0:1, :], nmax[0:1, :]).then_inc(flag_ready, 1)

            def expert_pass(p):
                ub = U0 + p * NE * NU
                xb = X_EXP + p * X_PER_PASS
                cb = NT * FFN_CHUNKS + p * NE * EXP_CHUNKS
                sb_ = p * 4 * (NE + 1)

                def gather_split(i, e=None):
                    for g in range(2):
                        s = (slice(None), slice(4 * g, 4 * g + 4), slice(0, P))
                        split_bank(i + g, hT_lo[s], hT_hi[s], bank(6 + g).rearrange("p (c n) -> p c n", c=4), e, 9)

                def act_split(i, e):
                    s = (slice(None), slice(0, 4), slice(0, P))
                    split_bank(i, aT_lo[s], aT_hi[s], bank(6).rearrange("p (j n) -> p j n", j=4), e, 9)

                def add_scattered(i, e=None):
                    v.wait_ge(scattered, per(sb_ + i + 1, e, 4))
                    xs = x[:, i % 4 // 2, (i % 2) * COLS:(i % 2 + 1) * COLS]
                    v.tensor_tensor(xs, xs, bank(6 + i % 2), ALU.add).then_inc(scat_added, 1)

                if p:
                    link_free = v.tensor_scalar(slot, slot, -float(P), None, ALU.add)
                    link_free.then_inc(router_step, 1)
                    v.wait_ge(router_step, 2)
                for t in range(NT):
                    oh = onehot[:, t, 0:NE, :]
                    v.tensor_tensor(oh, bc(iota, 1, NE), bc(slot[:, 8 * t:8 * t + 8], 2, P), ALU.is_equal)\
                        .then_inc(onehot_ready, 1)
                    v.wait_ge(onehot_ready, 4 * p + 2 * t + 1)
                    v.tensor_tensor(onehot_gated[:, t, :, :], oh, bc(gates[:, 8 * t:8 * t + 8], 2, P), ALU.mult)\
                        .then_inc(onehot_ready, 1)
                gather_split(xb)
                with v.Fori(0, NE) as e:
                    for i, (kind, k, half) in enumerate(EXP):
                        v.wait_ge(used, per(ub + i + 1, e, NU))
                        if kind == "g" and half:
                            v.wait_ge(sig_ready, per(cb + k + 1, e, EXP_CHUNKS))
                            sg, ac = sig[:, k % 2, :], act[:, k % 2, :]
                            v.scalar_tensor_tensor(out=ac, in0=sg, scalar=1.0, in1=bank(k % 2), op0=ALU.add,
                                                   op1=ALU.mult).then_inc(silu_step, 1)
                            if k == 0:
                                for q in range(2):
                                    add_scattered(q, e)
                        if kind == "u" and half == 0 and k == 0:
                            for q in range(2, 4):
                                add_scattered(q, e)
                        if kind == "u" and half == 0 and k >= 1:
                            act_split(xb + 2 + k - 1, e)
                        if kind == "u" and half:
                            ac = act[:, k % 2, :]
                            v.wait_ge(silu_step, per(cb + k + 1, e, EXP_CHUNKS))
                            v.scalar_tensor_tensor(out=ac, in0=ac, scalar=0.5, in1=bank(2 + k % 2), op0=ALU.mult,
                                                   op1=ALU.mult).then_inc(act_ready, 1)
                            if k == EXP_CHUNKS - 1:
                                gather_split(xb + 2 + 6, e)
                        if kind == "d" and half and k == EXP_CHUNKS - 2:
                            act_split(xb + 2 + 8, e)
                        split_piece(ub + i + SLOTS, PIECE, e)
                for q in range(4):
                    add_scattered(4 * NE + q)

            expert_pass(0)
            most = v.value_load(nmax_i[0:1, 0:1], min_val=0, max_val=SEQ)
            with v.If(most > P):
                expert_pass(1)
            v.engine_nop().then_inc(stored, 1)

        @block.tensor
        def _(pe):
            def product(out, xh, xl, wh, wl, start, stop):
                pe.matmul(out, xh, wh, start=start, stop=False)
                pe.matmul(out, xh, wl, start=False, stop=False)
                return pe.matmul(out, xl, wh, start=False, stop=stop)

            def transpose_h(i, waits):
                for t in range(NT):
                    waits(t)
                    for g in range(2):
                        for c in range(4):
                            cc = 4 * g + c
                            ins = pe.transpose(bank(2 * t + g)[:, c * P:(c + 1) * P], h[:, t, cc * P:(cc + 1) * P],
                                               ident[:, :])
                        ins.then_inc(transposed, 1)

            def normed_wait(n):
                return lambda t: pe.wait_ge(normed, n + t + 1)

            def piece_wait(u):
                pe.wait_ge(lo_ready, u + 1)

            def project(pieces, kc, bank_of, free=None):
                u0 = first(pieces)
                for i, (_, n, c0, c1, w) in enumerate(pieces):
                    u = u0 + i
                    piece_wait(u)
                    s = u % SLOTS
                    for t in range(NT):
                        if free is not None and c0 == 0:
                            free(n, t)
                        for c in range(c0, c1):
                            o = (c - c0) * w
                            ins = product(bank_of(n, t)[:, 0:w], hT_hi[:, c, t * P:(t + 1) * P],
                                          hT_lo[:, c, t * P:(t + 1) * P], w_hi[:, s, o:o + w], w_lo[:, s, o:o + w],
                                          c == 0, c == kc - 1)
                    ins.then_inc(used, 1)

            def attention(s0, kind):
                def scores(i):
                    t, p = i // 8, i % 8
                    nk = P * (t + 1)
                    if i >= 2:
                        pe.wait_ge(masked, s0 + i - 1)
                    for m in range(2):
                        if kind == "AB":
                            r = slice(m * HD, (m + 1) * HD)
                            q = qkT0[r, p if p < 4 else 8 + p - 4, t * P:(t + 1) * P]
                            kk = qkT0[r, 4 + p if p < 4 else 12, 0:nk]
                        else:
                            q = qT1[0:C_QK, 2 * p + m, t * P:(t + 1) * P]
                            kk = kT1[0:C_QK, 2 * p + m, 0:nk]
                        ins = pe.matmul(bank(6 * (i % 2) + m)[:, 0:nk], q, kk, start=True, stop=True)
                    ins.then_inc(scored, 1)

                def transposes(i):
                    t, p = i // 8, i % 8
                    maps = 1 if kind == "AB" and p < 4 else 2
                    pe.wait_ge(probs_ready, s0 + i + 1)
                    if i >= 2:
                        pe.wait_ge(probsT_ready, s0 + i - 1)
                    for m in range(maps):
                        for b in range(t + 1):
                            j = m * (t + 1) + b
                            ins = pe.transpose(bank(2 + i % 2)[:, j * P:(j + 1) * P],
                                               probs[:, i % 2, m, b * P:(b + 1) * P], ident[:, :])
                    ins.then_inc(probs_transposed, 1)

                def values(i):
                    t, p = i // 8, i % 8
                    pe.wait_ge(probsT_ready, s0 + i + 1)
                    if i == 8:
                        pe.wait_ge(merged, s0 // 8 + 1)
                    maps = 1 if kind == "AB" and p < 4 else 2
                    for m in range(maps):
                        if kind == "AB" and p < 4:
                            out = bank(4)[:, p * P:(p + 1) * P]
                            col, w = ZA_V + p * A_VD, A_VD
                        elif kind == "AB":
                            hd = p - 4 + 4 * m
                            out = bank(5)[:, hd * HD:(hd + 1) * HD]
                            col, w = ZB_V + m * HD, HD
                        else:
                            hd = 2 * p + m
                            out = bank(4 + hd // 8)[:, (hd % 8) * C_V:(hd % 8 + 1) * C_V]
                            col, w = hd * C_V, C_V
                        for b in range(t + 1):
                            vv = (z if kind == "AB" else v1)[:, b, col:col + w]
                            ins = pe.matmul(out, probsT[:, i % 2, m * (t + 1) + b, :], vv,
                                            start=b == 0, stop=b == t)
                    ins.then_inc(pv_done, 1)

                scores(0)
                for i in range(17):
                    if i + 1 < 16:
                        scores(i + 1)
                    if i < 16:
                        transposes(i)
                    if i >= 1:
                        values(i - 1)

            pe.wait_ge(early_loaded, 80)
            transpose_h(X_NORM0, normed_wait(0))

            def free0(n, t):
                k = 2 * n + t
                if n == 0:
                    pe.wait_ge(lo_split, X_NORM0 + 2 * t + 2)
                if k >= 8:
                    pe.wait_ge(evacuated, k - 7)
            project(IN0, KC, lambda n, t: bank((4 + 2 * n + t) % 8), free0)
            pe.wait_ge(evacuated, 10)
            for t in range(NT):
                pe.wait_ge(qk_normed, t + 1)
                for g in range(4):
                    for j in range(4 * g, min(4 * g + 4, 13)):
                        if j < 8:
                            src = z[:, t, j * P:(j + 1) * P]
                        else:
                            src = z[:, t, ZB_Q + (j - 8) * P:ZB_Q + (j - 7) * P]
                        ins = pe.transpose(bank(4 * t + g)[:, (j % 4) * P:(j % 4 + 1) * P], src, ident[:, :])
                    ins.then_inc(qk_transposed, 1)
            pe.wait_ge(qkT_ready, 8)
            attention(0, "AB")
            transpose_h(X_MERGE0, lambda t: pe.wait_ge(merged, t + 1))

            def split_wait(i):
                def free(n, t):
                    if n == 0:
                        pe.wait_ge(lo_split, i + 2 * t + 2)
                return free
            project(OUT0, KC, lambda n, t: bank(4 + 2 * n + t), split_wait(X_MERGE0))
            transpose_h(X_NORM1, normed_wait(2))
            pe.wait_ge(lo_split, X_NORM1 + 4)
            f0 = first(FFN)

            def transpose_act(k, w):
                for t in range(NT):
                    pe.wait_ge(act_ready, 2 * k + t + 1)
                    for j in range(w // P):
                        ins = pe.transpose(bank(t)[:, j * P:(j + 1) * P], act[:, t, j * P:(j + 1) * P], ident[:, :])
                    ins.then_inc(transposed, 1)

            for i, (name, k, c0, c1, w) in enumerate(FFN):
                u = f0 + i
                s = u % SLOTS
                piece_wait(u)
                for t in range(NT):
                    if name in ("ffn_g", "ffn_u"):
                        if name == "ffn_g" and c0 == 0 and k >= 1:
                            pe.wait_ge(lo_split, X_FFN + 2 * k + t - 1)
                        out = bank(t if name == "ffn_g" else 2 + t)[:, 0:w]
                        for c in range(c0, c1):
                            o = (c - c0) * w
                            ins = product(out, hT_hi[:, c, t * P:(t + 1) * P], hT_lo[:, c, t * P:(t + 1) * P],
                                          w_hi[:, s, o:o + w], w_lo[:, s, o:o + w], c == 0, c == KC - 1)
                    else:
                        if c0 == 0:
                            pe.wait_ge(lo_split, X_FFN + 2 * k + t + 1)
                        last = k == FFN_CHUNKS - 1
                        for j in range(c0, c1):
                            for n in range(2):
                                o = (j - c0) * D + n * COLS
                                ins = product(bank(4 + 2 * t + n), aT_hi[:, j, t * P:(t + 1) * P],
                                              aT_lo[:, j, t * P:(t + 1) * P], w_hi[:, s, o:o + COLS],
                                              w_lo[:, s, o:o + COLS], k == 0 and j == 0,
                                              last and j == w // P - 1)
                ins.then_inc(used, 1)
                if name == "ffn_u" and c1 == KC and k == 0:
                    transpose_act(0, w)
                if name == "ffn_d" and c1 * P == w and k + 1 < FFN_CHUNKS:
                    transpose_act(k + 1, min(COLS, FF - (k + 1) * COLS))
            transpose_h(X_NORM2, normed_wait(4))
            project(IN1, KC, lambda n, t: bank(4 + t), split_wait(X_NORM2))
            for t in range(NT):
                pe.wait_ge(normed, 7 + t)
                for c in range(3):
                    ins = pe.transpose(bank(t)[:, c * P:(c + 1) * P], z1[:, t, c * P:(c + 1) * P], ident[:, :])
                ins.then_inc(transposed, 1)

            def free_uq(n, t):
                if n == 0:
                    pe.wait_ge(lo_split, X_LORA + t + 1)
                    pe.wait_ge(evacuated, 12)
            project(UQ, 2, lambda n, t: bank(2 + 2 * n + t), free_uq)

            def transpose_heads1(q):
                for t in range(NT):
                    pe.wait_ge(qk_normed, 2 + 2 * q + t + 1)
                    for g in range(4):
                        for j in range(4):
                            hd = 4 * g + j
                            ins = pe.transpose(bank(4 * t + g)[0:C_QK, j * P:(j + 1) * P],
                                               qk1[:, t, hd * C_QK:(hd + 1) * C_QK], ident[:, :])
                        ins.then_inc(qk_transposed, 1)

            transpose_heads1(0)
            u = first(UKV)
            piece_wait(u)
            pe.wait_ge(qkT_ready, 16)
            for t in range(NT):
                for n in range(4):
                    o = n * COLS
                    ins = product(bank(4 * t + n), hT_hi[:, 2, t * P:(t + 1) * P], hT_lo[:, 2, t * P:(t + 1) * P],
                                  w_hi[:, u % SLOTS, o:o + COLS], w_lo[:, u % SLOTS, o:o + COLS], True, True)
            ins.then_inc(used, 1)
            transpose_heads1(1)
            pe.wait_ge(qkT_ready, 24)
            attention(16, "C")
            transpose_h(X_MERGE1, lambda t: pe.wait_ge(merged, 3 + t))
            project(OUT1, KC, lambda n, t: bank(4 + 2 * n + t), split_wait(X_MERGE1))
            transpose_h(X_NORM3, normed_wait(8))
            for t in range(NT):
                pe.wait_ge(lo_split, X_NORM3 + 2 * t + 2)
                for c in range(KC):
                    ins = product(bank(4 + t)[:, 0:NE], hT_hi[:, c, t * P:(t + 1) * P], hT_lo[:, c, t * P:(t + 1) * P],
                                  rw_hi[:, c, :], rw_lo[:, c, :], c == 0, c == KC - 1)
                ins.then_inc(routed, 1)
            pe.wait_ge(ranks_ready, 1)
            sel = rt[:, 192:208]
            pe.matmul(bank(6)[:, 0:8], triu, sel[:, 0:8], start=True, stop=True)
            pe.matmul(bank(6)[:, 8:16], ones, sel[:, 0:8], start=True, stop=False)
            pe.matmul(bank(6)[:, 8:16], triu, sel[:, 8:16], start=False, stop=True)
            pe.matmul(bank(6)[:, 16:24], ones, sel[:, 0:8], start=True, stop=False)
            pe.matmul(bank(6)[:, 16:24], ones, sel[:, 8:16], start=False, stop=True).then_inc(counted, 1)

            def expert_pass(p):
                ub = U0 + p * NE * NU
                xb = X_EXP + p * X_PER_PASS
                cb = NT * FFN_CHUNKS + p * NE * EXP_CHUNKS
                sb_ = p * 4 * (NE + 1)

                def gather(e):
                    for g in range(2):
                        for c in range(4):
                            for t in range(NT):
                                cc = 4 * g + c
                                if isinstance(e, int):
                                    oh = onehot[:, t, e, :]
                                else:
                                    oh = onehot[:, t, bass.ds(e, 1), :].rearrange("p e n -> p (e n)")
                                ins = pe.matmul(bank(6 + g)[:, c * P:(c + 1) * P], h[:, t, cc * P:(cc + 1) * P], oh,
                                                start=t == 0, stop=t == NT - 1)
                        ins.then_inc(transposed, 1)

                def scatter(q):
                    t, n = q // 2, q % 2
                    pe.matmul(bank(6 + n), scatT[:, t * P:(t + 1) * P], y_exp[:, n * COLS:(n + 1) * COLS],
                              start=True, stop=True).then_inc(scattered, 1)

                pe.wait_ge(onehot_ready, 4 * p + 4)
                if p:
                    pe.wait_ge(scat_added, 4 * (NE + 1))
                for b in range(4):
                    for j in range(4):
                        e, t = 2 * b + j // 2, j % 2
                        ins = pe.transpose(bank(b)[:, j * P:(j + 1) * P], onehot_gated[:, t, e, :], ident[:, :])
                    ins.then_inc(scat_transposed, 1)
                gather(0)
                pe.wait_ge(scat_ready, 4 * p + 4)
                with pe.Fori(0, NE) as e:
                    pe.wait_ge(lo_split, per(xb + 2, e, 9))
                    for i, (kind, k, half) in enumerate(EXP):
                        s = (ub + i) % SLOTS
                        pe.wait_ge(lo_ready, per(ub + i + 1, e, NU))
                        if kind in "gu":
                            if half == 0:
                                pe.wait_ge(act_ready, per(cb + k - 1, e, EXP_CHUNKS))
                            out = bank((0 if kind == "g" else 2) + k % 2)
                            for c in range(4):
                                o = c * COLS
                                ins = product(out, hT_hi[:, 4 * half + c, 0:P], hT_lo[:, 4 * half + c, 0:P],
                                              w_hi[:, s, o:o + COLS], w_lo[:, s, o:o + COLS],
                                              half == 0 and c == 0, half == 1 and c == 3)
                        else:
                            if half == 0:
                                pe.wait_ge(lo_split, per(xb + 2 + (k if k < 6 else 8) + 1, e, 9))
                                if k == 0:
                                    pe.wait_ge(y_evac, per(2 + 2 * NE * p, e, 2))
                            for j in range(2):
                                for n in range(2):
                                    o = j * D + n * COLS
                                    ins = product(bank(4 + n), aT_hi[:, 2 * half + j, 0:P],
                                                  aT_lo[:, 2 * half + j, 0:P], w_hi[:, s, o:o + COLS],
                                                  w_lo[:, s, o:o + COLS], k == 0 and half == 0 and j == 0,
                                                  k == EXP_CHUNKS - 1 and half == 1 and j == 1)
                        ins.then_inc(used, 1)

                        def transpose_act(kk):
                            pe.wait_ge(act_ready, per(cb + kk + 1, e, EXP_CHUNKS))
                            for j in range(4):
                                ins = pe.transpose(bank(6)[:, j * P:(j + 1) * P],
                                                   act[:, kk % 2, j * P:(j + 1) * P], ident[:, :])
                            ins.then_inc(transposed, 1)

                        if kind == "g" and half and k == 0:
                            pe.wait_ge(y_evac, per(2 + 2 * NE * p, e, 2))
                            scatter(0)
                            scatter(1)
                        if kind == "u" and half == 0 and k == 0:
                            pe.wait_ge(scat_added, per(sb_ + 2, e, 4))
                            scatter(2)
                            scatter(3)
                        if kind == "u" and half == 0 and k >= 1:
                            if k == 1:
                                pe.wait_ge(scat_added, per(sb_ + 4, e, 4))
                            transpose_act(k - 1)
                        if kind == "u" and half and k == EXP_CHUNKS - 1:
                            pe.wait_ge(lo_split, per(xb + 2 + 6, e, 9))
                            gather(e + 1)
                        if kind == "d" and half and k == EXP_CHUNKS - 2:
                            pe.wait_ge(lo_split, per(xb + 2 + 8, e, 9))
                            transpose_act(EXP_CHUNKS - 1)
                pe.wait_ge(y_evac, 2 + 2 * NE * (p + 1))
                scatter(0)
                scatter(1)
                pe.wait_ge(scat_added, sb_ + 4 * NE + 2)
                scatter(2)
                scatter(3)

            expert_pass(0)
            pe.wait_ge(flag_ready, 1)
            most = pe.value_load(nmax_i[0:1, 0:1], min_val=0, max_val=SEQ)
            with pe.If(most > P):
                expert_pass(1)


_INS = ["x", "l0_norm_attn", "l0_w_in", "l0_a_q_norm", "l0_a_k_norm", "l0_a_lambda", "l0_a_subln",
        "l0_b_q_norm", "l0_b_k_norm", "l0_b_sinks", "l0_w_out", "l0_norm_ffn", "l0_ffn_w_gu",
        "l0_ffn_w_down", "l1_norm_attn", "l1_c_w_in", "l1_c_q_lora_norm", "l1_c_kv_lora_norm",
        "l1_c_w_uq", "l1_c_w_ukv", "l1_c_q_norm", "l1_c_k_norm", "l1_c_w_out", "l1_norm_ffn",
        "l1_router", "l1_exp_w_gu", "l1_exp_w_down"]


def shape_tables():
    def rope(dim):
        inv = (np.float32(10000.0) ** (-np.arange(0, dim, 2, dtype=np.float32) / np.float32(dim))).astype(np.float32)
        ang = np.arange(SEQ, dtype=np.float32)[:, None] * inv[None, :]
        return [np.cos(ang), np.sin(ang)]

    q = (P + np.arange(P))[:, None] // CHUNK
    k = np.arange(SEQ)[None, :] // CHUNK
    causal = k <= q
    window = causal & (k >= q - 2)
    masks = np.where(np.stack([causal, window], 1), 0.0, NEG)
    i = np.arange(P)
    e = np.arange(NE)
    tie = np.broadcast_to((e[None, :] < e[:, None]).reshape(1, NE * NE), (P, NE * NE))
    return {
        "ident": np.eye(P), "masks": masks, "rope": np.concatenate(rope(HD) + rope(C_ROPE), 1),
        "triu": i[:, None] < i[None, :], "iota": np.broadcast_to(i[None, :], (P, P)), "tie": tie,
    }


def kernel(**inputs):
    import concourse.bacc as _bacc
    from concourse.bass_utils import run_bass_kernel_spmd as _run

    nc = _bacc.Bacc("TRN2", target_bir_lowering=False, num_devices=1)
    arrays, A = {}, {}
    data = {name: np.ascontiguousarray(inputs[name]) for name in _INS}
    data.update({n: np.ascontiguousarray(t, dtype=np.float32) for n, t in shape_tables().items()})
    for name, arr in data.items():
        arrays[f"in_{name}"] = arr
        A[name] = nc.dram_tensor(f"in_{name}", arr.shape, mybir.dt.from_np(arr.dtype), kind="ExternalInput").ap()
    A["out"] = nc.dram_tensor("out_0", data["x"].shape, mybir.dt.float32, kind="ExternalOutput").ap()
    build(nc, A)
    r = _run(nc, [arrays], core_ids=[0])
    return r.results[0]["out_0"]
```

```python
import math
import numpy as np
import concourse.bass as bass
from concourse import mybir
from contextlib import ExitStack

P = 128
D = 1024
SEQ = 256
NT = SEQ // P
KC = D // P
CHUNK = 64
EPS = 1e-6
A_HEADS, A_MAPS, HD, A_VD = 4, 2, 64, 128
B_HEADS, B_KV = 8, 2
ZA_Q, ZA_K, ZA_V = 0, 512, 1024
ZB_Q, ZB_K, ZB_V = 1536, 2048, 2176
L0_IN = 2304
N_QK_A, N_QK_B = 16, 10
C_HEADS, C_NOPE, C_ROPE, C_V = 16, 64, 32, 64
C_QK = C_NOPE + C_ROPE
C_QR, C_KVR = 256, 128
C_IN = C_QR + C_KVR + C_ROPE
FF = 2816
NE, FFE = 8, 3584
LAM_INIT = 0.8 - 0.6 * math.exp(-0.3 * 0)
NEG = -1.0e30
COLS = 512

RING = 6
SLOTS = 3
PIECE = 2048


def dense_pieces(name, rows, cols, order=None):
    out = []
    for n in order or range(-(-cols // COLS)):
        w = min(COLS, cols - n * COLS)
        step = min(rows // P, PIECE // w)
        for c in range(0, rows // P, step):
            out.append((name, n, c, c + step, w))
    return out


IN0_ORDER = (3, 4, 0, 1, 2)
IN0_HEADS = (8, 2, 8, 8)
IN0 = dense_pieces("w_in0", D, L0_IN, IN0_ORDER)
OUT0 = dense_pieces("w_out0", D, D)
IN1 = dense_pieces("w_in1", D, C_IN)
UQ = dense_pieces("w_uq", C_QR, C_HEADS * C_QK)
UKV = [("w_ukv", 0, 0, 1, 2048)]
OUT1 = dense_pieces("w_out1", D, D)


def ffn_pieces():
    out, chunks = [], [(k, min(COLS, FF - k * COLS)) for k in range(-(-FF // COLS))]

    def down(k, w):
        return [("ffn_d", k, j, min(j + 2, w // P), w) for j in range(0, w // P, 2)]

    for k, w in chunks:
        step = PIECE // w
        for kind in ("ffn_g", "ffn_u"):
            out += [(kind, k, c, c + step, w) for c in range(0, KC, step)]
        if k:
            out += down(k - 1, COLS)
    return out + down(*chunks[-1])


FFN = ffn_pieces()
FFN_CHUNKS = -(-FF // COLS)
EXP_CHUNKS = FFE // COLS
EXP = []
for _k in range(EXP_CHUNKS):
    EXP += [("g", _k, 0), ("g", _k, 1), ("u", _k, 0), ("u", _k, 1)]
    if _k:
        EXP += [("d", _k - 1, 0), ("d", _k - 1, 1)]
EXP += [("d", EXP_CHUNKS - 1, 0), ("d", EXP_CHUNKS - 1, 1)]
NU = len(EXP)
assert NU % RING == 0 and NU % SLOTS == 0

STREAM = IN0 + OUT0 + FFN + IN1 + UKV + UQ + OUT1
U0 = len(STREAM)


def first(pieces):
    return STREAM.index(pieces[0])


def piece_floats(piece):
    return PIECE if piece[0].startswith("ffn_d") else (piece[3] - piece[2]) * piece[4]


X_NORM0, X_MERGE0, X_NORM1 = 0, 4, 8
X_FFN = 12
X_NORM2 = X_FFN + NT * FFN_CHUNKS
X_LORA = X_NORM2 + 4
X_MERGE1 = X_LORA + 2
X_NORM3 = X_MERGE1 + 4
X_EXP = X_NORM3 + 4
X_PER_EXPERT = EXP_CHUNKS + 2
X_PER_PASS = NE * X_PER_EXPERT

R_NORM0, R_QK0, R_SUB, R_NORM1, R_NORM2, R_LORA, R_KQ1, R_NORM3 = 0, 2, 10, 12, 14, 16, 18, 22
R_COLS = [1, 1] + [n for n in IN0_HEADS for _ in range(NT)] + [4, 4, 1, 1, 1, 1, 2, 2, 16, 16, 16, 16, 1, 1]
R_OFF = [sum(R_COLS[:i]) for i in range(len(R_COLS))]


def build(nc, A):
    f32, f32r, i32 = mybir.dt.float32, mybir.dt.float32r, mybir.dt.int32
    ALU, ACT, AX = mybir.AluOpType, mybir.ActivationFunctionType, mybir.AxisListType
    ctx = ExitStack()
    with ctx:
        def sb(name, shape, dt=f32):
            return ctx.enter_context(nc.sbuf_tensor(name, shape, dt))

        def sem(name):
            return ctx.enter_context(nc.semaphore(name))

        ring = sb("ring", [P, RING, PIECE])
        w_hi = sb("w_hi", [P, SLOTS, PIECE], f32r)
        w_lo = sb("w_lo", [P, SLOTS, PIECE], f32r)
        x = sb("x_res", [P, NT, D])
        h = sb("h_tok", [P, NT, D])
        hT_hi = sb("hT_hi", [P, KC, SEQ], f32r)
        hT_lo = sb("hT_lo", [P, KC, SEQ], f32r)
        aT_hi = sb("aT_hi", [P, 4, SEQ], f32r)
        aT_lo = sb("aT_lo", [P, 4, SEQ], f32r)
        ident = sb("ident", [P, P])
        stat = sb("stat", [P, sum(R_COLS)])
        neg_half = sb("neg_half", [P, 26])
        subln = sb("subln", [P, A_VD])
        sinks = sb("sinks", [P, 2, B_HEADS])
        small = sb("small", [P, 3, 16])
        q_scale = sb("q_scale", [P, 2, NT, 16])
        k_rope = sb("k_rope", [P, NT, 68])
        rinv = sb("rinv", [P, NT, 16])
        lam = sb("lam", [P, 8])
        rw_hi = sb("rw_hi", [P, KC, NE], f32r)
        rw_lo = sb("rw_lo", [P, KC, NE], f32r)
        rw = sb("rw", [P, KC, NE])
        nmax = sb("nmax", [1, 1])
        nmax_i = sb("nmax_i", [1, 1], i32)
        rope = sb("rope", [P, NT, 96])
        tabs = sb("tabs", [P, 1024])
        arena1 = sb("arena1", [P, 5120])
        arena2 = sb("arena2", [P, 8192])
        arena3 = sb("arena3", [P, 2560])

        z = arena1[:, 0:NT * L0_IN].rearrange("p (t n) -> p t n", t=NT)
        k1 = arena1[:, 0:NT * 1536].rearrange("p (t n) -> p t n", t=NT)
        v1 = arena1[:, 3072:3072 + NT * 1024].rearrange("p (t n) -> p t n", t=NT)
        triu = arena1[:, 0:P]
        iota = arena1[:, P:2 * P]
        ones = arena1[:, 2 * P:3 * P]
        tie = arena1[:, 384:448].rearrange("p (e f) -> p e f", e=NE)
        rt = arena1[:, 512:1024]
        onehot_gated = arena1[:, 1024:3072].rearrange("p (t e s) -> p t e s", t=NT, e=NE)
        qkT0 = arena2[:, 0:13 * SEQ].rearrange("p (s n) -> p s n", s=13)
        qT1 = arena2[:, 0:16 * SEQ].rearrange("p (s n) -> p s n", s=16)
        kT1 = arena2[:, 16 * SEQ:32 * SEQ].rearrange("p (s n) -> p s n", s=16)
        z1 = arena2[:, 16 * SEQ:16 * SEQ + NT * C_IN].rearrange("p (t n) -> p t n", t=NT)
        zg = arena2[:, 16 * SEQ + 1024:16 * SEQ + 1024 + NT * 384].rearrange("p (t n) -> p t n", t=NT)
        onehot = arena2[:, 0:2304].rearrange("p (t e s) -> p t e s", t=NT, e=NE + 1)
        scatT_all = arena2[:, 2304:4352].rearrange("p (e n) -> p e n", e=NE)
        scatT = arena2[:, 4352:4608]
        y_exp = arena2[:, 4608:5632]
        gain = arena3[:, 0:D]
        raw_gains = arena3[:, D:D + 4 * HD].rearrange("p (k d) -> p k d", k=4)
        raw_lam = arena3[:, D + 256:D + 512].rearrange("p (k d) -> p k d", k=4)
        raw_gains1 = arena3[:, D + 512:D + 704].rearrange("p (k d) -> p k d", k=2)
        lora_gain = arena3[:, D:D + C_QR + C_KVR]
        sq = arena3[:, 0:1024]
        sq1 = arena3[:, 0:2560]
        probs = arena3[:, 0:1536].rearrange("p (b m n) -> p b m n", b=3, m=2)
        probsT = arena3[:, 1536:2560].rearrange("p (b m n) -> p b m n", b=2, m=4)
        sig = arena3[:, 0:1024].rearrange("p (b n) -> p b n", b=2)
        act = arena3[:, 1024:2048].rearrange("p (b n) -> p b n", b=2)
        hflat = h[:, :, :].rearrange("p t n -> p (t n)")
        rope_tmp = hflat[:, 1536:2048]
        q1 = hflat[:, 0:1536]
        tab0 = tabs[:, 0:1024].rearrange("p (k t c d) -> p k t c d", k=4, t=NT, c=2)
        tab1 = tabs[:, 0:512].rearrange("p (k t c) -> p k t c", k=2, t=NT)

        PS = ctx.enter_context(nc.psum_tensor("PS", [P, 8, COLS], f32))

        def bank(b):
            return PS[:, b, :]

        x_loaded = sem("x_loaded")
        gain0_loaded = sem("gain0_loaded")
        gain_loaded = sem("gain_loaded")
        ident_loaded = sem("ident_loaded")
        early_loaded = sem("early_loaded")
        tab_in = sem("tab_in")
        lora_loaded = sem("lora_loaded")
        moe_loaded = sem("moe_loaded")
        ring_loaded = [sem(f"ring_loaded{i}") for i in range(RING)]
        hi_ready = sem("hi_ready")
        lo_ready = sem("lo_ready")
        used = sem("pieces_used")
        neg_half_set = sem("neg_half_set")
        tabs_built = sem("tabs_built")
        pool_step = sem("pool_step")
        dve_step = sem("dve_step")
        act_step = sem("act_step")
        squared = sem("squared")
        ms_ready = sem("ms_ready")
        rstd_ready = sem("rstd_ready")
        normed = sem("normed")
        x_updated = sem("x_updated")
        transposed = sem("transposed")
        hi_split = sem("hi_split")
        lo_split = sem("lo_split")
        evacuated = sem("evacuated")
        qk_normed = sem("qk_normed")
        qk_transposed = sem("qk_transposed")
        qkT_ready = sem("qkT_ready")
        scored = sem("scored")
        first_tile = sem("first_tile_done")
        qkT_copied = sem("qkT_copied")
        kv_ready = sem("kv_ready")
        q_evac = sem("q_evac")
        q_squared = sem("q_squared")
        bias_ready = sem("bias_ready")
        exp_done = sem("exp_done")
        probs_ready = sem("probs_ready")
        probs_transposed = sem("probs_transposed")
        probsT_ready = sem("probsT_ready")
        pv_done = sem("pv_done")
        merged = sem("merged")
        lam_exp = sem("lam_exp")
        sig_ready = sem("sig_ready")
        act_ready = sem("act_ready")
        silu_step = sem("silu_step")
        routed = sem("routed")
        router_step = sem("router_step")
        logit_exp = sem("logit_exp")
        ranks_ready = sem("ranks_ready")
        counted = sem("counted")
        onehot_ready = sem("onehot_ready")
        scat_transposed = sem("scat_transposed")
        scat_ready = sem("scat_ready")
        y_evac = sem("y_evac")
        scattered = sem("scattered")
        scat_added = sem("scat_added")
        flag_ready = sem("flag_ready")
        stored = sem("stored")

        block = ctx.enter_context(nc.Block())

        def rows(name, c0, c1, n0, w):
            return A[name][c0 * P:c1 * P, n0:n0 + w].rearrange("(c p) n -> p c n", p=P)

        def piece_source(piece):
            name, n, c0, c1, w = piece
            if name == "ffn_g":
                return rows("l0_ffn_w_gu", c0, c1, n * COLS, w)
            if name == "ffn_u":
                return rows("l0_ffn_w_gu", c0, c1, FF + n * COLS, w)
            if name == "ffn_d":
                return rows("l0_ffn_w_down", n * 4 + c0, n * 4 + c1, 0, D)
            src = {"w_in0": "l0_w_in", "w_out0": "l0_w_out", "w_in1": "l1_c_w_in", "w_uq": "l1_c_w_uq",
                   "w_ukv": "l1_c_w_ukv", "w_out1": "l1_c_w_out"}[name]
            return rows(src, c0, c1, n * COLS, w)

        def expert_source(e, piece):
            kind, k, half = piece
            if kind == "d":
                r = k * COLS + half * 2 * P
                return A["l1_exp_w_down"][e, r:r + 2 * P, :].rearrange("(c p) n -> p c n", p=P)
            n0 = k * COLS + (FFE if kind == "u" else 0)
            return A["l1_exp_w_gu"][e, half * 4 * P:(half + 1) * 4 * P, n0:n0 + COLS]\
                .rearrange("(c p) n -> p c n", p=P)

        def per(value, e, step):
            return value if e is None else e * step + value

        def bc(ap, axis, n):
            shape = list(ap.shape)
            return ap.unsqueeze(axis).broadcast_to(shape[:axis] + [n] + shape[axis:])

        @block.sync
        def _(sp):
            def load(u, src, n, e=None):
                if u >= RING:
                    sp.wait_ge(lo_ready, per(u - RING + 1, e, NU))
                c = src.shape[1]
                dst = ring[:, u % RING, 0:n].rearrange("p (c n) -> p c n", c=c)
                sp.dma_start(dst, src).then_inc(ring_loaded[u % RING], 16)

            for t in range(NT):
                sp.dma_start(x[:, t, :], A["x"][0, t * P:(t + 1) * P, :]).then_inc(x_loaded, 16)
            sp.dma_start(gain, A["l0_norm_attn"].partition_broadcast(P)).then_inc(gain0_loaded, 16)
            sp.dma_start(ident[:, :], A["ident"]).then_inc(ident_loaded, 16)
            for u, piece in enumerate(STREAM):
                load(u, piece_source(piece), piece_floats(piece))

            def expert_pass(base):
                with sp.Fori(0, NE) as e:
                    for k in range(NU):
                        load(base + k, expert_source(e, EXP[k]), PIECE, e)

            expert_pass(U0)
            sp.wait_ge(flag_ready, 1)
            most = sp.value_load(nmax_i[0:1, 0:1], min_val=0, max_val=SEQ)
            with sp.If(most > P):
                expert_pass(U0 + NE * NU)

        @block.gpsimd
        def _(pool):
            steps = [0]

            def link(ins):
                steps[0] += 1
                ins.then_inc(pool_step, 1)
                pool.wait_ge(pool_step, steps[0])

            pool.memset(neg_half[:, :], -0.5).then_inc(neg_half_set, 1)
            pool.wait_ge(neg_half_set, 1)

            def rsqrt(r):
                pool.wait_ge(ms_ready, r + 1)
                s = stat[:, R_OFF[r]:R_OFF[r] + R_COLS[r]]
                pool.tensor_tensor(s, s, neg_half[:, 0:R_COLS[r]], ALU.pow).then_inc(rstd_ready, 1)

            def build_tables(tab, g, half, lead, cos0, sin0):
                for k in range(g.shape[1]):
                    for t in range(NT):
                        cos, sin = rope[:, t, cos0:cos0 + half], rope[:, t, sin0:sin0 + half]
                        c, s = tab(k, t)
                        if lead:
                            link(pool.tensor_tensor(c[:, 0:lead], g[:, 0, 0:lead], g[:, 1, 0:lead], ALU.mult))
                        link(pool.tensor_tensor(c[:, lead:lead + half], g[:, k, lead:lead + half], cos, ALU.mult))
                        link(pool.tensor_tensor(c[:, lead + half:lead + 2 * half],
                                                g[:, k, lead + half:lead + 2 * half], cos, ALU.mult))
                        link(pool.tensor_tensor(s[:, half:2 * half], g[:, k, lead:lead + half], sin, ALU.mult))
                        link(pool.tensor_tensor(s[:, 0:half], g[:, k, lead + half:lead + 2 * half], sin, ALU.mult))
                        link(pool.tensor_scalar(s[:, 0:half], s[:, 0:half], -1.0, None, ALU.mult))

            rsqrt(R_NORM0)
            rsqrt(R_NORM0 + 1)
            pool.wait_ge(tab_in, 16 * 7)
            build_tables(lambda k, t: (tab0[:, k, t, 0, :], tab0[:, k, t, 1, :]), raw_gains, 32, 0, 0, 32)
            pool.engine_nop().then_inc(tabs_built, 1)
            for r in range(R_QK0, R_NORM1):
                rsqrt(r)
            pool.wait_ge(merged, 2)
            pool.dma_start(gain, A["l0_norm_ffn"].partition_broadcast(P)).then_inc(gain_loaded, 16)
            rsqrt(R_NORM1)
            rsqrt(R_NORM1 + 1)
            pool.wait_ge(transposed, X_NORM2)
            pool.dma_start(gain, A["l1_norm_attn"].partition_broadcast(P)).then_inc(gain_loaded, 16)
            pool.dma_start(lora_gain[:, 0:C_QR], A["l1_c_q_lora_norm"].partition_broadcast(P))\
                .then_inc(lora_loaded, 16)
            pool.dma_start(lora_gain[:, C_QR:C_QR + C_KVR], A["l1_c_kv_lora_norm"].partition_broadcast(P))\
                .then_inc(lora_loaded, 16)
            pool.dma_start(raw_gains1[:, 0, :], A["l1_c_q_norm"].partition_broadcast(P)).then_inc(lora_loaded, 16)
            pool.dma_start(raw_gains1[:, 1, :], A["l1_c_k_norm"].partition_broadcast(P)).then_inc(lora_loaded, 16)
            pool.wait_ge(lora_loaded, 64)
            build_tables(lambda k, t: (tab1[:, k, t, 0:96], tab1[:, k, t, 96:128]), raw_gains1, 16, 64, 64, 80)
            pool.engine_nop().then_inc(tabs_built, 1)
            for r in range(R_NORM2, R_NORM3):
                rsqrt(r)
            pool.wait_ge(merged, 4)
            pool.dma_start(gain, A["l1_norm_ffn"].partition_broadcast(P)).then_inc(gain_loaded, 16)
            pool.dma_start(triu, A["triu"]).then_inc(moe_loaded, 16)
            pool.dma_start(iota, A["iota"]).then_inc(moe_loaded, 16)
            pool.dma_start(arena1[:, 384:448], A["tie"]).then_inc(moe_loaded, 16)
            pool.memset(ones, 1.0).then_inc(pool_step, 1)
            steps[0] += 1
            pool.wait_ge(pool_step, steps[0])
            pool.memset(y_exp, 0.0).then_inc(y_evac, 1)
            pool.memset(scatT, 0.0).then_inc(y_evac, 1)
            pool.memset(onehot[:, :, NE, :], 0.0).then_inc(pool_step, 1)
            steps[0] += 1
            pool.wait_ge(pool_step, steps[0])
            pool.engine_nop().then_inc(tabs_built, 1)
            rsqrt(R_NORM3)
            rsqrt(R_NORM3 + 1)

        @block.scalar
        def _(a):
            steps = [0]

            def link(ins):
                steps[0] += 1
                ins.then_inc(act_step, 1)
                a.wait_ge(act_step, steps[0])

            for k, name in enumerate(("l0_a_q_norm", "l0_a_k_norm", "l0_b_q_norm", "l0_b_k_norm")):
                a.dma_start(raw_gains[:, k, :], A[name].partition_broadcast(P)).then_inc(tab_in, 16)
            for t in range(NT):
                a.dma_start(rope[:, t, :], A["rope"][t * P:(t + 1) * P, :]).then_inc(tab_in, 16)
            a.dma_start(arena3[:, D + 256:D + 512],
                        A["l0_a_lambda"].rearrange("k d -> (k d)").partition_broadcast(P)).then_inc(tab_in, 16)
            a.dma_start(subln[:, :], A["l0_a_subln"].partition_broadcast(P)).then_inc(early_loaded, 16)
            a.dma_start(sinks[:, 0, :], A["l0_b_sinks"].partition_broadcast(P)).then_inc(early_loaded, 16)
            a.dma_start(rw[:, :, :], A["l1_router"].rearrange("(c p) e -> p c e", p=P)).then_inc(early_loaded, 16)

            def split_piece(u, n, e=None):
                a.wait_ge(ring_loaded[u % RING], per(16 * (u // RING + 1), e, 16 * NU // RING))
                if u >= SLOTS:
                    a.wait_ge(used, per(u - SLOTS + 1, e, NU))
                a.activation(w_hi[:, u % SLOTS, 0:n], ring[:, u % RING, 0:n], ACT.Copy).then_inc(hi_ready, 1)

            def split_ahead(u):
                v = u + SLOTS
                split_piece(v, piece_floats(STREAM[v]) if v < U0 else PIECE)

            def after(u, task=None):
                if task is not None:
                    a.wait_ge(used, u + 1)
                    task()
                split_ahead(u)

            def split_bank(i, dst, src, e=None, step=0):
                a.wait_ge(transposed, per(i + 1, e, step))
                a.activation(dst, src, ACT.Copy).then_inc(hi_split, 1)

            def split_h(i):
                for t in range(NT):
                    for g in range(2):
                        split_bank(i + 2 * t + g, hT_hi[:, 4 * g:4 * g + 4, t * P:(t + 1) * P],
                                   bank(2 * t + g).rearrange("p (c n) -> p c n", c=4))

            def norm_squares(r, sums):
                for t in range(NT):
                    if sums is None:
                        a.wait_ge(x_loaded, 32)
                    else:
                        a.wait_ge(x_updated, sums[t])
                    a.activation(h[:, t, :], x[:, t, :], ACT.Square,
                                 accum_out=stat[:, R_OFF[r + t]:R_OFF[r + t] + 1]).then_inc(squared, 1)

            def attention(s0, kind):
                def exps(i):
                    t, p = i // 8, i % 8
                    nk = P * (t + 1)
                    a.wait_ge(bias_ready, s0 + i + 1)
                    if i >= 3:
                        a.wait_ge(probs_transposed, s0 + i - 2)
                    sm = small[:, i % 3, :]
                    for m in range(2):
                        ins = a.activation(probs[:, i % 3, m, 0:nk], bank(6 * (i % 2) + m)[:, 0:nk], ACT.Exp,
                                           bias=sm[:, 2 + m:3 + m], scale=q_scale[:, 0, t, 2 * p + m:2 * p + m + 1],
                                           accum_out=sm[:, 4 + m:5 + m])
                    if kind == "AB" and p >= 4:
                        ins = a.activation(sm[:, 8:10], sm[:, 6:8], ACT.Exp)
                    ins.then_inc(exp_done, 1)

                exps(0)
                exps(1)
                for j in range(16):
                    if j + 2 < 16:
                        exps(j + 2)
                    t, p = j // 8, j % 8
                    nb = (t + 1) * (1 if kind == "AB" and p < 4 else 2)
                    a.wait_ge(probs_transposed, s0 + j + 1)
                    if j >= 2:
                        a.wait_ge(pv_done, s0 + j - 1)
                    a.activation(probsT[:, j % 2, 0:nb, :],
                                 bank(2 + j % 2)[:, 0:nb * P].rearrange("p (b n) -> p b n", b=nb),
                                 ACT.Copy).then_inc(probsT_ready, 1)
                    if kind == "AB" and p == 5:
                        a.wait_ge(pv_done, s0 + 8 * t + 4)
                        for hd in range(A_HEADS):
                            c = R_OFF[R_SUB + t] + hd
                            ins = a.activation(h[:, t, hd * P:(hd + 1) * P], bank(4)[:, hd * P:(hd + 1) * P],
                                               ACT.Square, accum_out=stat[:, c:c + 1])
                        ins.then_inc(squared, 1)

            norm_squares(R_NORM0, None)
            split_piece(0, piece_floats(STREAM[0]))
            split_h(X_NORM0)
            for u in range(1, SLOTS):
                split_piece(u, piece_floats(STREAM[u]))

            def evacuate(dst, b):
                a.activation(dst, b, ACT.Copy).then_inc(evacuated, 1)

            for i, (_, n, c0, c1, w) in enumerate(IN0):
                def task():
                    q = IN0_ORDER.index(n)
                    for t in range(NT):
                        dst, src = z[:, t, n * COLS:n * COLS + w], bank((4 + 2 * q + t) % 8)[:, 0:w]
                        if n * COLS == ZB_Q:
                            dst = dst.rearrange("p (s m d) -> p m s d", s=4, m=2)
                            src = src.rearrange("p (m s d) -> p m s d", s=4, m=2)
                        evacuate(dst, src)
                    if q == 0:
                        a.wait_ge(normed, 2)
                    if q < 4:
                        a.wait_ge(evacuated, 2 * q + 2)
                        for t in range(NT):
                            if q:
                                a.wait_ge(ms_ready, R_QK0 + 2 * (q - 1) + t + 1)
                            m = IN0_HEADS[q] * HD
                            a.activation(sq[:, t * COLS:t * COLS + m], z[:, t, n * COLS:n * COLS + m], ACT.Square)\
                                .then_inc(squared, 1)
                after(i, task if c1 == KC else None)
            a.wait_ge(lam_exp, 1)
            a.activation(lam[:, 2:4], lam[:, 0:2], ACT.Exp).then_inc(lam_exp, 1)

            def copy_heads(i, dst, b):
                a.wait_ge(qk_transposed, i + 1)
                a.activation(dst, b, ACT.Copy).then_inc(qkT_ready, 1)

            for t in range(NT):
                for g in range(0, 4, 2):
                    copy_heads(4 * t + g, qkT0[:, 4 * g:4 * g + 4, t * P:(t + 1) * P],
                               bank(4 * t + g).rearrange("p (s n) -> p s n", s=4))
            a.wait_ge(tabs_built, 1)
            attention(0, "AB")
            split_h(X_MERGE0)
            for i in range(len(OUT0) - 1):
                after(first(OUT0) + i)
            norm_squares(R_NORM1, (3, 4))
            split_h(X_NORM1)
            f0 = first(FFN)
            split_ahead(f0 - 1)
            for i, (name, k, c0, c1, w) in enumerate(FFN):
                def exps():
                    for t in range(NT):
                        if k >= 1:
                            a.wait_ge(act_ready, 2 * k)
                        a.activation(sig[:, t, 0:w], bank(t)[:, 0:w], ACT.Tanh, scale=0.5).then_inc(sig_ready, 1)

                def split_act(kk, ww):
                    for t in range(NT):
                        nj = ww // P
                        split_bank(X_FFN + 2 * kk + t, aT_hi[:, 0:nj, t * P:(t + 1) * P],
                                   bank(t)[:, 0:ww].rearrange("p (j n) -> p j n", j=nj))

                def acts():
                    if name == "ffn_u":
                        split_act(0, w)
                    else:
                        split_act(k + 1, min(COLS, FF - (k + 1) * COLS))
                if name == "ffn_g" and c1 == KC:
                    after(f0 + i, exps)
                elif (name == "ffn_u" and c1 == KC and k == 0) or \
                        (name == "ffn_d" and c1 * P == w and k + 1 < FFN_CHUNKS):
                    after(f0 + i, acts)
                elif i + 1 < len(FFN):
                    after(f0 + i)
            norm_squares(R_NORM2, (6, 8))
            split_h(X_NORM2)
            split_ahead(f0 + len(FFN) - 1)
            for i, (_, n, c0, c1, w) in enumerate(IN1):
                def task():
                    for t in range(NT):
                        evacuate(z1[:, t, :], bank(4 + t)[:, 0:w])
                        a.wait_ge(evacuated, 11 + t)
                        o = R_OFF[R_LORA + t]
                        for c0_, c1_, acc in ((0, C_QR, stat[:, o:o + 1]), (C_QR, C_QR + C_KVR, stat[:, o + 1:o + 2]),
                                              (C_QR + C_KVR, C_IN, k_rope[:, t, 64:65])):
                            ins = a.activation(hflat[:, C_IN * t + c0_:C_IN * t + c1_], z1[:, t, c0_:c1_],
                                               ACT.Square, accum_out=acc)
                        ins.then_inc(squared, 1)
                after(first(IN1) + i, task if c1 == KC else None)
            for t in range(NT):
                split_bank(X_LORA + t, hT_hi[:, 0:3, t * P:(t + 1) * P],
                           bank(t)[:, 0:3 * P].rearrange("p (c n) -> p c n", c=3))

            a.wait_ge(used, first(UKV) + 1)
            a.wait_ge(rstd_ready, R_LORA + NT)
            for t in range(NT):
                kb = k1[:, t, :].rearrange("p (s n) -> p s n", n=C_QK)
                vb = v1[:, t, :].rearrange("p (s n) -> p s n", n=C_V)
                o = R_OFF[R_LORA + t]
                for n in range(4):
                    src = bank(4 * t + n).rearrange("p (s n) -> p s n", n=C_NOPE + C_V)
                    a.activation(kb[:, 4 * n:4 * n + 4, 0:C_NOPE], src[:, :, 0:C_NOPE], ACT.Copy,
                                 scale=stat[:, o + 1:o + 2]).then_inc(kv_ready, 1)
                a.wait_ge(kv_ready, 8 * t + 4)
                if t:
                    a.wait_ge(ms_ready, R_KQ1 + 1)
                else:
                    a.wait_ge(normed, 8)
                    a.wait_ge(tabs_built, 2)
                a.activation(sq1[:, 0:1024].rearrange("p (s n) -> p s n", n=C_NOPE), kb[:, :, 0:C_NOPE], ACT.Square)\
                    .then_inc(squared, 1)
                for n in range(4):
                    src = bank(4 * t + n).rearrange("p (s n) -> p s n", n=C_NOPE + C_V)
                    a.activation(vb[:, 4 * n:4 * n + 4, :], src[:, :, C_NOPE:], ACT.Copy,
                                 scale=stat[:, o + 1:o + 2]).then_inc(kv_ready, 1)
                if t == 0:
                    split_ahead(first(UKV))

            def copy_heads1(q, t):
                dst = (kT1, qT1)[q]
                for g in range(0, 4, 2):
                    copy_heads(8 + 8 * t + 4 * q + g, dst[0:C_QK, 4 * g:4 * g + 4, t * P:(t + 1) * P],
                               bank(4 * t + g)[0:C_QK, :].rearrange("p (s n) -> p s n", s=4))

            for t in range(NT):
                a.wait_ge(used, first(UQ) + len(UQ))
                if t:
                    a.wait_ge(qk_transposed, 16)
                o = R_OFF[R_LORA + t]
                for n in range(3):
                    a.activation(q1[:, n * COLS:(n + 1) * COLS], bank(4 * t + n), ACT.Copy,
                                 scale=stat[:, o:o + 1]).then_inc(q_evac, 1)
                a.wait_ge(q_evac, 3 * t + 3)
                if t:
                    a.wait_ge(ms_ready, R_KQ1 + 2)
                a.activation(sq1[:, 1024:2560], q1, ACT.Square).then_inc(q_squared, 1)
                copy_heads1(0, t)
                copy_heads1(1, t)
            for i in range(len(UQ)):
                split_ahead(first(UQ) + i)
            attention(16, "C")
            split_h(X_MERGE1)
            for i in range(len(OUT1) - 1):
                after(first(OUT1) + i)
            norm_squares(R_NORM3, (11, 12))
            split_h(X_NORM3)
            split_ahead(U0 - 1)
            a.wait_ge(router_step, 1)
            a.activation(rt[:, 0:16], rt[:, 16:32], ACT.Exp).then_inc(logit_exp, 1)

            def expert_pass(p):
                ub = U0 + p * NE * NU
                xb = X_EXP + p * X_PER_PASS
                cb = NT * FFN_CHUNKS + p * NE * EXP_CHUNKS

                def gather_split(i, e=None):
                    for g in range(2):
                        split_bank(i + g, hT_hi[:, 4 * g:4 * g + 4, 0:P],
                                   bank(6 + g).rearrange("p (c n) -> p c n", c=4), e, X_PER_EXPERT)

                if p:
                    for i in range(SLOTS):
                        split_piece(ub + i, PIECE)
                gather_split(xb)
                for b in range(4):
                    a.wait_ge(scat_transposed, 4 * p + b + 1)
                    a.activation(scatT_all[:, 2 * b:2 * b + 2, :],
                                 bank(b).rearrange("p (e n) -> p e n", e=2), ACT.Copy).then_inc(scat_ready, 1)

                def expert(e, last):
                    for i, (kind, k, half) in enumerate(EXP):
                        a.wait_ge(used, per(ub + i + 1, e, NU))
                        if kind == "g" and half:
                            a.wait_ge(act_ready, per(cb + k - 1, e, EXP_CHUNKS))
                            a.activation(sig[:, k % 2, :], bank(k % 2), ACT.Tanh, scale=0.5).then_inc(sig_ready, 1)
                        if kind == "u" and half == 0 and k >= 1:
                            split_bank(xb + 2 + k - 1, aT_hi[:, :, 0:P],
                                       bank(6).rearrange("p (j n) -> p j n", j=4), e, X_PER_EXPERT)
                        if kind == "u" and half and k == 0:
                            a.wait_ge(scattered, per(4 + p * 4 * (NE + 1), e, 4))
                            if p == 0:
                                a.wait_ge(scat_ready, 4)
                            a.activation(scatT, scatT_all[:, bass.ds(e, 1), :].rearrange("p e n -> p (e n)"),
                                         ACT.Copy)
                        if kind == "u" and half and k == EXP_CHUNKS - 1 and not last:
                            gather_split(xb + 2 + 6, e)
                        if kind == "d" and half and k == EXP_CHUNKS - 2:
                            split_bank(xb + 2 + (6 if last else 8), aT_hi[:, :, 0:P],
                                       bank(6).rearrange("p (j n) -> p j n", j=4), e, X_PER_EXPERT)
                        if kind == "d" and half and k == EXP_CHUNKS - 1:
                            for n in range(2):
                                a.activation(y_exp[:, n * COLS:(n + 1) * COLS], bank(4 + n), ACT.Copy)\
                                    .then_inc(y_evac, 1)
                        if i + SLOTS < NU or not last:
                            split_piece(ub + i + SLOTS, PIECE, e)

                with a.Fori(0, NE - 1) as e:
                    expert(e, False)
                expert(NE - 1, True)

            expert_pass(0)
            a.wait_ge(flag_ready, 1)
            most = a.value_load(nmax_i[0:1, 0:1], min_val=0, max_val=SEQ)
            with a.If(most > P):
                expert_pass(1)
            a.wait_ge(stored, 1)
            for t in range(NT):
                a.dma_start(A["out"][0, t * P:(t + 1) * P, :], x[:, t, :]).then_inc(stored, 16)
            a.wait_ge(stored, 33)

        @block.vector
        def _(v):
            steps = [0]

            def link(ins):
                steps[0] += 1
                ins.then_inc(dve_step, 1)
                v.wait_ge(dve_step, steps[0])

            def split_piece(u, n, e=None):
                v.wait_ge(hi_ready, per(u + 1, e, NU))
                v.tensor_tensor(w_lo[:, u % SLOTS, 0:n], ring[:, u % RING, 0:n],
                                w_hi[:, u % SLOTS, 0:n].bitcast(f32), ALU.subtract).then_inc(lo_ready, 1)

            def split_ahead(u):
                w = u + SLOTS
                split_piece(w, piece_floats(STREAM[w]) if w < U0 else PIECE)

            def after(u, task=None):
                if task is not None:
                    v.wait_ge(used, u + 1)
                    task()
                split_ahead(u)

            def split_bank(i, dst, hi, src, e=None, step=0):
                v.wait_ge(hi_split, per(i + 1, e, step))
                v.tensor_tensor(dst, src, hi.bitcast(f32), ALU.subtract).then_inc(lo_split, 1)

            def split_h(i):
                for t in range(NT):
                    for g in range(2):
                        s = (slice(None), slice(4 * g, 4 * g + 4), slice(t * P, (t + 1) * P))
                        split_bank(i + 2 * t + g, hT_lo[s], hT_hi[s],
                                   bank(2 * t + g).rearrange("p (c n) -> p c n", c=4))

            def mean_square(r, inv, cols=None):
                s = stat[:, R_OFF[r]:R_OFF[r] + R_COLS[r]]
                v.tensor_scalar(s, s, inv, EPS, ALU.mult, ALU.add).then_inc(ms_ready, 1)

            def norm(i, r, nsq):
                for t in range(NT):
                    v.wait_ge(squared, nsq + t + 1)
                    mean_square(r + t, 1.0 / D)
                for t in range(NT):
                    v.wait_ge(rstd_ready, r + t + 1)
                    if t == 0 and i == 0:
                        v.wait_ge(gain0_loaded, 16)
                    elif t == 0:
                        v.wait_ge(gain_loaded, 16 * i)
                    v.scalar_tensor_tensor(out=h[:, t, :], in0=x[:, t, :], scalar=stat[:, R_OFF[r + t]:R_OFF[r + t] + 1],
                                           in1=gain, op0=ALU.mult, op1=ALU.mult).then_inc(normed, 1)

            def rotate(zt, nh, width, lead, half, cos, sin):
                s = zt.rearrange("p (s n) -> p s n", n=width)
                tmp = rope_tmp[:, 0:nh * 2 * half].rearrange("p (s n) -> p s n", n=2 * half)
                link(v.tensor_tensor(tmp[:, :, 0:half], s[:, :, lead + half:lead + 2 * half],
                                     bc(sin[:, 0:half], 1, nh), ALU.mult))
                link(v.tensor_tensor(tmp[:, :, half:2 * half], s[:, :, lead:lead + half],
                                     bc(sin[:, half:2 * half], 1, nh), ALU.mult))
                link(v.tensor_tensor(s, s, bc(cos, 1, nh), ALU.mult))
                return v.tensor_tensor(s[:, :, lead:], s[:, :, lead:], tmp, ALU.add)

            def query_scale(t, c0, r, nh, scale):
                s = stat[:, R_OFF[r]:R_OFF[r] + nh]
                link(v.tensor_scalar(q_scale[:, 0, t, c0:c0 + nh], s, scale, None, ALU.mult))
                link(v.tensor_scalar(q_scale[:, 1, t, c0:c0 + nh], s, -scale, None, ALU.mult))

            def attention(s0, kind):
                def front(i):
                    t, p = i // 8, i % 8
                    nk = P * (t + 1)
                    with_sink = kind == "AB" and p >= 4
                    sm = small[:, i % 3, :]
                    b = 6 * (i % 2)
                    v.wait_ge(scored, s0 + i + 1)
                    ins = v.memset(PS[0:CHUNK, b:b + 2, nk - CHUNK:nk], NEG)
                    if with_sink and t == 1:
                        link(ins)
                        ins = v.memset(PS[CHUNK:P, b:b + 2, 0:CHUNK], NEG)
                    link(ins)
                    link(v.tensor_reduce(sm[:, 0:2], PS[:, b:b + 2, 0:nk], AX.X, ALU.max))
                    if with_sink:
                        link(v.tensor_tensor(sm[:, 10:12], sm[:, 0:2], q_scale[:, 1, t, 2 * p:2 * p + 2], ALU.mult))
                        link(v.tensor_tensor(sm[:, 2:4], sm[:, 10:12], sinks[:, 1, p - 4:p + 1:4], ALU.min))
                        v.tensor_tensor(sm[:, 6:8], sm[:, 2:4], sinks[:, 0, p - 4:p + 1:4], ALU.add)\
                            .then_inc(bias_ready, 1)
                    else:
                        v.tensor_tensor(sm[:, 2:4], sm[:, 0:2], q_scale[:, 1, t, 2 * p:2 * p + 2], ALU.mult)\
                            .then_inc(bias_ready, 1)

                def back(i):
                    t, p = i // 8, i % 8
                    nk = P * (t + 1)
                    sm = small[:, i % 3, :]
                    v.wait_ge(exp_done, s0 + i + 1)
                    if kind == "C":
                        v.reciprocal(rinv[:, t, 2 * p:2 * p + 2], sm[:, 4:6]).then_inc(probs_ready, 1)
                    elif p >= 4:
                        link(v.tensor_tensor(sm[:, 4:6], sm[:, 4:6], sm[:, 8:10], ALU.add))
                        v.reciprocal(rinv[:, t, p - 4:p + 1:4], sm[:, 4:6]).then_inc(probs_ready, 1)
                    else:
                        link(v.reciprocal(sm[:, 12:14], sm[:, 4:6]))
                        link(v.tensor_scalar(sm[:, 14:15], sm[:, 13:14], lam[:, 4:5], None, ALU.mult))
                        p0, p1 = probs[:, i % 3, 0, 0:nk], probs[:, i % 3, 1, 0:nk]
                        link(v.tensor_scalar(p0, p0, sm[:, 12:13], None, ALU.mult))
                        v.scalar_tensor_tensor(out=p0, in0=p1, scalar=sm[:, 14:15], in1=p0,
                                               op0=ALU.mult, op1=ALU.add).then_inc(probs_ready, 1)

                def final(t):
                    v.wait_ge(pv_done, s0 + 8 * t + 8)
                    if kind == "AB":
                        o = R_OFF[R_SUB + t]
                        v.wait_ge(squared, 11 + t)
                        mean_square(R_SUB + t, 1.0 / A_VD)
                        link(v.tensor_tensor(h[:, t, 512:1024].rearrange("p (s n) -> p s n", n=HD),
                                             bank(5).rearrange("p (s n) -> p s n", n=HD),
                                             bc(rinv[:, t, 0:8], 2, HD), ALU.mult))
                        v.wait_ge(rstd_ready, R_SUB + t + 1)
                        ha = h[:, t, 0:512].rearrange("p (s n) -> p s n", n=A_VD)
                        link(v.tensor_tensor(ha, bank(4).rearrange("p (s n) -> p s n", n=A_VD),
                                             bc(stat[:, o:o + 4], 2, A_VD), ALU.mult))
                        v.tensor_tensor(ha, ha, bc(subln[:, :], 1, A_HEADS), ALU.mult).then_inc(merged, 1)
                    else:
                        for n in range(2):
                            ins = v.tensor_tensor(h[:, t, n * 512:(n + 1) * 512].rearrange("p (s n) -> p s n", n=C_V),
                                                  bank(4 + n).rearrange("p (s n) -> p s n", n=C_V),
                                                  bc(rinv[:, t, 8 * n:8 * n + 8], 2, C_V), ALU.mult)
                        ins.then_inc(merged, 1)

                front(0)
                front(1)
                for j in range(16):
                    if j + 2 < 16:
                        front(j + 2)
                    back(j)
                    if j == 8:
                        final(0)
                final(1)

            def add_residual(t, n, b):
                xs = x[:, t, n * COLS:(n + 1) * COLS]
                v.tensor_tensor(xs, xs, b, ALU.add).then_inc(x_updated, 1)

            def residual(pieces, k):
                u0, last = first(pieces), pieces[-1][1]
                for i, (_, n, c0, c1, w) in enumerate(pieces):
                    def task():
                        for t in range(NT):
                            add_residual(t, n, bank(4 + 2 * n + t))
                    if i + 1 < len(pieces):
                        after(u0 + i, task if c1 == KC else None)
                v.wait_ge(first_tile, k)
                add_residual(0, last, bank(4 + 2 * last))
                v.wait_ge(used, u0 + len(pieces))
                add_residual(1, last, bank(5 + 2 * last))

            norm(0, R_NORM0, 0)
            split_piece(0, piece_floats(STREAM[0]))
            split_h(X_NORM0)
            for u in range(1, SLOTS):
                split_piece(u, piece_floats(STREAM[u]))
            v.wait_ge(early_loaded, 48)
            link(v.tensor_copy(rw_hi[:, :, :], rw[:, :, :]))
            link(v.tensor_tensor(rw_lo[:, :, :], rw[:, :, :], rw_hi[:, :, :].bitcast(f32), ALU.subtract))
            link(v.tensor_scalar(subln[:, :], subln[:, :], 1.0 - LAM_INIT, None, ALU.mult))
            link(v.tensor_scalar(sinks[:, 1, :], sinks[:, 0, :], -1.0, None, ALU.mult))
            v.wait_ge(tab_in, 16 * 7)
            v.wait_ge(tabs_built, 1)
            tables = (2, 3, 0, 1)

            def chunk_heads(t, q):
                n = IN0_ORDER[q]
                return z[:, t, n * COLS:n * COLS + IN0_HEADS[q] * HD]

            for i, (_, n, c0, c1, w) in enumerate(IN0):
                def task():
                    q = IN0_ORDER.index(n)
                    if q == 4:
                        return
                    nh = IN0_HEADS[q]
                    for t in range(NT):
                        r = R_QK0 + 2 * q + t
                        v.wait_ge(squared, 3 + 2 * q + t)
                        link(v.tensor_reduce(stat[:, R_OFF[r]:R_OFF[r] + nh],
                                             sq[:, t * COLS:t * COLS + nh * HD].rearrange("p (s n) -> p s n", n=HD),
                                             AX.X, ALU.add))
                        mean_square(r, 1.0 / HD)
                    for t in range(NT):
                        r = R_QK0 + 2 * q + t
                        link(rotate(chunk_heads(t, q), nh, HD, 0, HD // 2, tab0[:, tables[q], t, 0, :],
                                    tab0[:, tables[q], t, 1, :]))
                        v.wait_ge(rstd_ready, r + 1)
                        if q in (1, 3):
                            s = chunk_heads(t, q).rearrange("p (s n) -> p s n", n=HD)
                            v.tensor_tensor(s, s, bc(stat[:, R_OFF[r]:R_OFF[r] + nh], 2, HD), ALU.mult)\
                                .then_inc(qk_normed, 1)
                        else:
                            query_scale(t, 8 if q == 0 else 0, r, nh, HD ** -0.5)
                after(i, task if c1 == KC else None)
            link(v.tensor_tensor(rope_tmp[:, 0:HD], raw_lam[:, 0, :], raw_lam[:, 1, :], ALU.mult))
            link(v.tensor_tensor(rope_tmp[:, HD:2 * HD], raw_lam[:, 2, :], raw_lam[:, 3, :], ALU.mult))
            v.tensor_reduce(lam[:, 0:2], rope_tmp[:, 0:2 * HD].rearrange("p (k n) -> p k n", k=2), AX.X, ALU.add)\
                .then_inc(lam_exp, 1)

            def copy_heads(i, dst, b):
                v.wait_ge(qk_transposed, i + 1)
                v.tensor_copy(dst, b).then_inc(qkT_copied, 1)

            for t in range(NT):
                for g in range(1, 4, 2):
                    m = min(4, 13 - 4 * g)
                    copy_heads(4 * t + g, qkT0[:, 4 * g:4 * g + m, t * P:(t + 1) * P],
                               bank(4 * t + g)[:, 0:m * P].rearrange("p (s n) -> p s n", s=m))
            v.wait_ge(lam_exp, 2)
            link(v.tensor_tensor(lam[:, 4:5], lam[:, 3:4], lam[:, 2:3], ALU.subtract))
            link(v.tensor_scalar(lam[:, 4:5], lam[:, 4:5], -LAM_INIT, None, ALU.add))
            attention(0, "AB")
            split_h(X_MERGE0)
            residual(OUT0, 1)
            norm(1, R_NORM1, 12)
            split_h(X_NORM1)
            f0 = first(FFN)
            split_ahead(f0 - 1)

            def silu(src_g, src_u, sg, ac, base):
                v.scalar_tensor_tensor(out=ac, in0=sg, scalar=1.0, in1=src_g, op0=ALU.add, op1=ALU.mult)\
                    .then_inc(silu_step, 1)
                v.wait_ge(silu_step, base + 1)
                v.scalar_tensor_tensor(out=ac, in0=ac, scalar=0.5, in1=src_u, op0=ALU.mult, op1=ALU.mult)\
                    .then_inc(act_ready, 1)

            for i, (name, k, c0, c1, w) in enumerate(FFN):
                def silus():
                    for t in range(NT):
                        v.wait_ge(sig_ready, 2 * k + t + 1)
                        silu(bank(t)[:, 0:w], bank(2 + t)[:, 0:w], sig[:, t, 0:w], act[:, t, 0:w],
                             2 * k + t)

                def split_act(kk, ww):
                    nj = ww // P
                    for t in range(NT):
                        s = (slice(None), slice(0, nj), slice(t * P, (t + 1) * P))
                        split_bank(X_FFN + 2 * kk + t, aT_lo[s], aT_hi[s],
                                   bank(t)[:, 0:ww].rearrange("p (j n) -> p j n", j=nj))

                def acts():
                    if name == "ffn_u":
                        silus()
                        split_act(0, w)
                    else:
                        split_act(k + 1, min(COLS, FF - (k + 1) * COLS))
                if name == "ffn_u" and c1 == KC and k:
                    after(f0 + i, silus)
                elif (name == "ffn_u" and c1 == KC) or \
                        (name == "ffn_d" and c1 * P == w and k + 1 < FFN_CHUNKS):
                    after(f0 + i, acts)
                elif i + 1 < len(FFN):
                    after(f0 + i)
            for t in range(NT):
                if t == 0:
                    v.wait_ge(first_tile, 2)
                else:
                    v.wait_ge(used, f0 + len(FFN))
                for n in range(2):
                    add_residual(t, n, bank(4 + 2 * t + n))
            norm(2, R_NORM2, 14)
            split_h(X_NORM2)
            split_ahead(f0 + len(FFN) - 1)
            for i in range(len(IN1)):
                after(first(IN1) + i)
            v.wait_ge(lora_loaded, 64)
            for t in range(NT):
                v.wait_ge(evacuated, 11 + t)
                v.tensor_tensor(zg[:, t, :], z1[:, t, 0:C_QR + C_KVR], lora_gain, ALU.mult).then_inc(normed, 1)
            for t in range(NT):
                o = R_OFF[R_LORA + t]
                v.wait_ge(squared, 17 + t)
                link(v.tensor_scalar(stat[:, o:o + 1], stat[:, o:o + 1], 1.0 / C_QR, EPS, ALU.mult, ALU.add))
                v.tensor_scalar(stat[:, o + 1:o + 2], stat[:, o + 1:o + 2], 1.0 / C_KVR, EPS, ALU.mult, ALU.add)\
                    .then_inc(ms_ready, 1)
            for t in range(NT):
                s = (slice(None), slice(0, 3), slice(t * P, (t + 1) * P))
                split_bank(X_LORA + t, hT_lo[s], hT_hi[s], bank(t)[:, 0:3 * P].rearrange("p (c n) -> p c n", c=3))
            v.wait_ge(tabs_built, 2)
            half = C_ROPE // 2
            for t in range(NT):
                kr, out, tmp = z1[:, t, C_QR + C_KVR:C_IN], k_rope[:, t, 0:32], k_rope[:, t, 32:64]
                cos, sin = tab1[:, 1, t, C_NOPE:C_QK], tab1[:, 1, t, 96:128]
                link(v.tensor_tensor(tmp[:, 0:half], kr[:, half:], sin[:, 0:half], ALU.mult))
                link(v.tensor_tensor(tmp[:, half:], kr[:, 0:half], sin[:, half:], ALU.mult))
                link(v.tensor_tensor(out, kr, cos, ALU.mult))
                link(v.tensor_tensor(out, out, tmp, ALU.add))
                link(v.tensor_scalar(k_rope[:, t, 64:65], k_rope[:, t, 64:65], C_QK * EPS, None, ALU.add))
            split_ahead(first(UKV))

            def key_heads(t):
                r = R_KQ1 + 2 * t
                s = stat[:, R_OFF[r]:R_OFF[r] + C_HEADS]
                kb = k1[:, t, :].rearrange("p (s n) -> p s n", n=C_QK)
                v.wait_ge(squared, 19 + t)
                link(v.tensor_reduce(s, sq1[:, 0:1024].rearrange("p (s n) -> p s n", n=C_NOPE), AX.X, ALU.add))
                v.tensor_scalar(s, s, k_rope[:, t, 64:65], 1.0 / C_QK, ALU.add, ALU.mult).then_inc(ms_ready, 1)
                v.wait_ge(rstd_ready, r + 1)
                v.tensor_tensor(kb[:, :, 0:C_NOPE], kb[:, :, 0:C_NOPE], bc(s, 2, C_NOPE), ALU.mult)
                v.tensor_tensor(kb[:, :, C_NOPE:], bc(k_rope[:, t, 0:C_ROPE], 1, C_HEADS), bc(s, 2, C_ROPE), ALU.mult)\
                    .then_inc(qk_normed, 1)

            def query_heads(t):
                r = R_KQ1 + 2 * t + 1
                v.wait_ge(q_squared, t + 1)
                link(v.tensor_reduce(stat[:, R_OFF[r]:R_OFF[r] + C_HEADS],
                                     sq1[:, 1024:2560].rearrange("p (s n) -> p s n", n=C_QK), AX.X, ALU.add))
                mean_square(r, 1.0 / C_QK)
                rotate(q1, C_HEADS, C_QK, C_NOPE, half, tab1[:, 0, t, 0:96], tab1[:, 0, t, 96:128])\
                    .then_inc(qk_normed, 1)
                v.wait_ge(rstd_ready, r + 1)
                query_scale(t, 0, r, C_HEADS, C_QK ** -0.5)

            for t in range(NT):
                key_heads(t)
                query_heads(t)
                for q in range(2):
                    for g in range(1, 4, 2):
                        copy_heads(8 + 8 * t + 4 * q + g, (kT1, qT1)[q][0:C_QK, 4 * g:4 * g + 4, t * P:(t + 1) * P],
                                   bank(4 * t + g)[0:C_QK, :].rearrange("p (s n) -> p s n", s=4))
            for i in range(len(UQ)):
                split_ahead(first(UQ) + i)
            attention(16, "C")
            split_h(X_MERGE1)
            residual(OUT1, 3)
            norm(3, R_NORM3, 20)
            split_h(X_NORM3)
            split_ahead(U0 - 1)
            L = rt[:, 32:48]
            Lt = L.rearrange("p (t e) -> p t e", t=NT)
            v.wait_ge(routed, 1)
            v.wait_ge(moe_loaded, 48)
            v.wait_ge(tabs_built, 3)
            link(v.tensor_copy(L, bank(4)[:, 0:NT * NE]))
            link(v.tensor_reduce(rt[:, 48:50], Lt, AX.X, ALU.max))
            v.tensor_tensor(rt[:, 16:32].rearrange("p (t e) -> p t e", t=NT), Lt, bc(rt[:, 48:50], 2, NE),
                            ALU.subtract).then_inc(router_step, 1)
            gt = rt[:, 64:192].rearrange("p (t e f) -> p t e f", t=NT, e=NE)
            eq = rt[:, 256:384].rearrange("p (t e f) -> p t e f", t=NT, e=NE)
            sel = rt[:, 192:208]
            gates = rt[:, 208:224]
            mine, others = bc(Lt, 3, NE), bc(Lt, 2, NE)
            link(v.tensor_tensor(gt, others, mine, ALU.is_gt))
            link(v.tensor_tensor(eq, others, mine, ALU.is_equal))
            link(v.tensor_tensor(eq, eq, bc(tie, 1, NT), ALU.mult))
            link(v.tensor_tensor(gt, gt, eq, ALU.add))
            link(v.tensor_reduce(sel.rearrange("p (t e) -> p t e", t=NT), gt, AX.X, ALU.add))
            v.tensor_scalar(sel, sel, 1.5, None, ALU.is_lt).then_inc(ranks_ready, 1)
            v.wait_ge(ranks_ready, 1)
            v.wait_ge(logit_exp, 1)
            gates3 = gates.rearrange("p (t e) -> p t e", t=NT)
            link(v.tensor_tensor(gates, rt[:, 0:16], sel, ALU.mult))
            link(v.tensor_reduce(rt[:, 52:54], gates3, AX.X, ALU.add))
            link(v.reciprocal(rt[:, 54:56], rt[:, 52:54]))
            link(v.tensor_tensor(gates3, gates3, bc(rt[:, 54:56], 2, NE), ALU.mult))
            slot = rt[:, 224:240]
            v.wait_ge(counted, 1)
            link(v.scalar_tensor_tensor(out=slot, in0=bank(6)[:, 0:16], scalar=1.0, in1=sel, op0=ALU.add, op1=ALU.mult))
            link(v.tensor_scalar(slot, slot, -1.0, None, ALU.add))
            link(v.tensor_reduce(nmax[0:1, :], bank(6)[0:1, 16:24], AX.X, ALU.max))
            v.tensor_copy(nmax_i[0:1, :], nmax[0:1, :]).then_inc(flag_ready, 1)

            def expert_pass(p):
                ub = U0 + p * NE * NU
                xb = X_EXP + p * X_PER_PASS
                cb = NT * FFN_CHUNKS + p * NE * EXP_CHUNKS
                sb_ = p * 4 * (NE + 1)

                def gather_split(i, e=None):
                    for g in range(2):
                        s = (slice(None), slice(4 * g, 4 * g + 4), slice(0, P))
                        split_bank(i + g, hT_lo[s], hT_hi[s], bank(6 + g).rearrange("p (c n) -> p c n", c=4), e, X_PER_EXPERT)

                def act_split(i, e):
                    s = (slice(None), slice(0, 4), slice(0, P))
                    split_bank(i, aT_lo[s], aT_hi[s], bank(6).rearrange("p (j n) -> p j n", j=4), e, X_PER_EXPERT)

                def add_scattered(i, e=None):
                    v.wait_ge(scattered, per(sb_ + i + 1, e, 4))
                    xs = x[:, i % 4 // 2, (i % 2) * COLS:(i % 2 + 1) * COLS]
                    v.tensor_tensor(xs, xs, bank(6 + i % 2), ALU.add).then_inc(scat_added, 1)

                if p:
                    v.tensor_scalar(slot, slot, -float(P), None, ALU.add).then_inc(router_step, 1)
                    v.wait_ge(router_step, 2)
                for t in range(NT):
                    v.tensor_tensor(onehot[:, t, 0:NE, :], bc(iota, 1, NE), bc(slot[:, 8 * t:8 * t + 8], 2, P),
                                    ALU.is_equal).then_inc(onehot_ready, 1)
                v.wait_ge(onehot_ready, 4 * p + 2)
                for t in range(NT):
                    v.tensor_tensor(onehot_gated[:, t, :, :], onehot[:, t, 0:NE, :],
                                    bc(gates[:, 8 * t:8 * t + 8], 2, P), ALU.mult).then_inc(onehot_ready, 1)
                if p:
                    for i in range(SLOTS):
                        split_piece(ub + i, PIECE)
                gather_split(xb)

                def expert(e, last):
                    for i, (kind, k, half) in enumerate(EXP):
                        v.wait_ge(used, per(ub + i + 1, e, NU))
                        if kind == "g" and half:
                            v.wait_ge(sig_ready, per(cb + k + 1, e, EXP_CHUNKS))
                            sg, ac = sig[:, k % 2, :], act[:, k % 2, :]
                            v.scalar_tensor_tensor(out=ac, in0=sg, scalar=1.0, in1=bank(k % 2), op0=ALU.add,
                                                   op1=ALU.mult).then_inc(silu_step, 1)
                            if k == 0:
                                for q in range(2):
                                    add_scattered(q, e)
                        if kind == "u" and half == 0 and k == 0:
                            for q in range(2, 4):
                                add_scattered(q, e)
                        if kind == "u" and half == 0 and k >= 1:
                            act_split(xb + 2 + k - 1, e)
                        if kind == "u" and half:
                            ac = act[:, k % 2, :]
                            v.wait_ge(silu_step, per(cb + k + 1, e, EXP_CHUNKS))
                            v.scalar_tensor_tensor(out=ac, in0=ac, scalar=0.5, in1=bank(2 + k % 2), op0=ALU.mult,
                                                   op1=ALU.mult).then_inc(act_ready, 1)
                            if k == EXP_CHUNKS - 1 and not last:
                                gather_split(xb + 2 + 6, e)
                        if kind == "d" and half and k == EXP_CHUNKS - 2:
                            act_split(xb + 2 + (6 if last else 8), e)
                        if i + SLOTS < NU or not last:
                            split_piece(ub + i + SLOTS, PIECE, e)

                with v.Fori(0, NE - 1) as e:
                    expert(e, False)
                expert(NE - 1, True)
                for q in range(4):
                    add_scattered(4 * NE + q)

            expert_pass(0)
            most = v.value_load(nmax_i[0:1, 0:1], min_val=0, max_val=SEQ)
            with v.If(most > P):
                expert_pass(1)
            v.engine_nop().then_inc(stored, 1)

        @block.tensor
        def _(pe):
            def product(out, xh, xl, wh, wl, start, stop):
                pe.matmul(out, xh, wh, start=start, stop=False)
                pe.matmul(out, xh, wl, start=False, stop=False)
                return pe.matmul(out, xl, wh, start=False, stop=stop)

            def transpose_h(i, waits):
                for t in range(NT):
                    waits(t)
                    for g in range(2):
                        for c in range(4):
                            cc = 4 * g + c
                            ins = pe.transpose(bank(2 * t + g)[:, c * P:(c + 1) * P], h[:, t, cc * P:(cc + 1) * P],
                                               ident[:, :])
                        ins.then_inc(transposed, 1)

            def normed_wait(n):
                return lambda t: pe.wait_ge(normed, n + t + 1)

            def piece_wait(u):
                pe.wait_ge(lo_ready, u + 1)

            def project(pieces, kc, bank_of, free=None, early_sum=False):
                u0 = first(pieces)
                for i, (_, n, c0, c1, w) in enumerate(pieces):
                    u = u0 + i
                    piece_wait(u)
                    s = u % SLOTS
                    for t in range(NT):
                        if free is not None and c0 == 0:
                            free(n, t)
                        for c in range(c0, c1):
                            o = (c - c0) * w
                            ins = product(bank_of(n, t)[:, 0:w], hT_hi[:, c, t * P:(t + 1) * P],
                                          hT_lo[:, c, t * P:(t + 1) * P], w_hi[:, s, o:o + w], w_lo[:, s, o:o + w],
                                          c == 0, c == kc - 1)
                        if early_sum and t == 0 and i == len(pieces) - 1:
                            ins.then_inc(first_tile, 1)
                    ins.then_inc(used, 1)

            def attention(s0, kind):
                def scores(i):
                    t, p = i // 8, i % 8
                    nk = P * (t + 1)
                    if i >= 2:
                        pe.wait_ge(exp_done, s0 + i - 1)
                    for m in range(2):
                        if kind == "AB":
                            r = slice(m * HD, (m + 1) * HD)
                            q = qkT0[r, p if p < 4 else 8 + p - 4, t * P:(t + 1) * P]
                            kk = qkT0[r, 4 + p if p < 4 else 12, 0:nk]
                        else:
                            q = qT1[0:C_QK, 2 * p + m, t * P:(t + 1) * P]
                            kk = kT1[0:C_QK, 2 * p + m, 0:nk]
                        ins = pe.matmul(bank(6 * (i % 2) + m)[:, 0:nk], q, kk, start=True, stop=True)
                    ins.then_inc(scored, 1)

                def transposes(i):
                    t, p = i // 8, i % 8
                    maps = 1 if kind == "AB" and p < 4 else 2
                    pe.wait_ge(probs_ready, s0 + i + 1)
                    if i >= 2:
                        pe.wait_ge(probsT_ready, s0 + i - 1)
                    for m in range(maps):
                        for b in range(t + 1):
                            j = m * (t + 1) + b
                            ins = pe.transpose(bank(2 + i % 2)[:, j * P:(j + 1) * P],
                                               probs[:, i % 3, m, b * P:(b + 1) * P], ident[:, :])
                    ins.then_inc(probs_transposed, 1)

                def values(i):
                    t, p = i // 8, i % 8
                    pe.wait_ge(probsT_ready, s0 + i + 1)
                    if i == 8:
                        pe.wait_ge(merged, s0 // 8 + 1)
                    maps = 1 if kind == "AB" and p < 4 else 2
                    for m in range(maps):
                        if kind == "AB" and p < 4:
                            out = bank(4)[:, p * P:(p + 1) * P]
                            col, w = ZA_V + p * A_VD, A_VD
                        elif kind == "AB":
                            hd = p - 4 + 4 * m
                            out = bank(5)[:, hd * HD:(hd + 1) * HD]
                            col, w = ZB_V + m * HD, HD
                        else:
                            hd = 2 * p + m
                            out = bank(4 + hd // 8)[:, (hd % 8) * C_V:(hd % 8 + 1) * C_V]
                            col, w = hd * C_V, C_V
                        for b in range(t + 1):
                            vv = (z if kind == "AB" else v1)[:, b, col:col + w]
                            ins = pe.matmul(out, probsT[:, i % 2, m * (t + 1) + b, :], vv,
                                            start=b == 0, stop=b == t)
                    ins.then_inc(pv_done, 1)

                scores(0)
                scores(1)
                for i in range(16):
                    if i + 2 < 16:
                        scores(i + 2)
                    transposes(i)
                    if i >= 1:
                        values(i - 1)
                values(15)

            pe.wait_ge(ident_loaded, 16)
            transpose_h(X_NORM0, normed_wait(0))

            def bank0(n, t):
                return bank((4 + 2 * IN0_ORDER.index(n) + t) % 8)

            def free0(n, t):
                k = 2 * IN0_ORDER.index(n) + t
                if k < NT:
                    pe.wait_ge(lo_split, X_NORM0 + 2 * t + 2)
                if k >= 8:
                    pe.wait_ge(evacuated, k - 7)
            project(IN0, KC, bank0, free0)
            pe.wait_ge(evacuated, 10)
            for t in range(NT):
                pe.wait_ge(qk_normed, 3 + t)
                for g in range(4):
                    for j in range(4 * g, min(4 * g + 4, 13)):
                        if j < 8:
                            src = z[:, t, j * P:(j + 1) * P]
                        else:
                            src = z[:, t, ZB_Q + (j - 8) * P:ZB_Q + (j - 7) * P]
                        ins = pe.transpose(bank(4 * t + g)[:, (j % 4) * P:(j % 4 + 1) * P], src, ident[:, :])
                    ins.then_inc(qk_transposed, 1)
            pe.wait_ge(qkT_ready, 4)
            pe.wait_ge(qkT_copied, 4)
            attention(0, "AB")
            transpose_h(X_MERGE0, lambda t: pe.wait_ge(merged, t + 1))

            def split_wait(i):
                def free(n, t):
                    if n == 0:
                        pe.wait_ge(lo_split, i + 2 * t + 2)
                return free
            project(OUT0, KC, lambda n, t: bank(4 + 2 * n + t), split_wait(X_MERGE0), early_sum=True)
            transpose_h(X_NORM1, normed_wait(2))
            pe.wait_ge(lo_split, X_NORM1 + 4)
            f0 = first(FFN)

            def transpose_act(k, w):
                for t in range(NT):
                    pe.wait_ge(act_ready, 2 * k + t + 1)
                    for j in range(w // P):
                        ins = pe.transpose(bank(t)[:, j * P:(j + 1) * P], act[:, t, j * P:(j + 1) * P], ident[:, :])
                    ins.then_inc(transposed, 1)

            for i, (name, k, c0, c1, w) in enumerate(FFN):
                u = f0 + i
                s = u % SLOTS
                piece_wait(u)
                for t in range(NT):
                    if name in ("ffn_g", "ffn_u"):
                        if name == "ffn_g" and c0 == 0 and k >= 1:
                            pe.wait_ge(lo_split, X_FFN + 2 * k + t - 1)
                        out = bank(t if name == "ffn_g" else 2 + t)[:, 0:w]
                        for c in range(c0, c1):
                            o = (c - c0) * w
                            ins = product(out, hT_hi[:, c, t * P:(t + 1) * P], hT_lo[:, c, t * P:(t + 1) * P],
                                          w_hi[:, s, o:o + w], w_lo[:, s, o:o + w], c == 0, c == KC - 1)
                    else:
                        if c0 == 0:
                            pe.wait_ge(lo_split, X_FFN + 2 * k + t + 1)
                        last = k == FFN_CHUNKS - 1
                        for j in range(c0, c1):
                            for n in range(2):
                                o = (j - c0) * D + n * COLS
                                ins = product(bank(4 + 2 * t + n), aT_hi[:, j, t * P:(t + 1) * P],
                                              aT_lo[:, j, t * P:(t + 1) * P], w_hi[:, s, o:o + COLS],
                                              w_lo[:, s, o:o + COLS], k == 0 and j == 0,
                                              last and j == w // P - 1)
                    if t == 0 and i == len(FFN) - 1:
                        ins.then_inc(first_tile, 1)
                ins.then_inc(used, 1)
                if name == "ffn_u" and c1 == KC and k == 0:
                    transpose_act(0, w)
                if name == "ffn_d" and c1 * P == w and k + 1 < FFN_CHUNKS:
                    transpose_act(k + 1, min(COLS, FF - (k + 1) * COLS))
            transpose_h(X_NORM2, normed_wait(4))
            project(IN1, KC, lambda n, t: bank(4 + t), split_wait(X_NORM2))
            for t in range(NT):
                pe.wait_ge(normed, 7 + t)
                for c in range(3):
                    ins = pe.transpose(bank(t)[:, c * P:(c + 1) * P], zg[:, t, c * P:(c + 1) * P], ident[:, :])
                ins.then_inc(transposed, 1)

            u = first(UKV)
            piece_wait(u)
            pe.wait_ge(lo_split, X_LORA + NT)
            pe.wait_ge(evacuated, 12)
            for t in range(NT):
                for n in range(4):
                    o = n * COLS
                    ins = product(bank(4 * t + n), hT_hi[:, 2, t * P:(t + 1) * P], hT_lo[:, 2, t * P:(t + 1) * P],
                                  w_hi[:, u % SLOTS, o:o + COLS], w_lo[:, u % SLOTS, o:o + COLS], True, True)
            ins.then_inc(used, 1)

            def free_uq(n, t):
                if n == 0:
                    pe.wait_ge(kv_ready, 8 * t + 8)
            project(UQ, C_QR // P, lambda n, t: bank(4 * t + n), free_uq)

            def transpose_heads1(t, src):
                for g in range(4):
                    for j in range(4):
                        hd = 4 * g + j
                        ins = pe.transpose(bank(4 * t + g)[0:C_QK, j * P:(j + 1) * P],
                                           src[:, hd * C_QK:(hd + 1) * C_QK], ident[:, :])
                    ins.then_inc(qk_transposed, 1)

            for t in range(NT):
                pe.wait_ge(qk_normed, 5 + 2 * t)
                pe.wait_ge(q_evac, 3 * t + 3)
                transpose_heads1(t, k1[:, t, :])
                pe.wait_ge(qk_normed, 6 + 2 * t)
                pe.wait_ge(qkT_ready, 6 + 4 * t)
                pe.wait_ge(qkT_copied, 6 + 4 * t)
                transpose_heads1(t, q1)
            pe.wait_ge(qkT_ready, 12)
            pe.wait_ge(qkT_copied, 12)
            attention(16, "C")
            transpose_h(X_MERGE1, lambda t: pe.wait_ge(merged, 3 + t))
            project(OUT1, KC, lambda n, t: bank(4 + 2 * n + t), split_wait(X_MERGE1), early_sum=True)
            transpose_h(X_NORM3, normed_wait(8))
            for t in range(NT):
                pe.wait_ge(lo_split, X_NORM3 + 2 * t + 2)
                for c in range(KC):
                    ins = product(bank(4)[:, NE * t:NE * (t + 1)], hT_hi[:, c, t * P:(t + 1) * P], hT_lo[:, c, t * P:(t + 1) * P],
                                  rw_hi[:, c, :], rw_lo[:, c, :], c == 0, c == KC - 1)
            ins.then_inc(routed, 1)
            pe.wait_ge(ranks_ready, 1)
            sel = rt[:, 192:208]
            pe.matmul(bank(6)[:, 0:8], triu, sel[:, 0:8], start=True, stop=True)
            pe.matmul(bank(6)[:, 8:16], ones, sel[:, 0:8], start=True, stop=False)
            pe.matmul(bank(6)[:, 8:16], triu, sel[:, 8:16], start=False, stop=True)
            pe.matmul(bank(6)[:, 16:24], ones, sel[:, 0:8], start=True, stop=False)
            pe.matmul(bank(6)[:, 16:24], ones, sel[:, 8:16], start=False, stop=True).then_inc(counted, 1)

            def expert_pass(p):
                ub = U0 + p * NE * NU
                xb = X_EXP + p * X_PER_PASS
                cb = NT * FFN_CHUNKS + p * NE * EXP_CHUNKS
                sb_ = p * 4 * (NE + 1)

                def gather(e):
                    for g in range(2):
                        for c in range(4):
                            for t in range(NT):
                                cc = 4 * g + c
                                if isinstance(e, int):
                                    oh = onehot[:, t, e, :]
                                else:
                                    oh = onehot[:, t, bass.ds(e, 1), :].rearrange("p e n -> p (e n)")
                                ins = pe.matmul(bank(6 + g)[:, c * P:(c + 1) * P], h[:, t, cc * P:(cc + 1) * P], oh,
                                                start=t == 0, stop=t == NT - 1)
                        ins.then_inc(transposed, 1)

                def scatter(q):
                    t, n = q // 2, q % 2
                    pe.matmul(bank(6 + n), scatT[:, t * P:(t + 1) * P], y_exp[:, n * COLS:(n + 1) * COLS],
                              start=True, stop=True).then_inc(scattered, 1)

                pe.wait_ge(onehot_ready, 4 * p + 2)
                if p:
                    pe.wait_ge(scat_added, 4 * (NE + 1))
                gather(0)
                pe.wait_ge(onehot_ready, 4 * p + 4)
                for b in range(4):
                    for j in range(4):
                        e, t = 2 * b + j // 2, j % 2
                        ins = pe.transpose(bank(b)[:, j * P:(j + 1) * P], onehot_gated[:, t, e, :], ident[:, :])
                    ins.then_inc(scat_transposed, 1)
                pe.wait_ge(scat_ready, 4 * p + 4)

                def expert(e, last):
                    pe.wait_ge(lo_split, per(xb + 2, e, X_PER_EXPERT))
                    for i, (kind, k, half) in enumerate(EXP):
                        s = (ub + i) % SLOTS
                        pe.wait_ge(lo_ready, per(ub + i + 1, e, NU))
                        if kind in "gu":
                            if half == 0:
                                pe.wait_ge(act_ready, per(cb + k - 1, e, EXP_CHUNKS))
                            out = bank((0 if kind == "g" else 2) + k % 2)
                            for c in range(4):
                                o = c * COLS
                                ins = product(out, hT_hi[:, 4 * half + c, 0:P], hT_lo[:, 4 * half + c, 0:P],
                                              w_hi[:, s, o:o + COLS], w_lo[:, s, o:o + COLS],
                                              half == 0 and c == 0, half == 1 and c == 3)
                        else:
                            if half == 0:
                                pe.wait_ge(lo_split, per(xb + 2 + (k if k < 6 or last else 8) + 1, e, X_PER_EXPERT))
                                if k == 0:
                                    pe.wait_ge(y_evac, per(2 + 2 * NE * p, e, 2))
                            for j in range(2):
                                for n in range(2):
                                    o = j * D + n * COLS
                                    ins = product(bank(4 + n), aT_hi[:, 2 * half + j, 0:P],
                                                  aT_lo[:, 2 * half + j, 0:P], w_hi[:, s, o:o + COLS],
                                                  w_lo[:, s, o:o + COLS], k == 0 and half == 0 and j == 0,
                                                  k == EXP_CHUNKS - 1 and half == 1 and j == 1)
                        ins.then_inc(used, 1)

                        def transpose_act(kk):
                            pe.wait_ge(act_ready, per(cb + kk + 1, e, EXP_CHUNKS))
                            for j in range(4):
                                ins = pe.transpose(bank(6)[:, j * P:(j + 1) * P],
                                                   act[:, kk % 2, j * P:(j + 1) * P], ident[:, :])
                            ins.then_inc(transposed, 1)

                        if kind == "g" and half and k == 0:
                            pe.wait_ge(y_evac, per(2 + 2 * NE * p, e, 2))
                            scatter(0)
                            scatter(1)
                        if kind == "u" and half == 0 and k == 0:
                            pe.wait_ge(scat_added, per(sb_ + 2, e, 4))
                            scatter(2)
                            scatter(3)
                        if kind == "u" and half == 0 and k >= 1:
                            if k == 1:
                                pe.wait_ge(scat_added, per(sb_ + 4, e, 4))
                            transpose_act(k - 1)
                        if kind == "u" and half and k == EXP_CHUNKS - 1 and not last:
                            pe.wait_ge(lo_split, per(xb + 2 + 6, e, X_PER_EXPERT))
                            gather(e + 1)
                        if kind == "d" and half and k == EXP_CHUNKS - 2:
                            pe.wait_ge(lo_split, per(xb + 2 + (6 if last else 8), e, X_PER_EXPERT))
                            transpose_act(EXP_CHUNKS - 1)

                with pe.Fori(0, NE - 1) as e:
                    expert(e, False)
                expert(NE - 1, True)
                pe.wait_ge(y_evac, 2 + 2 * NE * (p + 1))
                scatter(0)
                scatter(1)
                pe.wait_ge(scat_added, sb_ + 4 * NE + 2)
                scatter(2)
                scatter(3)

            expert_pass(0)
            pe.wait_ge(flag_ready, 1)
            most = pe.value_load(nmax_i[0:1, 0:1], min_val=0, max_val=SEQ)
            with pe.If(most > P):
                expert_pass(1)


_INS = ["x", "l0_norm_attn", "l0_w_in", "l0_a_q_norm", "l0_a_k_norm", "l0_a_lambda", "l0_a_subln",
        "l0_b_q_norm", "l0_b_k_norm", "l0_b_sinks", "l0_w_out", "l0_norm_ffn", "l0_ffn_w_gu",
        "l0_ffn_w_down", "l1_norm_attn", "l1_c_w_in", "l1_c_q_lora_norm", "l1_c_kv_lora_norm",
        "l1_c_w_uq", "l1_c_w_ukv", "l1_c_q_norm", "l1_c_k_norm", "l1_c_w_out", "l1_norm_ffn",
        "l1_router", "l1_exp_w_gu", "l1_exp_w_down"]


def shape_tables():
    def rope(dim):
        inv = (np.float32(10000.0) ** (-np.arange(0, dim, 2, dtype=np.float32) / np.float32(dim))).astype(np.float32)
        ang = np.arange(SEQ, dtype=np.float32)[:, None] * inv[None, :]
        return [np.cos(ang), np.sin(ang)]

    i = np.arange(P)
    e = np.arange(NE)
    tie = np.broadcast_to((e[None, :] < e[:, None]).reshape(1, NE * NE), (P, NE * NE))
    return {
        "ident": np.eye(P), "rope": np.concatenate(rope(HD) + rope(C_ROPE), 1),
        "triu": i[:, None] < i[None, :], "iota": np.broadcast_to(i[None, :], (P, P)), "tie": tie,
    }


def kernel(**inputs):
    import concourse.bacc as _bacc
    from concourse.bass_utils import run_bass_kernel_spmd as _run

    nc = _bacc.Bacc("TRN2", target_bir_lowering=False, num_devices=1)
    arrays, A = {}, {}
    data = {name: np.ascontiguousarray(inputs[name]) for name in _INS}
    data.update({n: np.ascontiguousarray(t, dtype=np.float32) for n, t in shape_tables().items()})
    for name, arr in data.items():
        arrays[f"in_{name}"] = arr
        A[name] = nc.dram_tensor(f"in_{name}", arr.shape, mybir.dt.from_np(arr.dtype), kind="ExternalInput").ap()
    A["out"] = nc.dram_tensor("out_0", data["x"].shape, mybir.dt.float32, kind="ExternalOutput").ap()
    build(nc, A)
    r = _run(nc, [arrays], core_ids=[0])
    return r.results[0]["out_0"]
```

```python
import math
import numpy as np
import concourse.bass as bass
from concourse import mybir
from contextlib import ExitStack

P = 128
D = 1024
SEQ = 256
NT = SEQ // P
KC = D // P
CHUNK = 64
EPS = 1e-6
A_HEADS, A_MAPS, HD, A_VD = 4, 2, 64, 128
B_HEADS, B_KV = 8, 2
ZA_Q, ZA_K, ZA_V = 0, 512, 1024
ZB_Q, ZB_K, ZB_V = 1536, 2048, 2176
L0_IN = 2304
N_QK_A, N_QK_B = 16, 10
C_HEADS, C_NOPE, C_ROPE, C_V = 16, 64, 32, 64
C_QK = C_NOPE + C_ROPE
C_QR, C_KVR = 256, 128
C_IN = C_QR + C_KVR + C_ROPE
FF = 2816
NE, FFE = 8, 3584
LAM_INIT = 0.8 - 0.6 * math.exp(-0.3 * 0)
NEG = -1.0e30
COLS = 512

RING = 6
SLOTS = 3
PIECE = 2048


def dense_pieces(name, rows, cols, order=None):
    out = []
    for n in order or range(-(-cols // COLS)):
        w = min(COLS, cols - n * COLS)
        step = min(rows // P, PIECE // w)
        for c in range(0, rows // P, step):
            out.append((name, n, c, c + step, w))
    return out


IN0_ORDER = (3, 4, 0, 1, 2)
LATE = SLOTS
IN0_HEADS = (8, 2, 8, 8)
IN0 = dense_pieces("w_in0", D, L0_IN, IN0_ORDER)
OUT0 = dense_pieces("w_out0", D, D)
IN1 = dense_pieces("w_in1", D, C_IN)
UQ = dense_pieces("w_uq", C_QR, C_HEADS * C_QK)
UKV = [("w_ukv", 0, 0, 1, 2048)]
OUT1 = dense_pieces("w_out1", D, D)


def ffn_pieces():
    out, chunks = [], [(k, min(COLS, FF - k * COLS)) for k in range(-(-FF // COLS))]

    def down(k, w):
        return [("ffn_d", k, j, min(j + 2, w // P), w) for j in range(0, w // P, 2)]

    for k, w in chunks:
        step = PIECE // w
        for kind in ("ffn_g", "ffn_u"):
            out += [(kind, k, c, c + step, w) for c in range(0, KC, step)]
        if k:
            out += down(k - 1, COLS)
    return out + down(*chunks[-1])


FFN = ffn_pieces()
FFN_CHUNKS = -(-FF // COLS)
EXP_CHUNKS = FFE // COLS
EXP = []
for _k in range(EXP_CHUNKS):
    EXP += [("g", _k, 0), ("g", _k, 1), ("u", _k, 0), ("u", _k, 1)]
    if _k:
        EXP += [("d", _k - 1, 0), ("d", _k - 1, 1)]
EXP += [("d", EXP_CHUNKS - 1, 0), ("d", EXP_CHUNKS - 1, 1)]
NU = len(EXP)
assert len(UQ) == SLOTS and NU % RING == 0 and NU % SLOTS == 0

STREAM = IN0 + OUT0 + FFN + IN1 + UKV + UQ + OUT1
FILL = (3, 1)
SCAT_BANKS = (1, 3, 4, 5)
HI_AHEAD, LO_AHEAD = 4, 5
U0 = len(STREAM)


def first(pieces):
    return STREAM.index(pieces[0])


def piece_floats(piece):
    return PIECE if piece[0].startswith("ffn_d") else (piece[3] - piece[2]) * piece[4]


X_NORM0, X_MERGE0, X_NORM1 = 0, 4, 8
X_FFN = 12
X_NORM2 = X_FFN + NT * FFN_CHUNKS
X_LORA = X_NORM2 + 4
X_MERGE1 = X_LORA + 2
X_NORM3 = X_MERGE1 + 4
X_EXP = X_NORM3 + 4
X_PER_EXPERT = EXP_CHUNKS + 2
X_PER_PASS = NE * X_PER_EXPERT

R_NORM0, R_QK0, R_SUB, R_NORM1, R_NORM2, R_LORA, R_KQ1, R_NORM3 = 0, 2, 10, 12, 14, 16, 18, 22
R_COLS = [1, 1] + [n for n in IN0_HEADS for _ in range(NT)] + [4, 4, 1, 1, 1, 1, 2, 2, 16, 16, 16, 16, 1, 1]
R_OFF = [sum(R_COLS[:i]) for i in range(len(R_COLS))]


def build(nc, A):
    f32, f32r, i32 = mybir.dt.float32, mybir.dt.float32r, mybir.dt.int32
    ALU, ACT, AX = mybir.AluOpType, mybir.ActivationFunctionType, mybir.AxisListType
    ctx = ExitStack()
    with ctx:
        def sb(name, shape, dt=f32):
            return ctx.enter_context(nc.sbuf_tensor(name, shape, dt))

        def sem(name):
            return ctx.enter_context(nc.semaphore(name))

        ring = sb("ring", [P, RING, PIECE])
        w_hi = sb("w_hi", [P, SLOTS, PIECE], f32r)
        w_lo = sb("w_lo", [P, SLOTS, PIECE], f32r)
        x = sb("x_res", [P, NT, D])
        h = sb("h_tok", [P, NT, D])
        hT_hi = sb("hT_hi", [P, KC, SEQ], f32r)
        hT_lo = sb("hT_lo", [P, KC, SEQ], f32r)
        aT_hi = sb("aT_hi", [P, 4, SEQ], f32r)
        aT_lo = sb("aT_lo", [P, 4, SEQ], f32r)
        ident = sb("ident", [P, P])
        stat = sb("stat", [P, sum(R_COLS)])
        neg_half = sb("neg_half", [P, 26])
        subln = sb("subln", [P, A_VD])
        sinks = sb("sinks", [P, 2, B_HEADS])
        small = sb("small", [P, 2, 32])
        q_scale = sb("q_scale", [P, 2, NT, 16])
        k_rope = sb("k_rope", [P, NT, 68])
        rinv = sb("rinv", [P, NT, 16])
        lam = sb("lam", [P, 8])
        rw_split = sb("rw_split", [P, KC, 2 * NE], f32r)
        rw = sb("rw", [P, KC, NE])
        nmax = sb("nmax", [1, 1])
        nmax_i = sb("nmax_i", [1, 1], i32)
        rope = sb("rope", [P, NT, 96])
        tabs = sb("tabs", [P, 1024])
        arena1 = sb("arena1", [P, 5120])
        arena2 = sb("arena2", [P, 8192])
        arena3 = sb("arena3", [P, 2560])

        z = arena1[:, 0:NT * L0_IN].rearrange("p (t n) -> p t n", t=NT)
        k1 = arena1[:, 0:NT * 1536].rearrange("p (t n) -> p t n", t=NT)
        v1 = arena1[:, 3072:3072 + NT * 1024].rearrange("p (t n) -> p t n", t=NT)
        triu = arena1[:, 0:P]
        iota = arena1[:, P:2 * P]
        ones = arena1[:, 2 * P:3 * P]
        tie = arena1[:, 384:448].rearrange("p (e f) -> p e f", e=NE)
        rt = arena1[:, 512:1024]
        onehot_gated = arena1[:, 1024:3072].rearrange("p (t e s) -> p t e s", t=NT, e=NE)
        qkT0 = arena2[:, 0:13 * SEQ].rearrange("p (s n) -> p s n", s=13)
        qT1 = arena2[:, 0:16 * SEQ].rearrange("p (s n) -> p s n", s=16)
        kT1 = arena2[:, 16 * SEQ:32 * SEQ].rearrange("p (s n) -> p s n", s=16)
        z1 = arena2[:, 16 * SEQ:16 * SEQ + NT * C_IN].rearrange("p (t n) -> p t n", t=NT)
        zg = arena2[:, 16 * SEQ + 1024:16 * SEQ + 1024 + NT * 384].rearrange("p (t n) -> p t n", t=NT)
        onehot = arena2[:, 0:2048].rearrange("p (t e s) -> p t e s", t=NT, e=NE)
        scatT_all = arena2[:, 2304:4352].rearrange("p (e n) -> p e n", e=NE)
        scatT = arena2[:, 4352:4608]
        y_exp = arena2[:, 4608:5632]
        gain = arena3[:, 0:D]
        raw_gains = arena3[:, D:D + 4 * HD].rearrange("p (k d) -> p k d", k=4)
        raw_lam = arena3[:, D + 256:D + 512].rearrange("p (k d) -> p k d", k=4)
        raw_gains1 = arena3[:, D + 512:D + 704].rearrange("p (k d) -> p k d", k=2)
        lora_gain = arena3[:, D:D + C_QR + C_KVR]
        sq = arena3[:, 0:1024]
        k_sq = arena3[:, 0:1024]
        q_sq = arena2[:, 2560:4096]
        probs = arena3[:, 0:2048].rearrange("p (b s m n) -> p b s m n", b=2, s=2, m=2)
        probsT = tabs[:, 0:1024].rearrange("p (b m n) -> p b m n", b=2, m=4)
        sig = arena3[:, 0:1024].rearrange("p (b n) -> p b n", b=2)
        act = arena3[:, 1024:2048].rearrange("p (b n) -> p b n", b=2)
        hflat = h[:, :, :].rearrange("p t n -> p (t n)")
        rope_tmp = hflat[:, 1536:2048]
        q1 = (hflat[:, 0:1536], arena3[:, 1024:2560])
        tab0 = tabs[:, 0:1024].rearrange("p (k t c d) -> p k t c d", k=4, t=NT, c=2)
        tab1 = tabs[:, 0:512].rearrange("p (k t c) -> p k t c", k=2, t=NT)

        PS = ctx.enter_context(nc.psum_tensor("PS", [P, 8, COLS], f32))

        def bank(b):
            return PS[:, b, :]

        x_loaded = [sem(f"x_loaded{t}") for t in range(NT)]
        gain0_loaded = sem("gain0_loaded")
        gain_loaded = sem("gain_loaded")
        ident_loaded = sem("ident_loaded")
        early_loaded = sem("early_loaded")
        tab_in = sem("tab_in")
        lora_loaded = sem("lora_loaded")
        moe_loaded = sem("moe_loaded")
        ring_loaded = [sem(f"ring_loaded{i}") for i in range(RING)]
        hi_ready = sem("hi_ready")
        lo_ready = sem("lo_ready")
        used = sem("pieces_used")
        neg_half_set = sem("neg_half_set")
        tabs_built = sem("tabs_built")
        pool_step = sem("pool_step")
        dve_step = sem("dve_step")
        act_step = sem("act_step")
        squared = sem("squared")
        ms_ready = sem("ms_ready")
        rstd_ready = sem("rstd_ready")
        normed = sem("normed")
        x_updated = sem("x_updated")
        transposed = sem("transposed")
        hi_split = sem("hi_split")
        lo_split = sem("lo_split")
        evacuated = sem("evacuated")
        qk_normed = sem("qk_normed")
        qk_transposed = sem("qk_transposed")
        qkT_ready = sem("qkT_ready")
        scored = sem("scored")
        first_tile = sem("first_tile_done")
        qkT_copied = sem("qkT_copied")
        k_ready = sem("keys_ready")
        v_ready = sem("last_values_ready")
        v_copied = sem("first_values_copied")
        key_rotated = sem("key_rotated")
        q_evac = sem("q_evac")
        q_squared = sem("q_squared")
        bias_ready = sem("bias_ready")
        exp_done = sem("exp_done")
        probs_ready = sem("probs_ready")
        probs_transposed = sem("probs_transposed")
        probsT_ready = sem("probsT_ready")
        pv_done = sem("pv_done")
        merged = sem("merged")
        lam_exp = sem("lam_exp")
        sig_ready = sem("sig_ready")
        act_ready = sem("act_ready")
        silu_step = sem("silu_step")
        routed = sem("routed")
        router_step = sem("router_step")
        logit_exp = sem("logit_exp")
        ranks_ready = sem("ranks_ready")
        counted = sem("counted")
        onehot_ready = sem("onehot_ready")
        scat_transposed = sem("scat_transposed")
        scat_ready = sem("scat_ready")
        y_evac = sem("y_evac")
        scattered = sem("scattered")
        scat_added = sem("scat_added")
        flag_ready = sem("flag_ready")
        stored = sem("stored")

        block = ctx.enter_context(nc.Block())

        def rows(name, c0, c1, n0, w):
            return A[name][c0 * P:c1 * P, n0:n0 + w].rearrange("(c p) n -> p c n", p=P)

        def piece_source(piece):
            name, n, c0, c1, w = piece
            if name == "ffn_g":
                return rows("l0_ffn_w_gu", c0, c1, n * COLS, w)
            if name == "ffn_u":
                return rows("l0_ffn_w_gu", c0, c1, FF + n * COLS, w)
            if name == "ffn_d":
                return rows("l0_ffn_w_down", n * 4 + c0, n * 4 + c1, 0, D)
            src = {"w_in0": "l0_w_in", "w_out0": "l0_w_out", "w_in1": "l1_c_w_in", "w_uq": "l1_c_w_uq",
                   "w_ukv": "l1_c_w_ukv", "w_out1": "l1_c_w_out"}[name]
            return rows(src, c0, c1, n * COLS, w)

        def expert_source(e, piece):
            kind, k, half = piece
            if kind == "d":
                r = k * COLS + half * 2 * P
                return A["l1_exp_w_down"][e, r:r + 2 * P, :].rearrange("(c p) n -> p c n", p=P)
            n0 = k * COLS + (FFE if kind == "u" else 0)
            return A["l1_exp_w_gu"][e, half * 4 * P:(half + 1) * 4 * P, n0:n0 + COLS]\
                .rearrange("(c p) n -> p c n", p=P)

        def per(value, e, step):
            return value if e is None else e * step + value

        def bc(ap, axis, n):
            shape = list(ap.shape)
            return ap.unsqueeze(axis).broadcast_to(shape[:axis] + [n] + shape[axis:])

        @block.sync
        def _(sp):
            def load(u, src, n, e=None):
                if u >= RING:
                    sp.wait_ge(lo_ready, per(u - RING + 1, e, NU))
                c = src.shape[1]
                dst = ring[:, u % RING, 0:n].rearrange("p (c n) -> p c n", c=c)
                sp.dma_start(dst, src).then_inc(ring_loaded[u % RING], 16)

            for t in range(NT):
                sp.dma_start(x[:, t, :], A["x"][0, t * P:(t + 1) * P, :]).then_inc(x_loaded[t], 16)
            sp.dma_start(gain, A["l0_norm_attn"].partition_broadcast(P)).then_inc(gain0_loaded, 16)
            sp.dma_start(ident[:, :], A["ident"]).then_inc(ident_loaded, 16)
            for u, piece in enumerate(STREAM):
                if u == SLOTS:
                    for k, name in enumerate(("l0_a_q_norm", "l0_a_k_norm", "l0_b_q_norm", "l0_b_k_norm")):
                        sp.dma_start(raw_gains[:, k, :], A[name].partition_broadcast(P)).then_inc(tab_in, 16)
                    for t in range(NT):
                        sp.dma_start(rope[:, t, :], A["rope"][t * P:(t + 1) * P, :]).then_inc(tab_in, 16)
                    sp.dma_start(arena3[:, D + 256:D + 512],
                                A["l0_a_lambda"].rearrange("k d -> (k d)").partition_broadcast(P)).then_inc(tab_in, 16)
                    sp.dma_start(subln[:, :], A["l0_a_subln"].partition_broadcast(P)).then_inc(early_loaded, 16)
                    sp.dma_start(sinks[:, 0, :], A["l0_b_sinks"].partition_broadcast(P)).then_inc(early_loaded, 16)
                    sp.dma_start(rw[:, :, :], A["l1_router"].rearrange("(c p) e -> p c e", p=P)).then_inc(early_loaded, 16)
                load(u, piece_source(piece), piece_floats(piece))

            def expert_pass(base):
                with sp.Fori(0, NE) as e:
                    for k in range(NU):
                        load(base + k, expert_source(e, EXP[k]), PIECE, e)

            def store(p):
                for q in range(4):
                    t, c = q // 2, slice((q % 2) * COLS, (q % 2 + 1) * COLS)
                    sp.wait_ge(scat_added, 4 * (NE + 1) * p + 4 * NE + q + 1)
                    sp.dma_start(A["out"][0, t * P:(t + 1) * P, c], x[:, t, c]).then_inc(stored, 16)
                sp.wait_ge(stored, 64 * (p + 1))

            expert_pass(U0)
            store(0)
            sp.wait_ge(flag_ready, 1)
            most = sp.value_load(nmax_i[0:1, 0:1], min_val=0, max_val=SEQ)
            with sp.If(most > P):
                expert_pass(U0 + NE * NU)
                store(1)

        @block.gpsimd
        def _(pool):
            steps = [0]

            def link(ins):
                steps[0] += 1
                ins.then_inc(pool_step, 1)
                pool.wait_ge(pool_step, steps[0])

            pool.memset(neg_half[:, :], -0.5).then_inc(neg_half_set, 1)
            pool.wait_ge(neg_half_set, 1)

            def rsqrt(r):
                pool.wait_ge(ms_ready, r + 1)
                s = stat[:, R_OFF[r]:R_OFF[r] + R_COLS[r]]
                pool.tensor_tensor(s, s, neg_half[:, 0:R_COLS[r]], ALU.pow).then_inc(rstd_ready, 1)

            def build_tables(tab, g, half, lead, cos0, sin0):
                for k in range(g.shape[1]):
                    for t in range(NT):
                        cos, sin = rope[:, t, cos0:cos0 + half], rope[:, t, sin0:sin0 + half]
                        c, s = tab(k, t)
                        if lead:
                            link(pool.tensor_tensor(c[:, 0:lead], g[:, 0, 0:lead], g[:, 1, 0:lead], ALU.mult))
                        link(pool.tensor_tensor(c[:, lead:lead + half], g[:, k, lead:lead + half], cos, ALU.mult))
                        link(pool.tensor_tensor(c[:, lead + half:lead + 2 * half],
                                                g[:, k, lead + half:lead + 2 * half], cos, ALU.mult))
                        link(pool.tensor_tensor(s[:, half:2 * half], g[:, k, lead:lead + half], sin, ALU.mult))
                        link(pool.tensor_tensor(s[:, 0:half], g[:, k, lead + half:lead + 2 * half], sin, ALU.mult))
                        link(pool.tensor_scalar(s[:, 0:half], s[:, 0:half], -1.0, None, ALU.mult))

            rsqrt(R_NORM0)
            rsqrt(R_NORM0 + 1)
            pool.wait_ge(tab_in, 16 * 7)
            build_tables(lambda k, t: (tab0[:, k, t, 0, :], tab0[:, k, t, 1, :]), raw_gains, 32, 0, 0, 32)
            pool.engine_nop().then_inc(tabs_built, 1)
            for r in range(R_QK0, R_NORM1):
                rsqrt(r)
            pool.wait_ge(probs_transposed, 16)
            pool.dma_start(gain, A["l0_norm_ffn"].partition_broadcast(P)).then_inc(gain_loaded, 16)
            rsqrt(R_NORM1)
            rsqrt(R_NORM1 + 1)
            pool.wait_ge(transposed, X_NORM2)
            pool.dma_start(gain, A["l1_norm_attn"].partition_broadcast(P)).then_inc(gain_loaded, 16)
            pool.dma_start(lora_gain[:, 0:C_QR], A["l1_c_q_lora_norm"].partition_broadcast(P))\
                .then_inc(lora_loaded, 16)
            pool.dma_start(lora_gain[:, C_QR:C_QR + C_KVR], A["l1_c_kv_lora_norm"].partition_broadcast(P))\
                .then_inc(lora_loaded, 16)
            pool.dma_start(raw_gains1[:, 0, :], A["l1_c_q_norm"].partition_broadcast(P)).then_inc(lora_loaded, 16)
            pool.dma_start(raw_gains1[:, 1, :], A["l1_c_k_norm"].partition_broadcast(P)).then_inc(lora_loaded, 16)
            rsqrt(R_NORM2)
            rsqrt(R_NORM2 + 1)
            pool.wait_ge(lora_loaded, 64)
            build_tables(lambda k, t: (tab1[:, k, t, 0:96], tab1[:, k, t, 96:128]), raw_gains1, 16, 64, 64, 80)
            pool.engine_nop().then_inc(tabs_built, 1)
            for r in range(R_LORA, R_KQ1):
                rsqrt(r)
            half = C_ROPE // 2
            for t in range(NT):
                pool.wait_ge(evacuated, 11 + t)
                pool.wait_ge(squared, 17 + t)
                kr, out, tmp = z1[:, t, C_QR + C_KVR:C_IN], k_rope[:, t, 0:32], k_rope[:, t, 32:64]
                cos, sin = tab1[:, 1, t, C_NOPE:C_QK], tab1[:, 1, t, 96:128]
                link(pool.tensor_tensor(tmp[:, 0:half], kr[:, half:], sin[:, 0:half], ALU.mult))
                link(pool.tensor_tensor(tmp[:, half:], kr[:, 0:half], sin[:, half:], ALU.mult))
                link(pool.tensor_tensor(out, kr, cos, ALU.mult))
                link(pool.tensor_tensor(out, out, tmp, ALU.add))
                pool.tensor_scalar(k_rope[:, t, 64:65], k_rope[:, t, 64:65], C_QK * EPS, None, ALU.add)\
                    .then_inc(key_rotated, 1)
            for r in range(R_KQ1, R_NORM3):
                rsqrt(r)
            pool.wait_ge(qk_transposed, 24)
            pool.dma_start(triu, A["triu"]).then_inc(moe_loaded, 16)
            pool.dma_start(iota, A["iota"]).then_inc(moe_loaded, 16)
            pool.dma_start(arena1[:, 384:448], A["tie"]).then_inc(moe_loaded, 16)
            pool.memset(ones, 1.0).then_inc(pool_step, 1)
            steps[0] += 1
            pool.wait_ge(pool_step, steps[0])
            pool.wait_ge(probs_transposed, 32)
            pool.dma_start(gain, A["l1_norm_ffn"].partition_broadcast(P)).then_inc(gain_loaded, 16)
            pool.wait_ge(merged, 4)
            pool.memset(y_exp, 0.0).then_inc(y_evac, 1)
            pool.memset(scatT, 0.0).then_inc(y_evac, 1)
            pool.engine_nop().then_inc(tabs_built, 1)
            rsqrt(R_NORM3)
            rsqrt(R_NORM3 + 1)

        @block.scalar
        def _(a):
            steps = [0]

            def link(ins):
                steps[0] += 1
                ins.then_inc(act_step, 1)
                a.wait_ge(act_step, steps[0])

            def split_piece(u, n, e=None):
                a.wait_ge(ring_loaded[u % RING], per(16 * (u // RING + 1), e, 16 * NU // RING))
                if u >= SLOTS:
                    a.wait_ge(used, per(u - SLOTS + 1, e, NU))
                a.activation(w_hi[:, u % SLOTS, 0:n], ring[:, u % RING, 0:n], ACT.Copy).then_inc(hi_ready, 1)

            def split_ahead(u):
                v = u + SLOTS
                split_piece(v, piece_floats(STREAM[v]) if v < U0 else PIECE)

            def after(u, task=None):
                if task is not None:
                    a.wait_ge(used, u + 1)
                    task()
                split_ahead(u)

            def split_bank(i, dst, src, e=None, step=0):
                a.wait_ge(transposed, per(i + 1, e, step))
                a.activation(dst, src, ACT.Copy).then_inc(hi_split, 1)

            def split_h(i):
                for t in range(NT):
                    for g in range(2):
                        split_bank(i + 2 * t + g, hT_hi[:, 4 * g:4 * g + 4, t * P:(t + 1) * P],
                                   bank(2 * t + g).rearrange("p (c n) -> p c n", c=4))

            def norm_squares(r, sums):
                for t in range(NT):
                    if sums is None:
                        a.wait_ge(x_loaded[t], 16)
                    else:
                        a.wait_ge(x_updated, sums[t])
                    a.activation(h[:, t, :], x[:, t, :], ACT.Square,
                                 accum_out=stat[:, R_OFF[r + t]:R_OFF[r + t] + 1]).then_inc(squared, 1)

            def attention(s0, kind, ahead=()):
                def exps(i):
                    t, j = i // 4, i % 4
                    nk = P * (t + 1)
                    a.wait_ge(bias_ready, s0 // 2 + i + 1)
                    if i >= 2:
                        a.wait_ge(probs_transposed, s0 + 2 * i - 2)
                    sm = small[:, i % 2, :]
                    if kind == "AB" and j >= 2:
                        a.activation(sm[:, 16:20], sm[:, 12:16], ACT.Exp)
                    for s in range(2):
                        for m in range(2):
                            o, c = 2 * m + s, 4 * j + 2 * s + m
                            ins = a.activation(probs[:, i % 2, s, m, 0:nk],
                                               bank(6 * (i % 2) + m)[:, s * SEQ:s * SEQ + nk], ACT.Exp,
                                               bias=sm[:, 4 + o:5 + o], scale=q_scale[:, 0, t, c:c + 1],
                                               accum_out=sm[:, 8 + o:9 + o])
                        ins.then_inc(exp_done, 1)

                def copy_probs(j):
                    t, p = j // 8, j % 8
                    nb = (t + 1) * (1 if kind == "AB" and p < 4 else 2)
                    a.wait_ge(probs_transposed, s0 + j + 1)
                    if j >= 2:
                        a.wait_ge(pv_done, s0 + j - 1)
                    a.activation(probsT[:, j % 2, 0:nb, :],
                                 bank(2 + j % 2)[:, 0:nb * P].rearrange("p (b n) -> p b n", b=nb),
                                 ACT.Copy).then_inc(probsT_ready, 1)
                    if kind == "AB" and p == 5:
                        a.wait_ge(pv_done, s0 + 8 * t + 4)
                        for hd in range(A_HEADS):
                            c = R_OFF[R_SUB + t] + hd
                            ins = a.activation(h[:, t, hd * P:(hd + 1) * P], bank(4)[:, hd * P:(hd + 1) * P],
                                               ACT.Square, accum_out=stat[:, c:c + 1])
                        ins.then_inc(squared, 1)

                exps(0)
                exps(1)
                for j in range(8):
                    copy_probs(2 * j)
                    copy_probs(2 * j + 1)
                    if j + 2 < 8:
                        exps(j + 2)
                    if HI_AHEAD <= j < HI_AHEAD + len(ahead):
                        split_ahead(ahead[j - HI_AHEAD])

            norm_squares(R_NORM0, None)
            split_h(X_NORM0)
            for u in range(SLOTS):
                split_piece(u, piece_floats(STREAM[u]))

            def evacuate(dst, b):
                a.activation(dst, b, ACT.Copy).then_inc(evacuated, 1)

            for i, (_, n, c0, c1, w) in enumerate(IN0):
                def task():
                    q = IN0_ORDER.index(n)
                    for t in range(NT):
                        dst, src = z[:, t, n * COLS:n * COLS + w], bank((4 + 2 * q + t) % 8)[:, 0:w]
                        if n * COLS == ZB_Q:
                            dst = dst.rearrange("p (s m d) -> p m s d", s=4, m=2)
                            src = src.rearrange("p (m s d) -> p m s d", s=4, m=2)
                        evacuate(dst, src)
                    if q == 0:
                        a.wait_ge(normed, 2)
                    if q < 4:
                        a.wait_ge(evacuated, 2 * q + 2)
                        for t in range(NT):
                            if q:
                                a.wait_ge(ms_ready, R_QK0 + 2 * (q - 1) + t + 1)
                            m = IN0_HEADS[q] * HD
                            a.activation(sq[:, t * COLS:t * COLS + m], z[:, t, n * COLS:n * COLS + m], ACT.Square)\
                                .then_inc(squared, 1)
                if i < len(IN0) - LATE:
                    after(i, task if c1 == KC else None)
                elif c1 == KC:
                    a.wait_ge(used, i + 1)
                    task()
                if i == 1:
                    a.wait_ge(lam_exp, 1)
                    a.activation(lam[:, 2:4], lam[:, 0:2], ACT.Exp).then_inc(lam_exp, 1)

            def copy_heads(i, dst, b):
                a.wait_ge(qk_transposed, i + 1)
                a.activation(dst, b, ACT.Copy).then_inc(qkT_ready, 1)

            for t in range(NT):
                for g in range(0, 4, 2):
                    copy_heads(4 * t + g, qkT0[:, 4 * g:4 * g + 4, t * P:(t + 1) * P],
                               bank(4 * t + g).rearrange("p (s n) -> p s n", s=4))
            a.wait_ge(tabs_built, 1)
            attention(0, "AB", range(len(IN0) - LATE, len(IN0)))
            split_h(X_MERGE0)
            for i in range(len(OUT0) - 2):
                after(first(OUT0) + i)
            norm_squares(R_NORM1, (3, 4))
            split_h(X_NORM1)
            f0 = first(FFN)
            split_ahead(f0 - 2)
            split_ahead(f0 - 1)
            for i, (name, k, c0, c1, w) in enumerate(FFN):
                def exps():
                    for t in range(NT):
                        if k >= 1:
                            a.wait_ge(act_ready, 2 * k)
                        a.activation(sig[:, t, 0:w], bank(t)[:, 0:w], ACT.Tanh, scale=0.5).then_inc(sig_ready, 1)

                def split_act(kk, ww):
                    for t in range(NT):
                        nj = ww // P
                        split_bank(X_FFN + 2 * kk + t, aT_hi[:, 0:nj, t * P:(t + 1) * P],
                                   bank(2 + t)[:, 0:ww].rearrange("p (j n) -> p j n", j=nj))

                def acts():
                    if name == "ffn_u":
                        split_act(0, w)
                    else:
                        split_act(k + 1, min(COLS, FF - (k + 1) * COLS))
                if name == "ffn_g" and c1 == KC:
                    after(f0 + i, exps)
                elif (name == "ffn_u" and c1 == KC and k == 0) or \
                        (name == "ffn_d" and c1 * P == w and k + 1 < FFN_CHUNKS):
                    after(f0 + i, acts)
                elif i + 1 < len(FFN):
                    after(f0 + i)
            norm_squares(R_NORM2, (6, 8))
            split_h(X_NORM2)
            split_ahead(f0 + len(FFN) - 1)
            for i, (_, n, c0, c1, w) in enumerate(IN1):
                def task():
                    for t in range(NT):
                        evacuate(z1[:, t, :], bank(4 + t)[:, 0:w])
                if c1 < KC:
                    after(first(IN1) + i)
                else:
                    a.wait_ge(used, first(IN1) + i + 1)
                    task()
            for t in range(NT):
                split_bank(X_LORA + t, hT_hi[:, 0:3, t * P:(t + 1) * P],
                           bank(t)[:, 0:3 * P].rearrange("p (c n) -> p c n", c=3))
            for t in range(NT):
                a.wait_ge(evacuated, 11 + t)
                o = R_OFF[R_LORA + t]
                for c0, c1, acc in ((0, C_QR, stat[:, o:o + 1]), (C_QR, C_QR + C_KVR, stat[:, o + 1:o + 2]),
                                    (C_QR + C_KVR, C_IN, k_rope[:, t, 64:65])):
                    ins = a.activation(hflat[:, C_IN * t + c0:C_IN * t + c1], z1[:, t, c0:c1], ACT.Square,
                                       accum_out=acc)
                ins.then_inc(squared, 1)
            split_ahead(first(IN1) + len(IN1) - 1)

            for t in range(NT):
                if t == 0:
                    a.wait_ge(first_tile, 3)
                    a.wait_ge(rstd_ready, R_LORA + NT)
                else:
                    a.wait_ge(used, first(UKV) + 1)
                kb = k1[:, t, :].rearrange("p (s n) -> p s n", n=C_QK)
                o = R_OFF[R_LORA + t]
                for n in range(4):
                    src = bank(4 * t + n).rearrange("p (s n) -> p s n", n=C_NOPE + C_V)
                    a.activation(kb[:, 4 * n:4 * n + 4, 0:C_NOPE], src[:, :, 0:C_NOPE], ACT.Copy,
                                 scale=stat[:, o + 1:o + 2]).then_inc(k_ready, 1)
                a.wait_ge(k_ready, 4 * t + 4)
                if t:
                    a.wait_ge(ms_ready, R_KQ1 + 1)
                a.activation(k_sq.rearrange("p (s n) -> p s n", n=C_NOPE), kb[:, :, 0:C_NOPE], ACT.Square)\
                    .then_inc(squared, 1)
                if t == 0:
                    split_ahead(first(UKV))
                else:
                    vb = v1[:, t, :].rearrange("p (s n) -> p s n", n=C_V)
                    for n in range(4):
                        src = bank(4 * t + n).rearrange("p (s n) -> p s n", n=C_NOPE + C_V)
                        ins = a.activation(vb[:, 4 * n:4 * n + 4, :], src[:, :, C_NOPE:], ACT.Copy,
                                           scale=stat[:, o + 1:o + 2])
                    ins.then_inc(v_ready, 1)
            for t in range(NT):
                if t == 0:
                    a.wait_ge(first_tile, 4)
                    a.wait_ge(normed, 8)
                    a.wait_ge(tabs_built, 2)
                else:
                    a.wait_ge(used, first(UQ) + len(UQ))
                o = R_OFF[R_LORA + t]
                for n in range(3):
                    a.activation(q1[t][:, n * COLS:(n + 1) * COLS], bank(4 * t + n), ACT.Copy,
                                 scale=stat[:, o:o + 1]).then_inc(q_evac, 1)
                a.wait_ge(q_evac, 3 * t + 3)
                if t:
                    a.wait_ge(ms_ready, R_KQ1 + NT + 1)
                a.activation(q_sq, q1[t], ACT.Square).then_inc(q_squared, 1)

            for t in range(NT):
                for q, dst in enumerate((kT1, qT1)):
                    for g in range(3):
                        if t == 0 and q == 1 and g == 2:
                            a.wait_ge(ms_ready, R_KQ1 + 2 * NT)
                        copy_heads(8 + 8 * t + 4 * q + g, dst[0:C_QK, 4 * g:4 * g + 4, t * P:(t + 1) * P],
                                   bank(4 * t + g)[0:C_QK, :].rearrange("p (s n) -> p s n", s=4))
            attention(16, "C", [first(UQ) + i for i in range(len(UQ))])
            split_h(X_MERGE1)
            for i in range(len(OUT1) - 2):
                after(first(OUT1) + i)
            norm_squares(R_NORM3, (11, 12))
            split_h(X_NORM3)
            split_ahead(U0 - 2)
            split_ahead(U0 - 1)
            a.wait_ge(router_step, 1)
            a.activation(rt[:, 0:16], rt[:, 16:32], ACT.Exp).then_inc(logit_exp, 1)

            def expert_pass(p):
                ub = U0 + p * NE * NU
                xb = X_EXP + p * X_PER_PASS
                cb = NT * FFN_CHUNKS + p * NE * EXP_CHUNKS

                def gather_split(i, e=None):
                    for g in range(2):
                        split_bank(i + g, hT_hi[:, 4 * g:4 * g + 4, 0:P],
                                   bank(6 + g).rearrange("p (c n) -> p c n", c=4), e, X_PER_EXPERT)

                if p:
                    for i in range(SLOTS):
                        split_piece(ub + i, PIECE)
                gather_split(xb)
                for b in range(4):
                    a.wait_ge(scat_transposed, 4 * p + b + 1)
                    a.activation(scatT_all[:, 2 * b:2 * b + 2, :],
                                 bank(SCAT_BANKS[b]).rearrange("p (e n) -> p e n", e=2), ACT.Copy)\
                        .then_inc(scat_ready, 1)

                def expert(e, last):
                    for i, (kind, k, half) in enumerate(EXP):
                        a.wait_ge(used, per(ub + i + 1, e, NU))
                        if kind == "g" and half:
                            a.wait_ge(act_ready, per(cb + k - 1, e, EXP_CHUNKS))
                            a.activation(sig[:, k % 2, :], bank(k % 2), ACT.Tanh, scale=0.5).then_inc(sig_ready, 1)
                        if kind == "u" and half == 0 and k >= 1:
                            split_bank(xb + 2 + k - 1, aT_hi[:, :, 0:P],
                                       bank(6).rearrange("p (j n) -> p j n", j=4), e, X_PER_EXPERT)
                        if kind == "u" and half and k == 0:
                            a.wait_ge(scattered, per(4 + p * 4 * (NE + 1), e, 4))
                            if p == 0:
                                a.wait_ge(scat_ready, 4)
                            a.activation(scatT, scatT_all[:, bass.ds(e, 1), :].rearrange("p e n -> p (e n)"),
                                         ACT.Copy)
                        if kind == "u" and half and k == EXP_CHUNKS - 1 and not last:
                            gather_split(xb + 2 + 6, e)
                        if kind == "d" and half and k == EXP_CHUNKS - 2:
                            split_bank(xb + 2 + (6 if last else 8), aT_hi[:, :, 0:P],
                                       bank(6).rearrange("p (j n) -> p j n", j=4), e, X_PER_EXPERT)
                        if kind == "d" and half and k == EXP_CHUNKS - 1:
                            for n in range(2):
                                a.activation(y_exp[:, n * COLS:(n + 1) * COLS], bank(4 + n), ACT.Copy)\
                                    .then_inc(y_evac, 1)
                        if i + SLOTS < NU or not last:
                            split_piece(ub + i + SLOTS, PIECE, e)

                with a.Fori(0, NE - 1) as e:
                    expert(e, False)
                expert(NE - 1, True)

            expert_pass(0)
            a.wait_ge(flag_ready, 1)
            most = a.value_load(nmax_i[0:1, 0:1], min_val=0, max_val=SEQ)
            with a.If(most > P):
                expert_pass(1)

        @block.vector
        def _(v):
            steps = [0]

            def link(ins):
                steps[0] += 1
                ins.then_inc(dve_step, 1)
                v.wait_ge(dve_step, steps[0])

            def split_piece(u, n, e=None):
                v.wait_ge(hi_ready, per(u + 1, e, NU))
                v.tensor_tensor(w_lo[:, u % SLOTS, 0:n], ring[:, u % RING, 0:n],
                                w_hi[:, u % SLOTS, 0:n].bitcast(f32), ALU.subtract).then_inc(lo_ready, 1)

            def split_ahead(u):
                w = u + SLOTS
                split_piece(w, piece_floats(STREAM[w]) if w < U0 else PIECE)

            def after(u, task=None):
                if task is not None:
                    v.wait_ge(used, u + 1)
                    task()
                split_ahead(u)

            def split_bank(i, dst, hi, src, e=None, step=0):
                v.wait_ge(hi_split, per(i + 1, e, step))
                v.tensor_tensor(dst, src, hi.bitcast(f32), ALU.subtract).then_inc(lo_split, 1)

            def split_h(i):
                for t in range(NT):
                    for g in range(2):
                        s = (slice(None), slice(4 * g, 4 * g + 4), slice(t * P, (t + 1) * P))
                        split_bank(i + 2 * t + g, hT_lo[s], hT_hi[s],
                                   bank(2 * t + g).rearrange("p (c n) -> p c n", c=4))

            def mean_square(r, inv, cols=None):
                s = stat[:, R_OFF[r]:R_OFF[r] + R_COLS[r]]
                v.tensor_scalar(s, s, inv, EPS, ALU.mult, ALU.add).then_inc(ms_ready, 1)

            def norm_mean(r, nsq, t):
                v.wait_ge(squared, nsq + t + 1)
                mean_square(r + t, 1.0 / D)

            def norm(i, r, nsq, first_mean=True):
                if first_mean:
                    norm_mean(r, nsq, 0)
                for t in range(NT):
                    if t:
                        norm_mean(r, nsq, 1)
                    v.wait_ge(rstd_ready, r + t + 1)
                    if t == 0 and i == 0:
                        v.wait_ge(gain0_loaded, 16)
                    elif t == 0:
                        v.wait_ge(gain_loaded, 16 * i)
                    v.scalar_tensor_tensor(out=h[:, t, :], in0=x[:, t, :], scalar=stat[:, R_OFF[r + t]:R_OFF[r + t] + 1],
                                           in1=gain, op0=ALU.mult, op1=ALU.mult).then_inc(normed, 1)

            def rotate(zt, nh, width, lead, half, cos, sin):
                s = zt.rearrange("p (s n) -> p s n", n=width)
                tmp = rope_tmp[:, 0:nh * 2 * half].rearrange("p (s n) -> p s n", n=2 * half)
                link(v.tensor_tensor(tmp[:, :, 0:half], s[:, :, lead + half:lead + 2 * half],
                                     bc(sin[:, 0:half], 1, nh), ALU.mult))
                link(v.tensor_tensor(tmp[:, :, half:2 * half], s[:, :, lead:lead + half],
                                     bc(sin[:, half:2 * half], 1, nh), ALU.mult))
                link(v.tensor_tensor(s, s, bc(cos, 1, nh), ALU.mult))
                return v.tensor_tensor(s[:, :, lead:], s[:, :, lead:], tmp, ALU.add)

            def query_scale(t, c0, r, nh, scale):
                s = stat[:, R_OFF[r]:R_OFF[r] + nh]
                link(v.tensor_scalar(q_scale[:, 0, t, c0:c0 + nh], s, scale, None, ALU.mult))
                link(v.tensor_scalar(q_scale[:, 1, t, c0:c0 + nh], s, -scale, None, ALU.mult))

            def attention(s0, kind, ahead=()):
                def front(i):
                    t, j = i // 4, i % 4
                    nk = P * (t + 1)
                    b = 6 * (i % 2)
                    sc = PS[:, b:b + 2, :].rearrange("p m (s n) -> p m s n", s=2)
                    fields = small[:, i % 2, :].rearrange("p (f m s) -> p f m s", m=2, s=2)
                    scale = q_scale[:, 1, t, 4 * j:4 * j + 4].rearrange("p (s m) -> p m s", s=2)
                    v.wait_ge(scored, s0 // 2 + i + 1)
                    ins = v.memset(sc[0:CHUNK, :, :, nk - CHUNK:nk], NEG)
                    if kind == "AB" and j >= 2:
                        if t == 1:
                            link(ins)
                            ins = v.memset(sc[CHUNK:P, :, :, 0:CHUNK], NEG)
                        link(ins)
                        link(v.tensor_reduce(fields[:, 0], sc[:, :, :, 0:nk], AX.X, ALU.max))
                        link(v.tensor_tensor(fields[:, 5], fields[:, 0], scale, ALU.mult))
                        link(v.tensor_tensor(fields[:, 1], fields[:, 5], sink_of(1, j), ALU.min))
                        v.tensor_tensor(fields[:, 3], fields[:, 1], sink_of(0, j), ALU.add)\
                            .then_inc(bias_ready, 1)
                    else:
                        link(ins)
                        link(v.tensor_reduce(fields[:, 0], sc[:, :, :, 0:nk], AX.X, ALU.max))
                        v.tensor_tensor(fields[:, 1], fields[:, 0], scale, ALU.mult).then_inc(bias_ready, 1)

                def sink_of(k, j):
                    return sinks[:, k, :].rearrange("p (m s) -> p m s", m=2)[:, :, 2 * j - 4:2 * j - 2]

                def back(i):
                    t, j = i // 4, i % 4
                    nk = P * (t + 1)
                    sm = small[:, i % 2, :]
                    fields = sm.rearrange("p (f m s) -> p f m s", m=2, s=2)
                    v.wait_ge(exp_done, s0 + 2 * i + 2)
                    if kind == "C":
                        link(v.reciprocal(rinv[:, t, 4 * j:4 * j + 4].rearrange("p (s m) -> p m s", s=2), fields[:, 2]))
                    elif j >= 2:
                        link(v.tensor_tensor(fields[:, 2], fields[:, 2], fields[:, 4], ALU.add))
                        link(v.reciprocal(rinv[:, t, 0:8].rearrange("p (m s) -> p m s", m=2)[:, :, 2 * j - 4:2 * j - 2],
                                          fields[:, 2]))
                    else:
                        link(v.reciprocal(sm[:, 24:28], sm[:, 8:12]))
                        v.tensor_scalar(sm[:, 28:30], sm[:, 26:28], lam[:, 4:5], None, ALU.mult)
                        for s in range(2):
                            p0 = probs[:, i % 2, s, 0, 0:nk]
                            ins = v.tensor_scalar(p0, p0, sm[:, 24 + s:25 + s], None, ALU.mult)
                        link(ins)
                        for s in range(2):
                            p0, p1 = probs[:, i % 2, s, 0, 0:nk], probs[:, i % 2, s, 1, 0:nk]
                            v.scalar_tensor_tensor(out=p0, in0=p1, scalar=sm[:, 28 + s:29 + s], in1=p0,
                                                   op0=ALU.mult, op1=ALU.add).then_inc(probs_ready, 1)
                    if kind == "AB" and j == 3:
                        v.wait_ge(squared, 11 + t)
                        mean_square(R_SUB + t, 1.0 / A_VD)

                def final(t):
                    v.wait_ge(pv_done, s0 + 8 * t + 8)
                    if kind == "AB":
                        o = R_OFF[R_SUB + t]
                        v.tensor_tensor(h[:, t, 512:1024].rearrange("p (s n) -> p s n", n=HD),
                                        bank(5).rearrange("p (s n) -> p s n", n=HD),
                                        bc(rinv[:, t, 0:8], 2, HD), ALU.mult)
                        v.wait_ge(rstd_ready, R_SUB + t + 1)
                        ha = h[:, t, 0:512].rearrange("p (s n) -> p s n", n=A_VD)
                        link(v.tensor_tensor(ha, bank(4).rearrange("p (s n) -> p s n", n=A_VD),
                                             bc(stat[:, o:o + 4], 2, A_VD), ALU.mult))
                        v.tensor_tensor(ha, ha, bc(subln[:, :], 1, A_HEADS), ALU.mult).then_inc(merged, 1)
                    else:
                        for n in range(2):
                            ins = v.tensor_tensor(h[:, t, n * 512:(n + 1) * 512].rearrange("p (s n) -> p s n", n=C_V),
                                                  bank(4 + n).rearrange("p (s n) -> p s n", n=C_V),
                                                  bc(rinv[:, t, 8 * n:8 * n + 8], 2, C_V), ALU.mult)
                        ins.then_inc(merged, 1)

                front(0)
                front(1)
                for j in range(8):
                    back(j)
                    if j + 2 < 8:
                        front(j + 2)
                    if j == 3:
                        final(0)
                    if LO_AHEAD <= j < LO_AHEAD + len(ahead):
                        split_ahead(ahead[j - LO_AHEAD])
                final(1)

            def add_residual(t, n, b):
                xs = x[:, t, n * COLS:(n + 1) * COLS]
                v.tensor_tensor(xs, xs, b, ALU.add).then_inc(x_updated, 1)

            def residual(pieces, k, r, nsq):
                u0, last = first(pieces), pieces[-1][1]
                for i, (_, n, c0, c1, w) in enumerate(pieces):
                    def task():
                        for t in range(NT):
                            add_residual(t, n, bank(4 + 2 * n + t))
                    if i + 2 < len(pieces):
                        after(u0 + i, task if c1 == KC else None)
                v.wait_ge(first_tile, k)
                add_residual(0, last, bank(4 + 2 * last))
                norm_mean(r, nsq, 0)
                v.wait_ge(used, u0 + len(pieces))
                add_residual(1, last, bank(5 + 2 * last))

            norm(0, R_NORM0, 0)
            split_h(X_NORM0)
            for u in range(SLOTS):
                split_piece(u, piece_floats(STREAM[u]))
            v.wait_ge(early_loaded, 48)
            link(v.tensor_copy(rw_split[:, :, 0:NE], rw[:, :, :]))
            link(v.tensor_tensor(rw_split[:, :, NE:2 * NE], rw[:, :, :], rw_split[:, :, 0:NE].bitcast(f32),
                                 ALU.subtract))
            link(v.tensor_scalar(subln[:, :], subln[:, :], 1.0 - LAM_INIT, None, ALU.mult))
            link(v.tensor_scalar(sinks[:, 1, :], sinks[:, 0, :], -1.0, None, ALU.mult))
            v.wait_ge(tab_in, 16 * 7)
            link(v.tensor_tensor(rope_tmp[:, 0:HD], raw_lam[:, 0, :], raw_lam[:, 1, :], ALU.mult))
            link(v.tensor_tensor(rope_tmp[:, HD:2 * HD], raw_lam[:, 2, :], raw_lam[:, 3, :], ALU.mult))
            v.tensor_reduce(lam[:, 0:2], rope_tmp[:, 0:2 * HD].rearrange("p (k n) -> p k n", k=2), AX.X, ALU.add)\
                .then_inc(lam_exp, 1)

            v.wait_ge(tabs_built, 1)
            tables = (2, 3, 0, 1)

            def chunk_heads(t, q):
                n = IN0_ORDER[q]
                return z[:, t, n * COLS:n * COLS + IN0_HEADS[q] * HD]

            for i, (_, n, c0, c1, w) in enumerate(IN0):
                def task():
                    q = IN0_ORDER.index(n)
                    if q == 4:
                        return
                    nh = IN0_HEADS[q]
                    for t in range(NT):
                        r = R_QK0 + 2 * q + t
                        v.wait_ge(squared, 3 + 2 * q + t)
                        link(v.tensor_reduce(stat[:, R_OFF[r]:R_OFF[r] + nh],
                                             sq[:, t * COLS:t * COLS + nh * HD].rearrange("p (s n) -> p s n", n=HD),
                                             AX.X, ALU.add))
                        mean_square(r, 1.0 / HD)
                    for t in range(NT):
                        r = R_QK0 + 2 * q + t
                        link(rotate(chunk_heads(t, q), nh, HD, 0, HD // 2, tab0[:, tables[q], t, 0, :],
                                    tab0[:, tables[q], t, 1, :]))
                        v.wait_ge(rstd_ready, r + 1)
                        if q in (1, 3):
                            s = chunk_heads(t, q).rearrange("p (s n) -> p s n", n=HD)
                            v.tensor_tensor(s, s, bc(stat[:, R_OFF[r]:R_OFF[r] + nh], 2, HD), ALU.mult)\
                                .then_inc(qk_normed, 1)
                        else:
                            query_scale(t, 8 if q == 0 else 0, r, nh, HD ** -0.5)
                if i < len(IN0) - LATE:
                    after(i, task if c1 == KC else None)
                elif c1 == KC:
                    v.wait_ge(used, i + 1)
                    task()
            def copy_heads(i, dst, b):
                v.wait_ge(qk_transposed, i + 1)
                v.tensor_copy(dst, b).then_inc(qkT_copied, 1)

            for t in range(NT):
                for g in range(1, 4, 2):
                    m = min(4, 13 - 4 * g)
                    copy_heads(4 * t + g, qkT0[:, 4 * g:4 * g + m, t * P:(t + 1) * P],
                               bank(4 * t + g)[:, 0:m * P].rearrange("p (s n) -> p s n", s=m))
            v.wait_ge(lam_exp, 2)
            link(v.tensor_tensor(lam[:, 4:5], lam[:, 3:4], lam[:, 2:3], ALU.subtract))
            link(v.tensor_scalar(lam[:, 4:5], lam[:, 4:5], -LAM_INIT, None, ALU.add))
            attention(0, "AB", range(len(IN0) - LATE, len(IN0)))
            split_h(X_MERGE0)
            residual(OUT0, 1, R_NORM1, 12)
            norm(1, R_NORM1, 12, False)
            split_h(X_NORM1)
            f0 = first(FFN)
            split_ahead(f0 - 2)
            split_ahead(f0 - 1)

            def silu(src_g, src_u, sg, ac, base):
                v.scalar_tensor_tensor(out=ac, in0=sg, scalar=1.0, in1=src_g, op0=ALU.add, op1=ALU.mult)\
                    .then_inc(silu_step, 1)
                v.wait_ge(silu_step, base + 1)
                v.scalar_tensor_tensor(out=ac, in0=ac, scalar=0.5, in1=src_u, op0=ALU.mult, op1=ALU.mult)\
                    .then_inc(act_ready, 1)

            for i, (name, k, c0, c1, w) in enumerate(FFN):
                def silus():
                    for t in range(NT):
                        v.wait_ge(sig_ready, 2 * k + t + 1)
                        silu(bank(t)[:, 0:w], bank(2 + t)[:, 0:w], sig[:, t, 0:w], act[:, t, 0:w],
                             2 * k + t)

                def split_act(kk, ww):
                    nj = ww // P
                    for t in range(NT):
                        s = (slice(None), slice(0, nj), slice(t * P, (t + 1) * P))
                        split_bank(X_FFN + 2 * kk + t, aT_lo[s], aT_hi[s],
                                   bank(2 + t)[:, 0:ww].rearrange("p (j n) -> p j n", j=nj))

                def acts():
                    if name == "ffn_u":
                        silus()
                        split_act(0, w)
                    else:
                        split_act(k + 1, min(COLS, FF - (k + 1) * COLS))
                if name == "ffn_u" and c1 == KC and k:
                    after(f0 + i, silus)
                elif (name == "ffn_u" and c1 == KC) or \
                        (name == "ffn_d" and c1 * P == w and k + 1 < FFN_CHUNKS):
                    after(f0 + i, acts)
                elif i + 1 < len(FFN):
                    after(f0 + i)
            for t in range(NT):
                if t == 0:
                    v.wait_ge(first_tile, 2)
                else:
                    norm_mean(R_NORM2, 14, 0)
                    v.wait_ge(used, f0 + len(FFN))
                for n in range(2):
                    add_residual(t, n, bank(4 + 2 * t + n))
            norm(2, R_NORM2, 14, False)
            split_h(X_NORM2)
            split_ahead(f0 + len(FFN) - 1)
            after(first(IN1))
            v.wait_ge(lora_loaded, 64)
            for t in range(NT):
                v.wait_ge(evacuated, 11 + t)
                v.tensor_tensor(zg[:, t, :], z1[:, t, 0:C_QR + C_KVR], lora_gain, ALU.mult).then_inc(normed, 1)
            for t in range(NT):
                s = (slice(None), slice(0, 3), slice(t * P, (t + 1) * P))
                split_bank(X_LORA + t, hT_lo[s], hT_hi[s], bank(t)[:, 0:3 * P].rearrange("p (c n) -> p c n", c=3))
            for t in range(NT):
                o = R_OFF[R_LORA + t]
                v.wait_ge(squared, 17 + t)
                link(v.tensor_scalar(stat[:, o:o + 1], stat[:, o:o + 1], 1.0 / C_QR, EPS, ALU.mult, ALU.add))
                v.tensor_scalar(stat[:, o + 1:o + 2], stat[:, o + 1:o + 2], 1.0 / C_KVR, EPS, ALU.mult, ALU.add)\
                    .then_inc(ms_ready, 1)
            split_ahead(first(IN1) + 1)
            v.wait_ge(tabs_built, 2)
            half = C_ROPE // 2

            def key_sums(t):
                r = R_KQ1 + t
                s = stat[:, R_OFF[r]:R_OFF[r] + C_HEADS]
                v.wait_ge(squared, 19 + t)
                v.wait_ge(key_rotated, t + 1)
                link(v.tensor_reduce(s, k_sq.rearrange("p (s n) -> p s n", n=C_NOPE), AX.X, ALU.add))
                v.tensor_scalar(s, s, k_rope[:, t, 64:65], 1.0 / C_QK, ALU.add, ALU.mult).then_inc(ms_ready, 1)

            def key_heads(t):
                r = R_KQ1 + t
                s = stat[:, R_OFF[r]:R_OFF[r] + C_HEADS]
                kb = k1[:, t, :].rearrange("p (s n) -> p s n", n=C_QK)
                v.wait_ge(rstd_ready, r + 1)
                v.tensor_tensor(kb[:, :, 0:C_NOPE], kb[:, :, 0:C_NOPE], bc(s, 2, C_NOPE), ALU.mult)
                v.tensor_tensor(kb[:, :, C_NOPE:], bc(k_rope[:, t, 0:C_ROPE], 1, C_HEADS), bc(s, 2, C_ROPE), ALU.mult)\
                    .then_inc(qk_normed, 1)

            def values(t):
                vb = v1[:, t, :].rearrange("p (s n) -> p s n", n=C_V)
                o = R_OFF[R_LORA + t]
                for n in range(4):
                    src = bank(4 * t + n).rearrange("p (s n) -> p s n", n=C_NOPE + C_V)
                    v.wait_ge(k_ready, 4 * t + n + 1)
                    ins = v.tensor_scalar(vb[:, 4 * n:4 * n + 4, :], src[:, :, C_NOPE:], stat[:, o + 1:o + 2], None,
                                          ALU.mult)
                ins.then_inc(v_copied, 1)

            def query_heads(t):
                r = R_KQ1 + NT + t
                v.wait_ge(q_squared, t + 1)
                link(v.tensor_reduce(stat[:, R_OFF[r]:R_OFF[r] + C_HEADS],
                                     q_sq.rearrange("p (s n) -> p s n", n=C_QK), AX.X, ALU.add))
                mean_square(r, 1.0 / C_QK)
                rotate(q1[t], C_HEADS, C_QK, C_NOPE, half, tab1[:, 0, t, 0:96], tab1[:, 0, t, 96:128])\
                    .then_inc(qk_normed, 1)

            def transposed_heads(t, q):
                g = 3
                copy_heads(8 + 8 * t + 4 * q + g, (kT1, qT1)[q][0:C_QK, 4 * g:4 * g + 4, t * P:(t + 1) * P],
                           bank(4 * t + g)[0:C_QK, :].rearrange("p (s n) -> p s n", s=4))

            for t in range(NT):
                v.wait_ge(rstd_ready, R_LORA + t + 1)
                if t == 0:
                    values(t)
                key_sums(t)
                if t == 0:
                    split_ahead(first(UKV))
            for t in range(NT):
                key_heads(t)
            query_heads(0)
            transposed_heads(0, 0)
            query_heads(1)
            transposed_heads(0, 1)
            transposed_heads(1, 0)
            for t in range(NT):
                v.wait_ge(rstd_ready, R_KQ1 + NT + t + 1)
                query_scale(t, 0, R_KQ1 + NT + t, C_HEADS, C_QK ** -0.5)
            transposed_heads(1, 1)
            attention(16, "C", [first(UQ) + i for i in range(len(UQ))])
            split_h(X_MERGE1)
            residual(OUT1, 5, R_NORM3, 20)
            norm(3, R_NORM3, 20, False)
            split_h(X_NORM3)
            L = rt[:, 32:48]
            Lt = L.rearrange("p (t e) -> p t e", t=NT)
            v.wait_ge(routed, 1)
            v.wait_ge(moe_loaded, 48)
            v.wait_ge(tabs_built, 3)
            halves = bank(4)[:, 0:2 * NT * NE].rearrange("p (t k e) -> p t k e", t=NT, k=2)
            link(v.tensor_copy(Lt, halves[:, :, 0]))
            link(v.tensor_tensor(Lt, Lt, halves[:, :, 1], ALU.add))
            link(v.tensor_reduce(rt[:, 48:50], Lt, AX.X, ALU.max))
            v.tensor_tensor(rt[:, 16:32].rearrange("p (t e) -> p t e", t=NT), Lt, bc(rt[:, 48:50], 2, NE),
                            ALU.subtract).then_inc(router_step, 1)
            gt = rt[:, 64:192].rearrange("p (t e f) -> p t e f", t=NT, e=NE)
            eq = rt[:, 256:384].rearrange("p (t e f) -> p t e f", t=NT, e=NE)
            sel = rt[:, 192:208]
            gates = rt[:, 208:224]
            mine, others = bc(Lt, 3, NE), bc(Lt, 2, NE)
            link(v.tensor_tensor(gt, others, mine, ALU.is_gt))
            link(v.tensor_tensor(eq, others, mine, ALU.is_equal))
            link(v.tensor_tensor(eq, eq, bc(tie, 1, NT), ALU.mult))
            link(v.tensor_tensor(gt, gt, eq, ALU.add))
            link(v.tensor_reduce(sel.rearrange("p (t e) -> p t e", t=NT), gt, AX.X, ALU.add))
            v.tensor_scalar(sel, sel, 1.5, None, ALU.is_lt).then_inc(ranks_ready, 1)
            v.wait_ge(ranks_ready, 1)
            v.wait_ge(logit_exp, 1)
            gates3 = gates.rearrange("p (t e) -> p t e", t=NT)
            link(v.tensor_tensor(gates, rt[:, 0:16], sel, ALU.mult))
            link(v.tensor_reduce(rt[:, 52:54], gates3, AX.X, ALU.add))
            link(v.reciprocal(rt[:, 54:56], rt[:, 52:54]))
            link(v.tensor_tensor(gates3, gates3, bc(rt[:, 54:56], 2, NE), ALU.mult))
            split_ahead(U0 - 2)
            slot = rt[:, 224:240]
            v.wait_ge(counted, 1)
            link(v.scalar_tensor_tensor(out=slot, in0=bank(6)[:, 0:16], scalar=1.0, in1=sel, op0=ALU.add, op1=ALU.mult))
            link(v.tensor_scalar(slot, slot, -1.0, None, ALU.add))

            def expert_pass(p):
                ub = U0 + p * NE * NU
                xb = X_EXP + p * X_PER_PASS
                cb = NT * FFN_CHUNKS + p * NE * EXP_CHUNKS
                sb_ = p * 4 * (NE + 1)

                def gather_split(i, e=None):
                    for g in range(2):
                        s = (slice(None), slice(4 * g, 4 * g + 4), slice(0, P))
                        split_bank(i + g, hT_lo[s], hT_hi[s], bank(6 + g).rearrange("p (c n) -> p c n", c=4), e, X_PER_EXPERT)

                def act_split(i, e):
                    s = (slice(None), slice(0, 4), slice(0, P))
                    split_bank(i, aT_lo[s], aT_hi[s], bank(6).rearrange("p (j n) -> p j n", j=4), e, X_PER_EXPERT)

                def add_scattered(i, e=None, b=6):
                    v.wait_ge(scattered, per(sb_ + i + 1, e, 4))
                    xs = x[:, i % 4 // 2, (i % 2) * COLS:(i % 2 + 1) * COLS]
                    v.tensor_tensor(xs, xs, bank(b + i % 2), ALU.add).then_inc(scat_added, 1)

                if p:
                    v.wait_ge(stored, 64)
                    v.tensor_scalar(slot, slot, -float(P), None, ALU.add).then_inc(router_step, 1)
                    v.wait_ge(router_step, 2)
                for e0, e1 in ((0, 1), (1, NE)):
                    if p == 0 and e0:
                        v.wait_ge(counted, 2)
                        link(v.tensor_reduce(nmax[0:1, :], bank(7)[0:1, 0:8], AX.X, ALU.max))
                        v.tensor_copy(nmax_i[0:1, :], nmax[0:1, :]).then_inc(flag_ready, 1)
                    for t in range(NT):
                        v.tensor_tensor(onehot[:, t, e0:e1, :], bc(iota, 1, e1 - e0),
                                        bc(slot[:, 8 * t + e0:8 * t + e1], 2, P), ALU.is_equal)\
                            .then_inc(onehot_ready, 1)
                v.wait_ge(onehot_ready, 6 * p + 4)
                for t in range(NT):
                    v.tensor_tensor(onehot_gated[:, t, :, :], onehot[:, t, 0:NE, :],
                                    bc(gates[:, 8 * t:8 * t + 8], 2, P), ALU.mult).then_inc(onehot_ready, 1)
                if p:
                    for i in range(SLOTS):
                        split_piece(ub + i, PIECE)
                gather_split(xb)
                if p == 0:
                    split_ahead(U0 - 1)

                def expert(e, last):
                    for i, (kind, k, half) in enumerate(EXP):
                        v.wait_ge(used, per(ub + i + 1, e, NU))
                        if kind == "g" and half:
                            v.wait_ge(sig_ready, per(cb + k + 1, e, EXP_CHUNKS))
                            sg, ac = sig[:, k % 2, :], act[:, k % 2, :]
                            v.scalar_tensor_tensor(out=ac, in0=sg, scalar=1.0, in1=bank(k % 2), op0=ALU.add,
                                                   op1=ALU.mult).then_inc(silu_step, 1)
                            if k == 0:
                                for q in range(2):
                                    add_scattered(q, e)
                        if kind == "u" and half == 0 and k == 0:
                            for q in range(2, 4):
                                add_scattered(q, e)
                        if kind == "u" and half == 0 and k >= 1:
                            act_split(xb + 2 + k - 1, e)
                        if kind == "u" and half:
                            ac = act[:, k % 2, :]
                            v.wait_ge(silu_step, per(cb + k + 1, e, EXP_CHUNKS))
                            v.scalar_tensor_tensor(out=ac, in0=ac, scalar=0.5, in1=bank(2 + k % 2), op0=ALU.mult,
                                                   op1=ALU.mult).then_inc(act_ready, 1)
                            if k == EXP_CHUNKS - 1 and not last:
                                gather_split(xb + 2 + 6, e)
                        if kind == "d" and half and k == EXP_CHUNKS - 2:
                            act_split(xb + 2 + (6 if last else 8), e)
                            if last:
                                split_piece(ub + NU - 1, PIECE, e)
                        if i + SLOTS < NU - 1 or not last:
                            split_piece(ub + i + SLOTS, PIECE, e)

                with v.Fori(0, NE - 1) as e:
                    expert(e, False)
                expert(NE - 1, True)
                for q in range(4):
                    add_scattered(4 * NE + q, b=6 if q < 2 else 0)

            expert_pass(0)
            most = v.value_load(nmax_i[0:1, 0:1], min_val=0, max_val=SEQ)
            with v.If(most > P):
                expert_pass(1)

        @block.tensor
        def _(pe):
            def product(out, xh, xl, wh, wl, start, stop):
                pe.matmul(out, xh, wh, start=start, stop=False)
                pe.matmul(out, xh, wl, start=False, stop=False)
                return pe.matmul(out, xl, wh, start=False, stop=stop)

            def keep_clock(b, n):
                for _ in range(n):
                    pe.matmul(bank(b), hT_hi[:, 0, 0:P], hT_hi[:, 0:2, :].rearrange("p c n -> p (c n)"),
                              start=True, stop=True)

            def transpose_h(i, waits):
                for t in range(NT):
                    waits(t)
                    for g in range(2):
                        for c in range(4):
                            cc = 4 * g + c
                            ins = pe.transpose(bank(2 * t + g)[:, c * P:(c + 1) * P], h[:, t, cc * P:(cc + 1) * P],
                                               ident[:, :])
                        ins.then_inc(transposed, 1)

            def normed_wait(n):
                return lambda t: pe.wait_ge(normed, n + t + 1)

            def piece_wait(u):
                pe.wait_ge(lo_ready, u + 1)

            def project(pieces, kc, bank_of, free=None, early_sum=False):
                u0 = first(pieces)
                for i, (_, n, c0, c1, w) in enumerate(pieces):
                    u = u0 + i
                    piece_wait(u)
                    s = u % SLOTS
                    for t in range(NT):
                        if free is not None and c0 == 0:
                            free(n, t)
                        for c in range(c0, c1):
                            o = (c - c0) * w
                            ins = product(bank_of(n, t)[:, 0:w], hT_hi[:, c, t * P:(t + 1) * P],
                                          hT_lo[:, c, t * P:(t + 1) * P], w_hi[:, s, o:o + w], w_lo[:, s, o:o + w],
                                          c == 0, c == kc - 1)
                        if early_sum and t == 0 and i == len(pieces) - 1:
                            ins.then_inc(first_tile, 1)
                    ins.then_inc(used, 1)

            def attention(s0, kind, between=None):
                def scores(i):
                    t = i // 4
                    nk = P * (t + 1)
                    if i >= 2:
                        pe.wait_ge(exp_done, s0 + 2 * i - 2)
                    for s in range(2):
                        p = 2 * (i % 4) + s
                        for m in range(2):
                            if kind == "AB":
                                r = slice(m * HD, (m + 1) * HD)
                                q = qkT0[r, p if p < 4 else 8 + p - 4, t * P:(t + 1) * P]
                                kk = qkT0[r, 4 + p if p < 4 else 12, 0:nk]
                            else:
                                q = qT1[0:C_QK, 2 * p + m, t * P:(t + 1) * P]
                                kk = kT1[0:C_QK, 2 * p + m, 0:nk]
                            ins = pe.matmul(bank(6 * (i % 2) + m)[:, s * SEQ:s * SEQ + nk], q, kk, start=True, stop=True)
                    ins.then_inc(scored, 1)

                def transposes(i):
                    t, p = i // 8, i % 8
                    maps = 1 if kind == "AB" and p < 4 else 2
                    if maps == 1:
                        pe.wait_ge(probs_ready, 4 * t + p + 1)
                    else:
                        pe.wait_ge(exp_done, s0 + i + 1)
                    if i >= 2:
                        pe.wait_ge(probsT_ready, s0 + i - 1)
                    for m in range(maps):
                        for b in range(t + 1):
                            j = m * (t + 1) + b
                            ins = pe.transpose(bank(2 + i % 2)[:, j * P:(j + 1) * P],
                                               probs[:, i // 2 % 2, i % 2, m, b * P:(b + 1) * P], ident[:, :])
                    ins.then_inc(probs_transposed, 1)

                def values(i):
                    t, p = i // 8, i % 8
                    pe.wait_ge(probsT_ready, s0 + i + 1)
                    if i == 8:
                        pe.wait_ge(merged, s0 // 8 + 1)
                    maps = 1 if kind == "AB" and p < 4 else 2
                    for m in range(maps):
                        if kind == "AB" and p < 4:
                            out = bank(4)[:, p * P:(p + 1) * P]
                            col, w = ZA_V + p * A_VD, A_VD
                        elif kind == "AB":
                            hd = p - 4 + 4 * m
                            out = bank(5)[:, hd * HD:(hd + 1) * HD]
                            col, w = ZB_V + m * HD, HD
                        else:
                            hd = 2 * p + m
                            out = bank(4 + hd // 8)[:, (hd % 8) * C_V:(hd % 8 + 1) * C_V]
                            col, w = hd * C_V, C_V
                        for b in range(t + 1):
                            vv = (z if kind == "AB" else v1)[:, b, col:col + w]
                            ins = pe.matmul(out, probsT[:, i % 2, m * (t + 1) + b, :], vv,
                                            start=b == 0, stop=b == t)
                    ins.then_inc(pv_done, 1)

                scores(0)
                if between is not None:
                    between()
                scores(1)
                for i in range(8):
                    keep_clock(2, FILL[i // 4])
                    if i + 2 < 8:
                        scores(i + 2)
                    transposes(2 * i)
                    transposes(2 * i + 1)
                    values(2 * i)
                    values(2 * i + 1)

            pe.wait_ge(ident_loaded, 16)
            transpose_h(X_NORM0, normed_wait(0))

            def bank0(n, t):
                return bank((4 + 2 * IN0_ORDER.index(n) + t) % 8)

            def free0(n, t):
                k = 2 * IN0_ORDER.index(n) + t
                if k < NT:
                    pe.wait_ge(lo_split, X_NORM0 + 2 * t + 2)
                if k >= 8:
                    pe.wait_ge(evacuated, k - 7)
            project(IN0, KC, bank0, free0)
            pe.wait_ge(evacuated, 10)
            for t in range(NT):
                pe.wait_ge(qk_normed, 3 + t)
                for g in range(4):
                    for j in range(4 * g, min(4 * g + 4, 13)):
                        if j < 8:
                            src = z[:, t, j * P:(j + 1) * P]
                        else:
                            src = z[:, t, ZB_Q + (j - 8) * P:ZB_Q + (j - 7) * P]
                        ins = pe.transpose(bank(4 * t + g)[:, (j % 4) * P:(j % 4 + 1) * P], src, ident[:, :])
                    ins.then_inc(qk_transposed, 1)
            pe.wait_ge(qkT_ready, 4)
            pe.wait_ge(qkT_copied, 4)
            attention(0, "AB")
            transpose_h(X_MERGE0, lambda t: pe.wait_ge(merged, t + 1))

            def split_wait(i):
                def free(n, t):
                    if n == 0:
                        pe.wait_ge(lo_split, i + 2 * t + 2)
                return free
            project(OUT0, KC, lambda n, t: bank(4 + 2 * n + t), split_wait(X_MERGE0), early_sum=True)
            transpose_h(X_NORM1, normed_wait(2))
            pe.wait_ge(lo_split, X_NORM1 + 4)
            f0 = first(FFN)

            def transpose_act(k, w):
                for t in range(NT):
                    pe.wait_ge(act_ready, 2 * k + t + 1)
                    for j in range(w // P):
                        ins = pe.transpose(bank(2 + t)[:, j * P:(j + 1) * P], act[:, t, j * P:(j + 1) * P], ident[:, :])
                    ins.then_inc(transposed, 1)

            for i, (name, k, c0, c1, w) in enumerate(FFN):
                u = f0 + i
                s = u % SLOTS
                piece_wait(u)
                for t in range(NT):
                    if name in ("ffn_g", "ffn_u"):
                        if name == "ffn_g" and c0 == 0 and k >= 1:
                            pe.wait_ge(act_ready, 2 * k + t - 1)
                        if name == "ffn_u" and c0 == 0 and k >= 1:
                            pe.wait_ge(lo_split, X_FFN + 2 * k + t - 1)
                        out = bank(t if name == "ffn_g" else 2 + t)[:, 0:w]
                        for c in range(c0, c1):
                            o = (c - c0) * w
                            ins = product(out, hT_hi[:, c, t * P:(t + 1) * P], hT_lo[:, c, t * P:(t + 1) * P],
                                          w_hi[:, s, o:o + w], w_lo[:, s, o:o + w], c == 0, c == KC - 1)
                    else:
                        if c0 == 0:
                            pe.wait_ge(lo_split, X_FFN + 2 * k + t + 1)
                        last = k == FFN_CHUNKS - 1
                        for j in range(c0, c1):
                            for n in range(2):
                                o = (j - c0) * D + n * COLS
                                ins = product(bank(4 + 2 * t + n), aT_hi[:, j, t * P:(t + 1) * P],
                                              aT_lo[:, j, t * P:(t + 1) * P], w_hi[:, s, o:o + COLS],
                                              w_lo[:, s, o:o + COLS], k == 0 and j == 0,
                                              last and j == w // P - 1)
                    if t == 0 and i == len(FFN) - 1:
                        ins.then_inc(first_tile, 1)
                ins.then_inc(used, 1)
                if name == "ffn_u" and c1 == KC and k == 0:
                    transpose_act(0, w)
                if name == "ffn_d" and c1 * P == w and k + 1 < FFN_CHUNKS:
                    transpose_act(k + 1, min(COLS, FF - (k + 1) * COLS))
            transpose_h(X_NORM2, normed_wait(4))
            project(IN1, KC, lambda n, t: bank(4 + t), split_wait(X_NORM2))
            for t in range(NT):
                pe.wait_ge(normed, 7 + t)
                for c in range(3):
                    ins = pe.transpose(bank(t)[:, c * P:(c + 1) * P], zg[:, t, c * P:(c + 1) * P], ident[:, :])
                ins.then_inc(transposed, 1)

            u = first(UKV)
            piece_wait(u)
            pe.wait_ge(lo_split, X_LORA + NT)
            pe.wait_ge(evacuated, 12)
            for t in range(NT):
                for n in range(4):
                    o = n * COLS
                    ins = product(bank(4 * t + n), hT_hi[:, 2, t * P:(t + 1) * P], hT_lo[:, 2, t * P:(t + 1) * P],
                                  w_hi[:, u % SLOTS, o:o + COLS], w_lo[:, u % SLOTS, o:o + COLS], True, True)
                ins.then_inc((first_tile, used)[t], 1)
            for t in range(NT):
                pe.wait_ge((v_copied, v_ready)[t], 1)
                for n in range(len(UQ)):
                    u = first(UQ) + n
                    piece_wait(u)
                    for c in range(C_QR // P):
                        o = c * COLS
                        ins = product(bank(4 * t + n), hT_hi[:, c, t * P:(t + 1) * P], hT_lo[:, c, t * P:(t + 1) * P],
                                      w_hi[:, u % SLOTS, o:o + COLS], w_lo[:, u % SLOTS, o:o + COLS],
                                      c == 0, c == C_QR // P - 1)
                    if t:
                        ins.then_inc(used, 1)
                    elif n == len(UQ) - 1:
                        ins.then_inc(first_tile, 1)

            def transpose_heads1(t, src):
                for g in range(4):
                    for j in range(4):
                        hd = 4 * g + j
                        ins = pe.transpose(bank(4 * t + g)[0:C_QK, j * P:(j + 1) * P],
                                           src[:, hd * C_QK:(hd + 1) * C_QK], ident[:, :])
                    ins.then_inc(qk_transposed, 1)

            for t in range(NT):
                pe.wait_ge(qk_normed, 5 + t)
                pe.wait_ge(q_evac, 3 * t + 3)
                transpose_heads1(t, k1[:, t, :])
                pe.wait_ge(qk_normed, 7 + t)
                pe.wait_ge(qkT_ready, 7 + 6 * t)
                pe.wait_ge(qkT_copied, 5 + 2 * t)
                if t == 0:
                    transpose_heads1(t, q1[t])

            def last_heads():
                transpose_heads1(1, q1[1])
                pe.wait_ge(qkT_ready, 16)
                pe.wait_ge(qkT_copied, 8)
            attention(16, "C", last_heads)
            transpose_h(X_MERGE1, lambda t: pe.wait_ge(merged, 3 + t))
            project(OUT1, KC, lambda n, t: bank(4 + 2 * n + t), split_wait(X_MERGE1), early_sum=True)
            transpose_h(X_NORM3, normed_wait(8))
            for t in range(NT):
                pe.wait_ge(lo_split, X_NORM3 + 2 * t + 2)
                for c in range(KC):
                    o = 2 * NE * t
                    pe.matmul(bank(4)[:, o:o + 2 * NE], hT_hi[:, c, t * P:(t + 1) * P], rw_split[:, c, :],
                              start=c == 0, stop=False)
                    ins = pe.matmul(bank(4)[:, o:o + NE], hT_lo[:, c, t * P:(t + 1) * P], rw_split[:, c, 0:NE],
                                    start=False, stop=c == KC - 1)
            ins.then_inc(routed, 1)
            pe.wait_ge(ranks_ready, 1)
            sel = rt[:, 192:208]
            pe.matmul(bank(6)[:, 0:8], triu, sel[:, 0:8], start=True, stop=True)
            pe.matmul(bank(6)[:, 8:16], ones, sel[:, 0:8], start=True, stop=False)
            pe.matmul(bank(6)[:, 8:16], triu, sel[:, 8:16], start=False, stop=True).then_inc(counted, 1)
            pe.matmul(bank(7)[:, 0:8], ones, sel[:, 0:8], start=True, stop=False)
            pe.matmul(bank(7)[:, 0:8], ones, sel[:, 8:16], start=False, stop=True).then_inc(counted, 1)

            def expert_pass(p):
                ub = U0 + p * NE * NU
                xb = X_EXP + p * X_PER_PASS
                cb = NT * FFN_CHUNKS + p * NE * EXP_CHUNKS
                sb_ = p * 4 * (NE + 1)

                def gather(e):
                    for g in range(2):
                        for c in range(4):
                            if g and c == 0 and isinstance(e, int) and e == 0:
                                pe.wait_ge(flag_ready, 1)
                            for t in range(NT):
                                cc = 4 * g + c
                                if isinstance(e, int):
                                    oh = onehot[:, t, e, :]
                                else:
                                    oh = onehot[:, t, bass.ds(e, 1), :].rearrange("p e n -> p (e n)")
                                ins = pe.matmul(bank(6 + g)[:, c * P:(c + 1) * P], h[:, t, cc * P:(cc + 1) * P], oh,
                                                start=t == 0, stop=t == NT - 1)
                        ins.then_inc(transposed, 1)

                def scatter(q, b=6):
                    t, n = q // 2, q % 2
                    pe.matmul(bank(b + n), scatT[:, t * P:(t + 1) * P], y_exp[:, n * COLS:(n + 1) * COLS],
                              start=True, stop=True).then_inc(scattered, 1)

                pe.wait_ge(onehot_ready, 6 * p + 2)
                if p:
                    pe.wait_ge(scat_added, 4 * (NE + 1))
                gather(0)
                pe.wait_ge(onehot_ready, 6 * p + 6)
                for b in range(4):
                    for j in range(4):
                        e, t = 2 * b + j // 2, j % 2
                        ins = pe.transpose(bank(SCAT_BANKS[b])[:, j * P:(j + 1) * P], onehot_gated[:, t, e, :],
                                           ident[:, :])
                    ins.then_inc(scat_transposed, 1)

                def expert(e, last):
                    pe.wait_ge(lo_split, per(xb + 2, e, X_PER_EXPERT))
                    for i, (kind, k, half) in enumerate(EXP):
                        s = (ub + i) % SLOTS
                        pe.wait_ge(lo_ready, per(ub + i + 1, e, NU))
                        if kind in "gu":
                            if kind == "u" and half == 0 and k == 0:
                                pe.wait_ge(scat_ready, 4 * p + 4)
                            if half == 0:
                                pe.wait_ge(act_ready, per(cb + k - 1, e, EXP_CHUNKS))
                            out = bank((0 if kind == "g" else 2) + k % 2)
                            for c in range(4):
                                o = c * COLS
                                ins = product(out, hT_hi[:, 4 * half + c, 0:P], hT_lo[:, 4 * half + c, 0:P],
                                              w_hi[:, s, o:o + COLS], w_lo[:, s, o:o + COLS],
                                              half == 0 and c == 0, half == 1 and c == 3)
                        else:
                            if half == 0:
                                pe.wait_ge(lo_split, per(xb + 2 + (k if k < 6 or last else 8) + 1, e, X_PER_EXPERT))
                                if k == 0:
                                    pe.wait_ge(y_evac, per(2 + 2 * NE * p, e, 2))
                            for j in range(2):
                                for n in range(2):
                                    o = j * D + n * COLS
                                    ins = product(bank(4 + n), aT_hi[:, 2 * half + j, 0:P],
                                                  aT_lo[:, 2 * half + j, 0:P], w_hi[:, s, o:o + COLS],
                                                  w_lo[:, s, o:o + COLS], k == 0 and half == 0 and j == 0,
                                                  k == EXP_CHUNKS - 1 and half == 1 and j == 1)
                        ins.then_inc(used, 1)

                        def transpose_act(kk):
                            pe.wait_ge(act_ready, per(cb + kk + 1, e, EXP_CHUNKS))
                            for j in range(4):
                                ins = pe.transpose(bank(6)[:, j * P:(j + 1) * P],
                                                   act[:, kk % 2, j * P:(j + 1) * P], ident[:, :])
                            ins.then_inc(transposed, 1)

                        if kind == "g" and half and k == 0:
                            pe.wait_ge(y_evac, per(2 + 2 * NE * p, e, 2))
                            scatter(0)
                            scatter(1)
                        if kind == "u" and half == 0 and k == 0:
                            pe.wait_ge(scat_added, per(sb_ + 2, e, 4))
                            scatter(2)
                            scatter(3)
                        if kind == "u" and half == 0 and k >= 1:
                            if k == 1:
                                pe.wait_ge(scat_added, per(sb_ + 4, e, 4))
                            transpose_act(k - 1)
                        if kind == "u" and half and k == EXP_CHUNKS - 1 and not last:
                            pe.wait_ge(lo_split, per(xb + 2 + 6, e, X_PER_EXPERT))
                            gather(e + 1)
                        if kind == "d" and half and k == EXP_CHUNKS - 2:
                            pe.wait_ge(lo_split, per(xb + 2 + (6 if last else 8), e, X_PER_EXPERT))
                            transpose_act(EXP_CHUNKS - 1)

                with pe.Fori(0, NE - 1) as e:
                    expert(e, False)
                expert(NE - 1, True)
                pe.wait_ge(y_evac, 2 + 2 * NE * (p + 1))
                scatter(0)
                scatter(1)
                scatter(2, 0)
                scatter(3, 0)

            expert_pass(0)
            pe.wait_ge(flag_ready, 1)
            most = pe.value_load(nmax_i[0:1, 0:1], min_val=0, max_val=SEQ)
            with pe.If(most > P):
                expert_pass(1)


_INS = ["x", "l0_norm_attn", "l0_w_in", "l0_a_q_norm", "l0_a_k_norm", "l0_a_lambda", "l0_a_subln",
        "l0_b_q_norm", "l0_b_k_norm", "l0_b_sinks", "l0_w_out", "l0_norm_ffn", "l0_ffn_w_gu",
        "l0_ffn_w_down", "l1_norm_attn", "l1_c_w_in", "l1_c_q_lora_norm", "l1_c_kv_lora_norm",
        "l1_c_w_uq", "l1_c_w_ukv", "l1_c_q_norm", "l1_c_k_norm", "l1_c_w_out", "l1_norm_ffn",
        "l1_router", "l1_exp_w_gu", "l1_exp_w_down"]


def shape_tables():
    def rope(dim):
        inv = (np.float32(10000.0) ** (-np.arange(0, dim, 2, dtype=np.float32) / np.float32(dim))).astype(np.float32)
        ang = np.arange(SEQ, dtype=np.float32)[:, None] * inv[None, :]
        return [np.cos(ang), np.sin(ang)]

    i = np.arange(P)
    e = np.arange(NE)
    tie = np.broadcast_to((e[None, :] < e[:, None]).reshape(1, NE * NE), (P, NE * NE))
    return {
        "ident": np.eye(P), "rope": np.concatenate(rope(HD) + rope(C_ROPE), 1),
        "triu": i[:, None] < i[None, :], "iota": np.broadcast_to(i[None, :], (P, P)), "tie": tie,
    }


def kernel(**inputs):
    import concourse.bacc as _bacc
    from concourse.bass_utils import run_bass_kernel_spmd as _run

    nc = _bacc.Bacc("TRN2", target_bir_lowering=False, num_devices=1)
    arrays, A = {}, {}
    data = {name: np.ascontiguousarray(inputs[name]) for name in _INS}
    data.update({n: np.ascontiguousarray(t, dtype=np.float32) for n, t in shape_tables().items()})
    for name, arr in data.items():
        arrays[f"in_{name}"] = arr
        A[name] = nc.dram_tensor(f"in_{name}", arr.shape, mybir.dt.from_np(arr.dtype), kind="ExternalInput").ap()
    A["out"] = nc.dram_tensor("out_0", data["x"].shape, mybir.dt.float32, kind="ExternalOutput").ap()
    build(nc, A)
    r = _run(nc, [arrays], core_ids=[0])
    return r.results[0]["out_0"]
```
